# Optimizing a Trainium2 kernel written in Bass

```python
import math
import jax
import jax.numpy as jnp
from jax import lax
import numpy as np

D_MODEL = 1024
BATCH = 1
SEQ = 2048
DEPTH = 1

POOL_WINDOWS = (2, 4, 8, 16)
POOL_GROUPS = 4
POOL_GROUP_DIM = D_MODEL // 8
POOL_WIDTH = POOL_GROUPS * POOL_GROUP_DIM
HEAD_DIM = 64
ATT_PATTERNS = ((128, 1), (512, 4), (2048, 16))
HEADS_PER_GROUP = 4
N_ATT_HEADS = HEADS_PER_GROUP * len(ATT_PATTERNS)
ATT_WIDTH = N_ATT_HEADS * HEAD_DIM
ATT_OUT_WIDTH = HEADS_PER_GROUP * HEAD_DIM
ALIBI_MAX_BIAS = 8.0
ATT_BLOCK = 128
IN_WIDTH = POOL_WIDTH + 3 * ATT_WIDTH + 2 * D_MODEL
N_EXPERT_GROUPS = 4
EXPERTS_PER_GROUP = 8
N_EXPERTS = N_EXPERT_GROUPS * EXPERTS_PER_GROUP
EXPERT_TOPK = 2
D_EXPERT = D_MODEL // 2
MOE_BLOCK = 128
RMS_EPS = 1e-6

kernel_name = 'hybrid_pool_dilated_attn_hmoe_block'

def _rmsnorm(x, g):
    xf = x.astype(jnp.float32)
    y = xf * lax.rsqrt(jnp.mean(xf * xf, axis=-1, keepdims=True) + RMS_EPS)
    return (y * g.astype(jnp.float32)).astype(x.dtype)

def _alibi_slopes():
    h = jnp.arange(1, N_ATT_HEADS + 1, dtype=jnp.float32)
    return jnp.exp2(-ALIBI_MAX_BIAS * h / N_ATT_HEADS)

def _multiscale_pool(u):
    b, s, _ = u.shape
    ug = u.astype(jnp.float32).reshape(b, s, POOL_GROUPS, POOL_GROUP_DIM)
    cs = jnp.cumsum(ug, axis=1)
    t = jnp.arange(s)
    outs = []
    for g, w in enumerate(POOL_WINDOWS):
        csg = cs[:, :, g]
        lagged = jnp.pad(csg[:, : s - w], ((0, 0), (w, 0), (0, 0)))
        count = jnp.minimum(t + 1, w).astype(jnp.float32)[None, :, None]
        outs.append((csg - lagged) / count - ug[:, :, g])
    return jnp.stack(outs, axis=2).astype(u.dtype)

def _dilated_window_attention(q, k, v, window, dilation, slopes):
    b, s, h, hd = q.shape
    sub_len = s // dilation
    nb = -(-sub_len // ATT_BLOCK)
    padded = nb * ATT_BLOCK
    reach = window // dilation

    def to_sub(t):
        t = t.reshape(b, sub_len, dilation, h, hd).transpose(0, 2, 3, 1, 4)
        return jnp.pad(t, ((0, 0), (0, 0), (0, 0), (0, padded - sub_len), (0, 0)))

    def key_blocks(t):
        t = jnp.pad(t, ((0, 0), (0, 0), (0, 0), (ATT_BLOCK, 0), (0, 0)))
        t = t.reshape(b, dilation, h, nb + 1, ATT_BLOCK, hd)
        return jnp.concatenate([t[:, :, :, :-1], t[:, :, :, 1:]], axis=4)

    qb = to_sub(q).reshape(b, dilation, h, nb, ATT_BLOCK, hd)
    kb = key_blocks(to_sub(k))
    vb = key_blocks(to_sub(v))
    scores = jnp.einsum('brhnqd,brhnkd->brhnqk', qb, kb,
                        preferred_element_type=jnp.float32) * (hd ** -0.5)
    qi = jnp.arange(ATT_BLOCK)[:, None]
    ki = jnp.arange(2 * ATT_BLOCK)[None, :]
    delta = ATT_BLOCK + qi - ki
    key_sub = (jnp.arange(nb)[:, None, None] - 1) * ATT_BLOCK + ki[None]
    valid = (delta >= 0) & (delta <= reach) & (key_sub >= 0)
    bias = -slopes[:, None, None] * (delta * dilation).astype(jnp.float32)
    scores = jnp.where(valid[None, None, None], scores + bias[None, None, :, None], -jnp.inf)
    mx = jnp.max(scores, axis=-1, keepdims=True)
    p = jnp.exp(scores - mx)
    den = jnp.sum(p, axis=-1, keepdims=True)
    o = jnp.einsum('brhnqk,brhnkd->brhnqd', p, vb.astype(jnp.float32)) / den
    lse = (mx + jnp.log(den))[..., 0]
    o = o.reshape(b, dilation, h, padded, hd)[:, :, :, :sub_len]
    o = o.transpose(0, 3, 1, 2, 4).reshape(b, s, h, hd)
    lse = lse.reshape(b, dilation, h, padded)[..., :sub_len]
    lse = lse.transpose(0, 3, 1, 2).reshape(b, s, h)
    return o, lse

def _token_mixer(h, w_in, w_pool_group, pool_scale, w_branch_pool, w_branch_att, w_out):
    b, s, _ = h.shape
    proj = h @ w_in
    splits = [POOL_WIDTH, POOL_WIDTH + ATT_WIDTH, POOL_WIDTH + 2 * ATT_WIDTH,
              POOL_WIDTH + 3 * ATT_WIDTH, POOL_WIDTH + 3 * ATT_WIDTH + D_MODEL]
    u, q, k, v, gate_pool, gate_att = jnp.split(proj, splits, axis=-1)

    pooled = _multiscale_pool(u)
    pooled = jnp.einsum('bsgc,gcd->bsgd', pooled, w_pool_group).reshape(b, s, POOL_WIDTH)
    y_pool = (pooled * pool_scale) @ w_branch_pool

    q = q.reshape(b, s, N_ATT_HEADS, HEAD_DIM)
    k = k.reshape(b, s, N_ATT_HEADS, HEAD_DIM)
    v = v.reshape(b, s, N_ATT_HEADS, HEAD_DIM)
    slopes = _alibi_slopes()
    outs, lses = [], []
    for g, (window, dilation) in enumerate(ATT_PATTERNS):
        hs = slice(g * HEADS_PER_GROUP, (g + 1) * HEADS_PER_GROUP)
        o, l = _dilated_window_attention(q[:, :, hs], k[:, :, hs], v[:, :, hs],
                                         window, dilation, slopes[hs])
        outs.append(o)
        lses.append(l)
    weights = jax.nn.softmax(jnp.stack(lses, axis=0), axis=0)
    o = jnp.sum(weights[..., None] * jnp.stack(outs, axis=0), axis=0)
    y_att = o.reshape(b, s, ATT_OUT_WIDTH).astype(h.dtype) @ w_branch_att

    merged = jax.nn.sigmoid(gate_pool) * y_pool + jax.nn.sigmoid(gate_att) * y_att
    return merged @ w_out

def _hier_moe(h, w_group_router, b_group_router, w_expert_router, b_expert_router,
              w_gate, w_up, w_down):
    t_count = h.shape[0]
    hf = h.astype(jnp.float32)
    g_logits = hf @ w_group_router.astype(jnp.float32) + b_group_router.astype(jnp.float32)
    g_prob = jax.nn.softmax(g_logits, axis=-1)
    g_sel = jnp.argmax(g_logits, axis=-1)
    p_group = jnp.take_along_axis(g_prob, g_sel[:, None], axis=1)[:, 0]
    e_logits = (hf @ w_expert_router.astype(jnp.float32)
                + b_expert_router.astype(jnp.float32)).reshape(t_count, N_EXPERT_GROUPS, EXPERTS_PER_GROUP)
    e_logits = jnp.take_along_axis(e_logits, g_sel[:, None, None], axis=1)[:, 0]
    top_v, top_i = lax.top_k(e_logits, EXPERT_TOPK)
    gate_w = p_group[:, None] * jax.nn.softmax(top_v, axis=-1)
    expert_id = g_sel[:, None] * EXPERTS_PER_GROUP + top_i

    n_assign = t_count * EXPERT_TOPK
    e_a = expert_id.reshape(-1).astype(jnp.int32)
    tok_a = jnp.repeat(jnp.arange(t_count, dtype=jnp.int32), EXPERT_TOPK)
    w_a = gate_w.reshape(-1)
    order = jnp.argsort(e_a)
    e_s, tok_s, w_s = e_a[order], tok_a[order], w_a[order]
    counts = jnp.zeros((N_EXPERTS,), jnp.int32).at[e_a].add(1)
    pad_counts = ((counts + MOE_BLOCK - 1) // MOE_BLOCK) * MOE_BLOCK
    pad_end = jnp.cumsum(pad_counts)
    pad_start = pad_end - pad_counts
    raw_start = jnp.cumsum(counts) - counts
    dest = pad_start[e_s] + jnp.arange(n_assign, dtype=jnp.int32) - raw_start[e_s]
    n_blocks = -(-n_assign // MOE_BLOCK) + N_EXPERTS
    n_slots = n_blocks * MOE_BLOCK
    slot_tok = jnp.zeros((n_slots,), jnp.int32).at[dest].set(tok_s)
    slot_w = jnp.zeros((n_slots,), h.dtype).at[dest].set(w_s.astype(h.dtype))
    block_start = jnp.arange(n_blocks, dtype=jnp.int32) * MOE_BLOCK
    block_expert = jnp.minimum(jnp.searchsorted(pad_end, block_start, side='right'),
                               N_EXPERTS - 1).astype(jnp.int32)

    def run_block(args):
        tok, e = args
        xb = h[tok]
        a = xb @ w_gate[e]
        u = xb @ w_up[e]
        return (jax.nn.silu(a) * u) @ w_down[e]

    y = lax.map(run_block, (slot_tok.reshape(n_blocks, MOE_BLOCK), block_expert))
    y = y.reshape(n_slots, D_MODEL) * slot_w[:, None]
    return jnp.zeros((t_count, D_MODEL), h.dtype).at[slot_tok].add(y)

def setup_inputs(seed: int = 0) -> dict:
    key = jax.random.key(seed)
    ks = jax.random.split(key, 24)
    f32 = jnp.float32
    L, D = DEPTH, D_MODEL

    def nrm(k, shape, scale):
        return jax.random.normal(k, shape, f32) * scale

    return {
        'x': nrm(ks[0], (BATCH, SEQ, D), 1.0),
        'c': nrm(ks[1], (BATCH, D), 1.0),
        'w_ada': nrm(ks[2], (L, D, 6 * D), 0.5 * D ** -0.5),
        'b_ada': nrm(ks[3], (L, 6 * D), 0.02),
        'g_pre_mix': 1.0 + nrm(ks[4], (L, D), 0.02),
        'g_post_mix': 1.0 + nrm(ks[5], (L, D), 0.02),
        'g_pre_ffn': 1.0 + nrm(ks[6], (L, D), 0.02),
        'g_post_ffn': 1.0 + nrm(ks[7], (L, D), 0.02),
        'w_in': nrm(ks[8], (L, D, IN_WIDTH), D ** -0.5),
        'w_pool_group': nrm(ks[9], (L, POOL_GROUPS, POOL_GROUP_DIM, POOL_GROUP_DIM), POOL_GROUP_DIM ** -0.5),
        'pool_scale': 1.0 + nrm(ks[10], (L, POOL_WIDTH), 0.02),
        'w_branch_pool': nrm(ks[11], (L, POOL_WIDTH, D), POOL_WIDTH ** -0.5),
        'w_branch_att': nrm(ks[12], (L, ATT_OUT_WIDTH, D), ATT_OUT_WIDTH ** -0.5),
        'w_out': nrm(ks[13], (L, D, D), D ** -0.5),
        'w_group_router': nrm(ks[14], (L, D, N_EXPERT_GROUPS), D ** -0.5),
        'b_group_router': nrm(ks[15], (L, N_EXPERT_GROUPS), 0.01),
        'w_expert_router': nrm(ks[16], (L, D, N_EXPERTS), D ** -0.5),
        'b_expert_router': nrm(ks[17], (L, N_EXPERTS), 0.01),
        'w_exp_gate': nrm(ks[18], (L, N_EXPERTS, D, D_EXPERT), D ** -0.5),
        'w_exp_up': nrm(ks[19], (L, N_EXPERTS, D, D_EXPERT), D ** -0.5),
        'w_exp_down': nrm(ks[20], (L, N_EXPERTS, D_EXPERT, D), D_EXPERT ** -0.5),
    }

def reference(x, c, w_ada, b_ada, g_pre_mix, g_post_mix, g_pre_ffn, g_post_ffn, w_in,
              w_pool_group, pool_scale, w_branch_pool, w_branch_att, w_out,
              w_group_router, b_group_router, w_expert_router, b_expert_router,
              w_exp_gate, w_exp_up, w_exp_down):
    b, s, d = x.shape
    for layer in range(DEPTH):
        mod = jax.nn.silu(c) @ w_ada[layer] + b_ada[layer]
        sh_m, sc_m, gt_m, sh_f, sc_f, gt_f = jnp.split(mod, 6, axis=-1)
        h = _rmsnorm(x, g_pre_mix[layer]) * (1.0 + sc_m[:, None]) + sh_m[:, None]
        y = _token_mixer(h, w_in[layer], w_pool_group[layer], pool_scale[layer],
                         w_branch_pool[layer], w_branch_att[layer], w_out[layer])
        x = x + gt_m[:, None] * _rmsnorm(y, g_post_mix[layer])
        h = _rmsnorm(x, g_pre_ffn[layer]) * (1.0 + sc_f[:, None]) + sh_f[:, None]
        y = _hier_moe(h.reshape(b * s, d), w_group_router[layer], b_group_router[layer],
                      w_expert_router[layer], b_expert_router[layer],
                      w_exp_gate[layer], w_exp_up[layer], w_exp_down[layer]).reshape(b, s, d)
        x = x + gt_f[:, None] * _rmsnorm(y, g_post_ffn[layer])
    return x


_drawn_inputs = setup_inputs


def setup_inputs(seed=0):
    import zlib

    import numpy as np

    out = dict(_drawn_inputs(seed))
    spreads = {}
    factors = {'g_post_ffn': 8.0, 'b_group_router': 4.119, 'b_expert_router': 3.374}
    for name, (base, spread) in spreads.items():
        noise = np.random.default_rng([zlib.crc32(name.encode()), seed]).standard_normal(out[name].shape)
        drawn = base * np.exp(spread * noise) if base else spread * noise
        out[name] = jnp.asarray(drawn.astype(out[name].dtype))
    for name, factor in factors.items():
        out[name] = (out[name] * factor).astype(out[name].dtype)
    return out
```

```python
from contextlib import ExitStack

import concourse.bass as bass
from concourse import mybir

P = 128
D = 1024
SEQ = 2048
KD = D // P
TILES = SEQ // P
TG = SEQ // 512
POOL_WINDOWS = (2, 4, 8, 16)
POOL_TILES = len(POOL_WINDOWS)
HEADS = 12
HPG = 4
DILATIONS = (1, 4, 16)
PAIRS_OF_GROUP = HPG // 2
IN_TILES = (4 * P + 3 * HEADS * 64 + 2 * D) // P
Q_TILE, K_TILE, V_TILE, GATE_TILE = 4, 10, 16, 22
EG, EPG = 4, 8
NE = EG * EPG
DE = 512
KE = DE // P
NB = 64
EPS = 1e-6

F32 = mybir.dt.float32
F32R = mybir.dt.float32r
I32 = mybir.dt.int32
ALU = mybir.AluOpType
ACT = mybir.ActivationFunctionType
AX = mybir.AxisListType
ds = bass.ds


class Chain:

    def __init__(self, eng, sem):
        self.eng, self.sem, self.at, self.n = eng, sem, 0, 0

    def link(self, ins):
        self.n += 1
        ins.then_inc(self.sem, 1)
        self.eng.wait_ge(self.sem, self.at + self.n)

    def turn(self, at):
        self.at, self.n = at, 0


class Scope:

    def __init__(self, nc, ctx, name):
        self.nc, self.ctx, self.name, self.sems = nc, ctx, name, []
        ctx.callback(self.clear)

    def sb(self, name, shape, dt=F32):
        return self.ctx.enter_context(self.nc.sbuf_tensor(f"{self.name}_{name}", shape, dt))

    def ps(self, name, shape, dt=F32):
        return self.ctx.enter_context(self.nc.psum_tensor(f"{self.name}_{name}", shape, dt))

    def sem(self, name):
        self.sems.append(self.nc.alloc_semaphore(f"{self.name}_{name}"))
        return self.sems[-1]

    def clear(self):
        self.nc.clear_and_free_semaphores(self.sems)
        self.nc.all_engine_barrier()


def condition(nc, c, w_ada, b_ada, gains, mod_dram):
    with ExitStack() as ctx:
        s = Scope(nc, ctx, "cond")
        RING, COLS = 4, 2048
        PARTS = 6 * D // COLS
        mod = s.sb("mod", [P, 6, D])
        ccol = s.sb("ccol", [P, KD])
        cexp = s.sb("cexp", [P, KD])
        cact = s.sb("cact", [P, KD])
        ring = s.sb("ring", [P, RING, COLS])
        acc = s.sb("acc", [P, 6 * D])
        ones = s.sb("ones", [P, P])
        gain = s.sb("gain", [P, 4, D])
        psum = s.ps("psum", [P, 2, 512])
        c_loaded, b_loaded, gain_loaded = s.sem("c_loaded"), s.sem("b_loaded"), s.sem("gain_loaded")
        chunk_loaded = [s.sem(f"chunk_loaded{r}") for r in range(RING)]
        chunk_used, act_ready, acc_zero = s.sem("chunk_used"), s.sem("act_ready"), s.sem("acc_zero")
        ones_ready, part_summed, sum_taken, mod_done, mod_stored = (
            s.sem("ones_ready"), s.sem("part_summed"), s.sem("sum_taken"), s.sem("mod_done"), s.sem("mod_stored"))
        steps = s.sem("steps")
        w = w_ada[0].rearrange("(p k) n -> p k n", k=KD)
        with nc.Block() as block:
            @block.sync
            def _(sp):
                sp.dma_start(ccol[:, :], c.rearrange("b (p k) -> (b p) k", k=KD)).then_inc(c_loaded, 16)
                for n in range(PARTS * KD):
                    part, k = divmod(n, KD)
                    if n >= RING:
                        sp.wait_ge(chunk_used, n - RING + 1)
                    sp.dma_start(ring[:, n % RING, :], w[:, k, ds(part * COLS, COLS)]).then_inc(chunk_loaded[n % RING], 16)
                sp.wait_ge(mod_done, 6)
                sp.dma_start(mod_dram, mod[0:1, :, :].rearrange("a m d -> a (m d)")).then_inc(mod_stored, 16)
                sp.wait_ge(mod_stored, 16)

            @block.scalar
            def _(act):
                act.wait_ge(acc_zero, 1)
                act.dma_start(acc[0:1, :], b_ada).then_inc(b_loaded, 16)
                for n, g in enumerate(gains):
                    act.dma_start(gain[:, n, :], g[0:1, :].partition_broadcast(P)).then_inc(gain_loaded, 16)
                act.wait_ge(c_loaded, 16)
                nc.scalar.activation(cexp[:, :], ccol[:, :], ACT.Exp, scale=-1.0).then_inc(act_ready, 1)

            @block.tensor
            def _(pe):
                pe.wait_ge(ones_ready, 1)
                for n in range(12):
                    if n % 4 == 0:
                        pe.wait_ge(chunk_used, (n // 4 + 1) * KD)
                    if n >= 2:
                        pe.wait_ge(sum_taken, n - 1)
                    pe.matmul(psum[:, n % 2, :], ones[:, :], acc[:, ds(n * 512, 512)], start=True, stop=True).then_inc(part_summed, 1)

            @block.gpsimd
            def _(pool):
                pool.memset(ones[:, :], 1.0).then_inc(ones_ready, 1)

            @block.vector
            def _(dve):
                chain = Chain(dve, steps)
                dve.memset(acc[:, :], 0.0).then_inc(acc_zero, 1)
                dve.wait_ge(act_ready, 1)
                chain.link(dve.tensor_scalar(cexp[:, :], cexp[:, :], 1.0, None, ALU.add))
                chain.link(dve.reciprocal(cexp[:, :], cexp[:, :]))
                chain.link(dve.tensor_tensor(cact[:, :], cexp[:, :], ccol[:, :], ALU.mult))
                dve.wait_ge(b_loaded, 16)
                mod_flat = mod[:, :, :].rearrange("p m d -> p (m d)")

                def take(n):
                    dve.wait_ge(part_summed, n + 1)
                    dve.tensor_copy(mod_flat[:, ds(n * 512, 512)], psum[:, n % 2, :]).then_inc(sum_taken, 1)

                for n in range(PARTS * KD):
                    part, k = divmod(n, KD)
                    dve.wait_ge(chunk_loaded[n % RING], 16 * (n // RING + 1))
                    if n:
                        dve.wait_ge(chunk_used, n)
                    sums = acc[:, ds(part * COLS, COLS)]
                    dve.scalar_tensor_tensor(out=sums, in0=ring[:, n % RING, :], scalar=cact[:, k:k + 1], in1=sums,
                                             op0=ALU.mult, op1=ALU.add).then_inc(chunk_used, 1)
                    if part and k == 1:
                        for m in range(4):
                            take((part - 1) * 4 + m)
                for m in range(4):
                    take((PARTS - 1) * 4 + m)
                dve.wait_ge(sum_taken, 12)
                dve.wait_ge(gain_loaded, 64)
                for half in range(2):
                    row = mod[:, 3 * half + 1, :]
                    dve.scalar_tensor_tensor(out=row, in0=row, scalar=1.0, in1=gain[:, 2 * half, :],
                                             op0=ALU.add, op1=ALU.mult).then_inc(mod_done, 2)
                    row = mod[:, 3 * half + 2, :]
                    dve.tensor_tensor(row, row, gain[:, 2 * half + 1, :], ALU.mult).then_inc(mod_done, 1)


def normalise(nc, x, mod_dram, ident, h_hi, h_lo):
    with ExitStack() as ctx:
        s = Scope(nc, ctx, "norm")
        mod = s.sb("mod", [P, 2, D])
        eps = s.sb("eps", [P, 1])
        root = s.sb("root", [P, 2])
        mod_loaded, eps_ready, root_ready = s.sem("mod_loaded"), s.sem("eps_ready"), s.sem("root_ready")
        xt = s.sb("xt", [P, 2, D])
        sq = s.sb("sq", [P, 2, D])
        h = s.sb("h", [P, 2, D])
        ms = s.sb("ms", [P, 2])
        rstd = s.sb("rstd", [P, 2])
        psum = s.ps("psum", [P, 2, D])
        loaded = [s.sem(f"loaded{i}") for i in range(2)]
        summed, rstd_ready, scaled, h_ready, turned, hi_ready, lo_ready, steps = (s.sem(n) for n in (
            "summed", "rstd_ready", "scaled", "h_ready", "turned", "hi_ready", "lo_ready", "steps"))
        hT_hi = h_hi[:, :, :].rearrange("p k (t c) -> p k t c", c=P)
        hT_lo = h_lo[:, :, :].rearrange("p k (t c) -> p k t c", c=P)
        with nc.Block() as block:
            @block.sync
            def _(sp):
                sp.dma_start(mod[:, :, :].rearrange("p m d -> p (m d)"),
                             mod_dram[0:1, 0:2 * D].partition_broadcast(P)).then_inc(mod_loaded, 16)
                for t in range(TILES):
                    if t >= 2:
                        sp.wait_ge(scaled, t - 1)
                    sp.dma_start(xt[:, t % 2, :], x[0, ds(t * P, P), :]).then_inc(loaded[t % 2], 16)

            @block.scalar
            def _(act):
                def split(t):
                    act.wait_ge(turned, t + 1)
                    nc.scalar.activation(hT_hi[:, :, t, :], psum[:, t % 2, :].rearrange("p (k c) -> p k c", c=P),
                                         ACT.Copy).then_inc(hi_ready, 1)

                act.wait_ge(eps_ready, 1)
                for t in range(TILES):
                    act.wait_ge(loaded[t % 2], 16 * (t // 2 + 1))
                    if t >= 2:
                        act.wait_ge(scaled, t - 1)
                    nc.scalar.activation(sq[:, t % 2, :], xt[:, t % 2, :], ACT.Square,
                                         accum_out=ms[:, t % 2:t % 2 + 1]).then_inc(summed, 1)
                    act.wait_ge(summed, t + 1)
                    nc.scalar.activation(root[:, t % 2:t % 2 + 1], ms[:, t % 2:t % 2 + 1], ACT.Sqrt, scale=1.0 / D,
                                         bias=eps[:, 0:1]).then_inc(root_ready, 1)
                    if t >= 1:
                        split(t - 1)
                split(TILES - 1)

            @block.gpsimd
            def _(pool):
                pool.memset(eps[:, :], EPS).then_inc(eps_ready, 1)
                pool.wait_ge(mod_loaded, 16)
                for t in range(TILES):
                    pool.wait_ge(scaled, t + 1)
                    pool.tensor_tensor(h[:, t % 2, :], h[:, t % 2, :], mod[:, 0, :], ALU.add).then_inc(h_ready, 1)

            @block.tensor
            def _(pe):
                for t in range(TILES):
                    pe.wait_ge(h_ready, t + 1)
                    if t >= 2:
                        pe.wait_ge(lo_ready, t - 1)
                    for k in range(KD):
                        mm = pe.transpose(psum[:, t % 2, ds(k * P, P)], h[:, t % 2, ds(k * P, P)], ident[:, :])
                    mm.then_inc(turned, 1)

            @block.vector
            def _(dve):
                dve.wait_ge(mod_loaded, 16)

                def low(t):
                    dve.wait_ge(hi_ready, t + 1)
                    dve.tensor_tensor(hT_lo[:, :, t, :], psum[:, t % 2, :].rearrange("p (k c) -> p k c", c=P),
                                      hT_hi[:, :, t, :], ALU.subtract).then_inc(lo_ready, 1)

                for t in range(TILES):
                    dve.wait_ge(root_ready, t + 1)
                    dve.reciprocal(rstd[:, t % 2:t % 2 + 1], root[:, t % 2:t % 2 + 1]).then_inc(rstd_ready, 1)
                    dve.wait_ge(rstd_ready, t + 1)
                    if t >= 2:
                        dve.wait_ge(turned, t - 1)
                    dve.scalar_tensor_tensor(out=h[:, t % 2, :], in0=xt[:, t % 2, :], scalar=rstd[:, t % 2:t % 2 + 1],
                                             in1=mod[:, 1, :], op0=ALU.mult, op1=ALU.mult).then_inc(scaled, 1)
                    if t >= 1:
                        low(t - 1)
                low(TILES - 1)


def project(nc, w_in, h_hi, h_lo, proj):
    with ExitStack() as ctx:
        s = Scope(nc, ctx, "proj")
        raw = s.sb("raw", [P, 2, KD, P])
        w_hi = s.sb("w_hi", [P, 2, KD, P], F32R)
        w_lo = s.sb("w_lo", [P, 2, KD, P], F32R)
        out = s.sb("out", [P, 2, SEQ])
        sums = s.sb("sums", [P, 2, SEQ])
        inv = s.sb("inv", [P, 16])
        psum = s.ps("psum", [P, 2, TG, 512])
        loaded = [s.sem(f"loaded{i}") for i in range(2)]
        hi_ready = [s.sem(f"hi_ready{i}") for i in range(2)]
        lo_ready = [s.sem(f"lo_ready{i}") for i in range(2)]
        summed = [s.sem(f"summed{i}") for i in range(2)]
        taken = [s.sem(f"taken{i}") for i in range(2)]
        tile_done = [s.sem(f"tile_done{i}") for i in range(2)]
        stored = [s.sem(f"stored{i}") for i in range(2)]
        steps = s.sem("steps")
        PAIRS = IN_TILES // 2
        with nc.Block() as block:
            @block.sync
            def _(sp):
                def load(j, u):
                    sp.dma_start(raw[:, u, :, :], w_in[0, :, ds((2 * j + u) * P, P)].rearrange("(k p) f -> p k f", p=P)
                                 ).then_inc(loaded[u], 16)

                def store(j, u):
                    sp.wait_ge(tile_done[u], j + 1)
                    sp.dma_start(proj[ds((2 * j + u) * P, P), :], out[:, u, :]).then_inc(stored[u], 16)

                for u in range(2):
                    load(0, u)
                with sp.Fori(1, PAIRS) as j:
                    for u in range(2):
                        sp.wait_ge(lo_ready[u], j)
                        load(j, u)
                    for u in range(2):
                        store(j - 1, u)
                for u in range(2):
                    store(PAIRS - 1, u)
                for u in range(2):
                    sp.wait_ge(stored[u], 16 * PAIRS)

            @block.scalar
            def _(act):
                with act.Fori(0, PAIRS) as j:
                    for u in range(2):
                        act.wait_ge(loaded[u], 16 * j + 16)
                        act.wait_ge(summed[u], TG * j + TG)
                        nc.scalar.activation(w_hi[:, u, :, :], raw[:, u, :, :], ACT.Copy).then_inc(hi_ready[u], 1)

            @block.gpsimd
            def _(pool):
                with pool.Fori(0, PAIRS) as j:
                    for u in range(2):
                        pool.wait_ge(hi_ready[u], j + 1)
                        pool.tensor_tensor(w_lo[:, u, :, :], raw[:, u, :, :], w_hi[:, u, :, :], ALU.subtract
                                           ).then_inc(lo_ready[u], 1)

            @block.tensor
            def _(pe):
                for u in range(2):
                    pe.sem_inc(summed[u], TG)
                with pe.Fori(0, PAIRS) as j:
                    for u in range(2):
                        pe.wait_ge(lo_ready[u], j + 1)
                        for tg in range(TG):
                            pe.wait_ge(taken[u], TG * j + tg + 1)
                            for k in range(KD):
                                tok = ds(tg * 512, 512)
                                bank = psum[:, u, tg, :]
                                pe.matmul(bank, w_hi[:, u, k, :], h_hi[:, k, tok], start=(k == 0), stop=False)
                                pe.matmul(bank, w_hi[:, u, k, :], h_lo[:, k, tok], start=False, stop=False)
                                mm = pe.matmul(bank, w_lo[:, u, k, :], h_hi[:, k, tok], start=False, stop=(k == KD - 1))
                            mm.then_inc(summed[u], 1)

            @block.vector
            def _(dve):
                chain = Chain(dve, steps)
                for u in range(2):
                    dve.sem_inc(taken[u], TG)
                for t in range(15):
                    last = dve.memset(inv[:, t:t + 1], 1.0 / (t + 1))
                chain.link(last)

                def take(j, u, dilation):
                    view = out[:, u, :].rearrange("p (r m) -> p m r", r=dilation)
                    per = 512 // dilation
                    for tg in range(TG):
                        dve.wait_ge(summed[u], TG * j + TG + tg + 1)
                        ins = dve.tensor_copy(view[:, ds(tg * per, per), :],
                                              psum[:, u, tg, :].rearrange("p (m r) -> p m r", r=dilation))
                        ins.then_inc(taken[u], 1)

                for j in range(POOL_TILES // 2):
                    for u in range(2):
                        window = POOL_WINDOWS[2 * j + u]
                        if j:
                            dve.wait_ge(stored[u], 16 * j)
                        take(j, u, 1)
                        dve.wait_ge(taken[u], TG * (j + 2))
                        chan = out[:, u, :]
                        reach, now = 1, chan
                        while reach < window:
                            new = sums[:, reach.bit_length() % 2, :]
                            dve.tensor_copy(new[:, :reach], now[:, :reach])
                            chain.link(dve.tensor_tensor(new[:, reach:], now[:, reach:], now[:, :SEQ - reach], ALU.add))
                            reach, now = 2 * reach, new
                        head = window - 1
                        chain.link(dve.tensor_tensor(now[:, :head], now[:, :head], inv[:, :head], ALU.mult))
                        chain.link(dve.tensor_tensor(chan[:, :head], now[:, :head], chan[:, :head], ALU.subtract))
                        chain.link(dve.scalar_tensor_tensor(out=chan[:, head:], in0=now[:, head:], scalar=1.0 / window,
                                                            in1=chan[:, head:], op0=ALU.mult, op1=ALU.subtract))
                        dve.sem_inc(tile_done[u], 1)
                first = POOL_TILES // 2
                groups = len(DILATIONS)
                with dve.Fori(0, 3) as part:
                    for g, dilation in enumerate(DILATIONS):
                        j = part * groups + (first + g)
                        for u in range(2):
                            dve.wait_ge(stored[u], 16 * j)
                            take(j, u, dilation)
                            dve.wait_ge(taken[u], TG * j + 2 * TG)
                            dve.sem_inc(tile_done[u], 1)
                with dve.Fori(first + 3 * groups, PAIRS) as j:
                    for u in range(2):
                        dve.wait_ge(stored[u], 16 * j)
                        take(j, u, 1)
                        dve.wait_ge(taken[u], TG * j + 2 * TG)
                        dve.sem_inc(tile_done[u], 1)


def constants(nc, ident):
    with ExitStack() as ctx:
        s = Scope(nc, ctx, "const")
        zeroed, ready = s.sem("zeroed"), s.sem("ready")
        with nc.Block() as block:
            @block.gpsimd
            def _(pool):
                pool.memset(ident[:, :], 0.0).then_inc(zeroed, 1)
                pool.wait_ge(zeroed, 1)
                pool.affine_select(out=ident[:, :], in_=ident[:, :], compare_op=ALU.not_equal, fill=1.0,
                                   base=0, pattern=[[-1, P]], channel_multiplier=1).then_inc(ready, 1)
                pool.wait_ge(ready, 1)


ROW = 66
MASKED = 1e38


def attend(nc, proj, ident, att):
    units = []
    for g, dilation in enumerate(DILATIONS):
        blocks_of_residue = TILES // dilation
        width = P if blocks_of_residue == 1 else 2 * P
        step = 512 // width
        for pair in range(PAIRS_OF_GROUP):
            for b in range(0, TILES, step):
                units.append((g, pair, b, step, width))
    N = len(units)
    pair_of = [PAIRS_OF_GROUP * g + pair for g, pair, *_ in units]
    first_of = [n == 0 or pair_of[n] != pair_of[n - 1] for n in range(N)]
    last_of = [max(n for n in range(N) if pair_of[n] == q) for q in range(6)]
    turn_of = [n + 2 * (pair_of[n] + 1) for n in range(N)]
    VP = nc_bufs = 2
    with ExitStack() as ctx:
        s = Scope(nc, ctx, "att")
        qkv = s.sb("qkv", [P, 2, 3, SEQ])
        v = s.sb("v", [P, 2, TILES, P])
        dist = s.sb("dist", [P, 3 * 2 * P])
        dist_own = s.sb("dist_own", [P, 4 * P])
        bias = s.sb("bias", [P, 2, 2, 3 * 2 * P])
        score = s.sb("score", [P, 2, 2, 512])
        prob = s.sb("prob", [P, 2, 2, 512])
        probT = s.sb("probT", [P, 2, 2, 512])
        neg = s.sb("neg", [P, 2, 2, 4])
        res = s.sb("res", [P, 4, 4, 2, ROW])
        p_score = s.ps("p_score", [P, 2, 2, 512])
        p_turn = s.ps("p_turn", [P, 2, 512])
        p_out = s.ps("p_out", [P, 2, 512])
        loaded = [s.sem(f"loaded{i}") for i in range(2)]
        stored = [s.sem(f"stored{i}") for i in range(4)]
        names = ("dist_ready", "biased", "bias_ready", "scored", "maxed", "negated", "exped", "turned0", "turned1",
                 "copied0", "copied1", "weighed", "res_ready", "made")
        (dist_ready, biased, bias_ready, scored, maxed, negated, exped, turned0, turned1, copied0, copied1,
         weighed, res_ready, made) = (s.sem(n) for n in names)
        turned, copied = (turned0, turned1), (copied0, copied1)

        def probs_dst(n, a):
            return probT[:, n % 2, a, :]

        def copy_turn(eng, copy, turn, a, dst):
            eng.wait_ge(turned[a], turn + 1)
            copy(dst, p_turn[:, a, :]).then_inc(copied[a], 1)

        def v_dst(q, half, a):
            return v[:, q % 2, ds(8 * half + 4 * a, 4), :].rearrange("p b f -> p (b f)")

        def copies(eng, copy, n, a):
            q = pair_of[n]
            if first_of[n]:
                if q >= 2:
                    eng.wait_ge(weighed, last_of[q - 2] + 1)
                for half in range(2):
                    copy_turn(eng, copy, turn_of[n] - 2 + half, a, v_dst(q, half, a))
            if n >= 2:
                eng.wait_ge(weighed, n - 1)
            copy_turn(eng, copy, turn_of[n], a, probs_dst(n, a))

        with nc.Block() as block:
            @block.sync
            def _(sp):
                def load(q):
                    g, pair = divmod(q, PAIRS_OF_GROUP)
                    if q >= 2:
                        sp.wait_ge(scored, last_of[q - 2] + 1)
                        sp.wait_ge(turned1, turn_of[last_of[q - 2]] + 1)
                    for part, tile0 in enumerate((Q_TILE, K_TILE, V_TILE)):
                        sp.dma_start(qkv[:, q % 2, part, :], proj[ds((tile0 + 2 * g + pair) * P, P), :]).then_inc(loaded[q % 2], 16)

                load(0)
                load(1)
                for n, (g, pair, b, step, width) in enumerate(units):
                    if first_of[n] and 2 <= pair_of[n] + 1 < 6:
                        load(pair_of[n] + 1)
                    dilation = DILATIONS[g]
                    rows = att[g].rearrange("(n i r) f -> r n i f", r=dilation, i=P)
                    per = TILES // dilation
                    if width == P:
                        dst = rows[b:b + step, 0, :, ds(2 * pair * ROW, 2 * ROW)].rearrange("r i f -> i r f")
                    else:
                        dst = rows[b // per, b % per:b % per + step, :, ds(2 * pair * ROW, 2 * ROW)].rearrange("n i f -> i n f")
                    sp.wait_ge(res_ready, n + 1)
                    sp.dma_start(dst, res[:, n % 4, 0:step, :, :].rearrange("p b a f -> p b (a f)")).then_inc(stored[n % 4], 16)
                for i in range(4):
                    sp.wait_ge(stored[i], 16 * len(range(i, N, 4)))

            @block.gpsimd
            def _(pool):
                chain = Chain(pool, made)
                own = dist[:, 256:512]
                chain.link(pool.iota(own, pattern=[[-1, 256]], base=P, channel_multiplier=1,
                                     allow_small_or_imprecise_dtypes=True))
                chain.link(pool.affine_select(out=own, in_=own, compare_op=ALU.is_ge, fill=MASKED, base=P,
                                              pattern=[[-1, 256]], channel_multiplier=1))
                chain.link(pool.affine_select(out=own, in_=own, compare_op=ALU.is_ge, fill=MASKED, base=0,
                                              pattern=[[1, 256]], channel_multiplier=-1))
                pool.memset(dist[:, 0:P], MASKED)
                pool.tensor_copy(dist[:, P:2 * P], own[:, P:2 * P])
                pool.tensor_copy(dist[:, 512:768], own)
                for m in range(4):
                    last = pool.tensor_copy(dist_own[:, ds(m * P, P)], own[:, P:2 * P])
                chain.link(last)
                for q in range(6):
                    g, pair = divmod(q, PAIRS_OF_GROUP)
                    if q >= 2:
                        pool.wait_ge(biased, 2 * (last_of[q - 2] + 1))
                    for a in range(2):
                        head = HPG * g + 2 * pair + a
                        slope = 2.0 ** (-8.0 * (head + 1) / HEADS) * DILATIONS[g]
                        src = dist_own if DILATIONS[g] == TILES else dist
                        w = src.shape[1]
                        pool.tensor_scalar(bias[:, q % 2, a, 0:w], src[:, :], -slope, None, ALU.mult).then_inc(bias_ready, 1)

            @block.tensor
            def _(pe):
                def scores(n):
                    g, pair, b, step, width = units[n]
                    q = pair_of[n]
                    pe.wait_ge(loaded[q % 2], 48 * (q // 2 + 1))
                    if n >= 2:
                        pe.wait_ge(biased, 2 * (n - 1))
                    for a in range(2):
                        part = ds(64 * a, 64)
                        for m in range(step):
                            blk = b + m
                            before = max(blk - 1, 0) if width == 2 * P else blk
                            if width == 2 * P and blk == 0:
                                for half in range(2):
                                    mm = pe.matmul(p_score[:, n % 2, a, ds(half * P, P)], qkv[part, q % 2, 0, 0:P],
                                                   qkv[part, q % 2, 1, 0:P], start=True, stop=True)
                                continue
                            mm = pe.matmul(p_score[:, n % 2, a, ds(m * width, width)],
                                           qkv[part, q % 2, 0, ds(blk * P, P)],
                                           qkv[part, q % 2, 1, ds(before * P, width)], start=True, stop=True)
                    mm.then_inc(scored, 1)

                def turns(n):
                    q = pair_of[n]

                    def turn(index, tile):
                        for a in range(2):
                            if index:
                                pe.wait_ge(copied[a], index)
                            for m in range(4):
                                tr = pe.transpose(p_turn[:, a, ds(m * P, P)], tile(a, m), ident[:, :])
                            tr.then_inc(turned[a], 1)

                    if first_of[n]:
                        for half in range(2):
                            turn(turn_of[n] - 2 + half, lambda a, m: qkv[:, q % 2, 2, ds((8 * half + 4 * a + m) * P, P)])
                    pe.wait_ge(exped, n + 1)
                    turn(turn_of[n], lambda a, m: prob[:, n % 2, a, ds(m * P, P)])

                def weigh(n):
                    g, pair, b, step, width = units[n]
                    q = pair_of[n]
                    for a in range(2):
                        pe.wait_ge(copied[a], turn_of[n] + 1)
                    if n >= 2:
                        pe.wait_ge(res_ready, n - 1)
                    halves = width // P
                    for a in range(2):
                        for m in range(step):
                            for half in range(halves):
                                blk = max(b + m + half + 1 - halves, 0)
                                mm = pe.matmul(p_out[:, n % 2, ds((m * 2 + a) * 64, 64)],
                                               probT[:, n % 2, a, ds((m * halves + half) * P, P)],
                                               v[:, q % 2, blk, ds(64 * a, 64)], start=(half == 0), stop=(half == halves - 1))
                    mm.then_inc(weighed, 1)

                scores(0)
                scores(1)
                for n in range(N):
                    turns(n)
                    if n + 2 < N:
                        scores(n + 2)
                    weigh(n)

            @block.scalar
            def _(act):
                def exps(n):
                    step, width = units[n][3:]
                    act.wait_ge(negated, n + 1)
                    if n >= 2:
                        act.wait_ge(turned[1], turn_of[n - 2] + 1)
                    for a in range(2):
                        for m in range(step):
                            ins = nc.scalar.activation(prob[:, n % 2, a, ds(m * width, width)],
                                                       score[:, n % 2, a, ds(m * width, width)], ACT.Exp,
                                                       bias=neg[:, n % 2, a, m:m + 1],
                                                       accum_out=res[:, n % 4, m, a, 65:66])
                    ins.then_inc(exped, 1)

                exps(0)
                for n in range(N):
                    if n + 1 < N:
                        exps(n + 1)
                    copies(act, lambda d, x: nc.scalar.activation(d, x, ACT.Copy), n, 0)

            @block.vector
            def _(dve):
                def soft(n):
                    g, pair, b, step, width = units[n]
                    q = pair_of[n]
                    dve.wait_ge(scored, n + 1)
                    dve.wait_ge(bias_ready, 2 * (q + 1))
                    if n >= 2:
                        dve.wait_ge(exped, n - 1)
                    if n >= 4:
                        dve.wait_ge(stored[n % 4], 16 * (n // 4))
                    first = width == P or b % (TILES // DILATIONS[g]) == 0
                    for a in range(2):
                        dve.scalar_tensor_tensor(out=score[:, n % 2, a, :], in0=p_score[:, n % 2, a, :], scalar=64 ** -0.5,
                                                 in1=bias[:, q % 2, a, ds(0 if first else 256, 512)],
                                                 op0=ALU.mult, op1=ALU.add).then_inc(biased, 1)
                    dve.wait_ge(biased, 2 * n + 2)
                    top = res[:, n % 4, 0:step, :, 64].rearrange("p b a -> p a b")
                    dve.tensor_reduce(top, score[:, n % 2, :, :].rearrange("p a (b w) -> p a b w", w=width), AX.X, ALU.max
                                      ).then_inc(maxed, 1)
                    dve.wait_ge(maxed, n + 1)
                    dve.tensor_scalar(neg[:, n % 2, :, 0:step], top, -1.0, None, ALU.mult).then_inc(negated, 1)

                def take(n):
                    step = units[n][3]
                    dve.wait_ge(weighed, n + 1)
                    dve.tensor_copy(res[:, n % 4, 0:step, :, 0:64],
                                    p_out[:, n % 2, 0:step * P].rearrange("p (b a f) -> p b a f", a=2, f=64)
                                    ).then_inc(res_ready, 1)

                soft(0)
                for n in range(N):
                    if n + 1 < N:
                        soft(n + 1)
                    if n >= 1:
                        take(n - 1)
                    copies(dve, dve.tensor_copy, n, 1)
                take(N - 1)


def merge(nc, proj, att, ident, w_pool_group, pool_scale, w_branch_pool, w_branch_att, merged):
    HALF = SEQ // 2
    KP, KA = POOL_TILES, 2
    with ExitStack() as ctx:
        s = Scope(nc, ctx, "merge")
        z_hi, z_lo = s.sb("z_hi", [P, KP, SEQ], F32R), s.sb("z_lo", [P, KP, SEQ], F32R)
        o_hi, o_lo = s.sb("o_hi", [P, KA, SEQ], F32R), s.sb("o_lo", [P, KA, SEQ], F32R)
        w_hi, w_lo = s.sb("w_hi", [P, KP + KA, D], F32R), s.sb("w_lo", [P, KP + KA, D], F32R)
        w_raw = s.sb("w_raw", [P, 2, D])
        pooled = s.sb("pooled", [P, 2, HALF])
        wg = s.sb("wg", [P, KP, P])
        scale = s.sb("scale", [P, KP])
        heads = s.sb("heads", [P, 2, 3, HPG, ROW])
        top = s.sb("top", [P, HPG])
        coef = s.sb("coef", [P, 3, HPG])
        part = s.sb("part", [P, 3, HPG])
        total = s.sb("total", [P, HPG])
        term = s.sb("term", [P, 3, HPG, 64])
        o = s.sb("o", [P, 2, KA * P])
        gate = s.sb("gate", [P, 2, 2, HALF])
        m = s.sb("m", [P, 2, HALF])
        psum = s.ps("psum", [P, 8, 512])
        w_loaded = [s.sem(f"w_loaded{i}") for i in range(2)]
        pooled_loaded = [s.sem(f"pooled_loaded{i}") for i in range(2)]
        heads_loaded = [s.sem(f"heads_loaded{i}") for i in range(2)]
        gate_loaded = [s.sem(f"gate_loaded{i}") for i in range(2)]
        m_stored = [s.sem(f"m_stored{i}") for i in range(2)]
        (small_loaded, w_hi_ready, w_lo_ready, z_summed, z_hi_ready, z_lo_ready, steps, shifted, coef_exp, o_ready,
         o_turned, o_hi_ready, o_lo_ready, gated, y_summed, gate_applied, m_ready) = (s.sem(n) for n in (
             "small_loaded", "w_hi_ready", "w_lo_ready", "z_summed", "z_hi_ready", "z_lo_ready", "steps", "shifted",
             "coef_exp", "o_ready", "o_turned", "o_hi_ready", "o_lo_ready", "gated", "y_summed", "gate_applied", "m_ready"))
        UNITS = KD * 2
        z_bank = lambda n: 2 * (n % 2)
        with nc.Block() as block:
            @block.sync
            def _(sp):
                sp.dma_start(wg[:, :, :], w_pool_group[0].rearrange("g c d -> c g d")).then_inc(small_loaded, 16)
                sp.dma_start(scale[:, :], pool_scale[0].rearrange("(g p) -> p g", p=P),
                             allow_slow_non_contiguous=True).then_inc(small_loaded, 16)
                for n in range(2 * KP):
                    g, half = divmod(n, 2)
                    if n >= 2:
                        sp.wait_ge(z_summed, n - 1)
                    sp.dma_start(pooled[:, n % 2, :], proj[ds(g * P, P), ds(half * HALF, HALF)]).then_inc(pooled_loaded[n % 2], 16)
                for t in range(TILES):
                    if t >= 2:
                        sp.wait_ge(o_ready, t - 1)
                    sp.dma_start(heads[:, t % 2, :, :, :].rearrange("p g h f -> p g (h f)"),
                                 att[:, ds(t * P, P), :].rearrange("g p f -> p g f")).then_inc(heads_loaded[t % 2], 16)
                    if t < KP + KA:
                        if t >= 2:
                            sp.wait_ge(w_lo_ready, t - 1)
                        rows = w_branch_pool[0, ds(t * P, P), :] if t < KP else w_branch_att[0, ds((t - KP) * P, P), :]
                        sp.dma_start(w_raw[:, t % 2, :], rows).then_inc(w_loaded[t % 2], 16)

                def load_gates(n):
                    d, half = divmod(n, 2)
                    if n >= 2:
                        sp.wait_ge(gate_applied, 4 * (n - 1))
                    for b in range(2):
                        sp.dma_start(gate[:, n % 2, b, :], proj[ds((GATE_TILE + b * KD + d) * P, P), ds(half * HALF, HALF)]
                                     ).then_inc(gate_loaded[n % 2], 16)

                load_gates(0)
                for n in range(UNITS):
                    if n + 1 < UNITS:
                        load_gates(n + 1)
                    d, half = divmod(n, 2)
                    sp.wait_ge(m_ready, 2 * (n + 1))
                    sp.dma_start(merged[ds(d * P, P), ds(half * HALF, HALF)], m[:, n % 2, :]).then_inc(m_stored[n % 2], 16)
                for i in range(2):
                    sp.wait_ge(m_stored[i], 16 * UNITS // 2)

            @block.scalar
            def _(act):
                for n in range(2 * KP):
                    g, half = divmod(n, 2)
                    act.wait_ge(z_summed, n + 1)
                    nc.scalar.activation(z_hi[:, g, ds(half * HALF, HALF)],
                                         psum[:, z_bank(n):z_bank(n) + 2, :].rearrange("p b c -> p (b c)"),
                                         ACT.Copy, scale=scale[:, g:g + 1]).then_inc(z_hi_ready, 1)
                for t in range(TILES):
                    if t < KP + KA:
                        act.wait_ge(w_loaded[t % 2], 16 * (t // 2 + 1))
                        nc.scalar.activation(w_hi[:, t, :], w_raw[:, t % 2, :], ACT.Copy).then_inc(w_hi_ready, 1)
                    act.wait_ge(shifted, t + 1)
                    nc.scalar.activation(coef[:, :, :], coef[:, :, :], ACT.Exp).then_inc(coef_exp, 1)
                    act.wait_ge(o_turned, t + 1)
                    nc.scalar.activation(o_hi[:, :, ds(t * P, P)],
                                         psum[:, 4 + t % 2, 0:KA * P].rearrange("p (k c) -> p k c", c=P),
                                         ACT.Copy).then_inc(o_hi_ready, 1)
                for n in range(UNITS):
                    act.wait_ge(gate_loaded[n % 2], 32 * (n // 2 + 1))
                    nc.scalar.activation(gate[:, n % 2, :, :], gate[:, n % 2, :, :], ACT.Sigmoid).then_inc(gated, 1)

            @block.gpsimd
            def _(pool):
                for t in range(KP + KA):
                    pool.wait_ge(w_hi_ready, t + 1)
                    pool.tensor_tensor(w_lo[:, t, :], w_raw[:, t % 2, :], w_hi[:, t, :], ALU.subtract).then_inc(w_lo_ready, 1)
                for n in range(UNITS):
                    for q in range(2):
                        pool.wait_ge(gate_applied, 4 * n + 2 * q + 2)
                        if n >= 2:
                            pool.wait_ge(m_stored[n % 2], 16 * (n // 2))
                        tok = ds(q * 512, 512)
                        pool.tensor_tensor(m[:, n % 2, tok], gate[:, n % 2, 0, tok], gate[:, n % 2, 1, tok], ALU.add
                                           ).then_inc(m_ready, 1)

            @block.tensor
            def _(pe):
                pe.wait_ge(small_loaded, 32)
                for n in range(2 * KP):
                    pe.wait_ge(pooled_loaded[n % 2], 16 * (n // 2 + 1))
                    if n >= 2:
                        pe.wait_ge(z_lo_ready, n - 1)
                    for q in range(2):
                        mm = pe.matmul(psum[:, z_bank(n) + q, :], wg[:, n // 2, :], pooled[:, n % 2, ds(q * 512, 512)],
                                       start=True, stop=True)
                    mm.then_inc(z_summed, 1)
                for t in range(TILES):
                    pe.wait_ge(o_ready, t + 1)
                    if t >= 2:
                        pe.wait_ge(o_lo_ready, t - 1)
                    for k in range(KA):
                        tr = pe.transpose(psum[:, 4 + t % 2, ds(k * P, P)], o[:, t % 2, ds(k * P, P)], ident[:, :])
                    tr.then_inc(o_turned, 1)
                pe.wait_ge(z_lo_ready, 2 * KP)
                pe.wait_ge(w_lo_ready, KP + KA)
                pe.wait_ge(o_lo_ready, TILES)
                for n in range(UNITS):
                    d, half = divmod(n, 2)
                    cols = ds(d * P, P)
                    for q in range(2):
                        turn = 2 * n + q
                        if turn >= 4:
                            pe.wait_ge(gate_applied, 2 * (turn - 3))
                        tok = ds(half * HALF + q * 512, 512)
                        for b, (k0, k1, in_hi, in_lo) in enumerate(((0, KP, z_hi, z_lo), (KP, KP + KA, o_hi, o_lo))):
                            bank = psum[:, 2 * (turn % 4) + b, :]
                            for k in range(k0, k1):
                                pe.matmul(bank, w_hi[:, k, cols], in_hi[:, k - k0, tok], start=(k == k0), stop=False)
                                pe.matmul(bank, w_hi[:, k, cols], in_lo[:, k - k0, tok], start=False, stop=False)
                                mm = pe.matmul(bank, w_lo[:, k, cols], in_hi[:, k - k0, tok], start=False, stop=(k == k1 - 1))
                            mm.then_inc(y_summed, 1)

            @block.vector
            def _(dve):
                chain = Chain(dve, steps)
                for n in range(2 * KP):
                    g, half = divmod(n, 2)
                    dve.wait_ge(z_hi_ready, n + 1)
                    tok = ds(half * HALF, HALF)
                    dve.scalar_tensor_tensor(out=z_lo[:, g, tok],
                                             in0=psum[:, z_bank(n):z_bank(n) + 2, :].rearrange("p b c -> p (b c)"),
                                             scalar=scale[:, g:g + 1], in1=z_hi[:, g, tok],
                                             op0=ALU.mult, op1=ALU.subtract).then_inc(z_lo_ready, 1)

                def low(t):
                    dve.wait_ge(o_hi_ready, t + 1)
                    dve.tensor_tensor(o_lo[:, :, ds(t * P, P)], psum[:, 4 + t % 2, 0:KA * P].rearrange("p (k c) -> p k c", c=P),
                                      o_hi[:, :, ds(t * P, P)], ALU.subtract).then_inc(o_lo_ready, 1)

                for t in range(TILES):
                    hd = heads[:, t % 2, :, :, :]
                    dve.wait_ge(heads_loaded[t % 2], 16 * (t // 2 + 1))
                    chain.link(dve.tensor_tensor(top[:, :], hd[:, 0, :, 64], hd[:, 1, :, 64], ALU.max))
                    chain.link(dve.tensor_tensor(top[:, :], top[:, :], hd[:, 2, :, 64], ALU.max))
                    dve.tensor_tensor(coef[:, :, :], hd[:, :, :, 64], top[:, :].unsqueeze(1).to_broadcast([P, 3, HPG]),
                                      ALU.subtract).then_inc(shifted, 1)
                    if t:
                        low(t - 1)
                    dve.wait_ge(coef_exp, t + 1)
                    chain.link(dve.tensor_tensor(part[:, :, :], coef[:, :, :], hd[:, :, :, 65], ALU.mult))
                    chain.link(dve.tensor_reduce(total[:, :], part[:, :, :].rearrange("p g h -> p h g"), AX.X, ALU.add))
                    chain.link(dve.reciprocal(total[:, :], total[:, :]))
                    chain.link(dve.tensor_tensor(coef[:, :, :], coef[:, :, :],
                                                 total[:, :].unsqueeze(1).to_broadcast([P, 3, HPG]), ALU.mult))
                    chain.link(dve.tensor_tensor(term[:, :, :, :], hd[:, :, :, 0:64],
                                                 coef[:, :, :].unsqueeze(3).to_broadcast([P, 3, HPG, 64]), ALU.mult))
                    if t >= 2:
                        dve.wait_ge(o_turned, t - 1)
                    flat = term[:, :, :, :].rearrange("p g h f -> p g (h f)")
                    chain.link(dve.tensor_tensor(o[:, t % 2, :], flat[:, 0, :], flat[:, 1, :], ALU.add))
                    dve.tensor_tensor(o[:, t % 2, :], o[:, t % 2, :], flat[:, 2, :], ALU.add).then_inc(o_ready, 1)
                low(TILES - 1)
                for n in range(UNITS):
                    dve.wait_ge(gated, n + 1)
                    for q in range(2):
                        turn = 2 * n + q
                        tok = ds(q * 512, 512)
                        for b in range(2):
                            dve.wait_ge(y_summed, 2 * turn + b + 1)
                            dve.tensor_tensor(gate[:, n % 2, b, tok], psum[:, 2 * (turn % 4) + b, :],
                                              gate[:, n % 2, b, tok], ALU.mult).then_inc(gate_applied, 1)


NR = EG + NE


def mix_out(nc, x, merged, w_out, mod_dram, ident, w_group_router, w_expert_router, b_group_router, b_expert_router,
            x1_dram, h_dram, logits):
    with ExitStack() as ctx:
        s = Scope(nc, ctx, "out")
        w_hi, w_lo = s.sb("w_hi", [P, KD, D], F32R), s.sb("w_lo", [P, KD, D], F32R)
        w_raw = s.sb("w_raw", [P, 2, D])
        mT = s.sb("mT", [P, 2, KD, P])
        m_hi, m_lo = s.sb("m_hi", [P, 2, KD, P], F32R), s.sb("m_lo", [P, 2, KD, P], F32R)
        mod = s.sb("mod", [P, 3, D])
        xt = s.sb("xt", [P, 2, D])
        sq = s.sb("sq", [P, D])
        x1 = s.sb("x1", [P, 3, D])
        h = s.sb("h", [P, 2, D])
        hT = s.sb("hT", [P, KD, P])
        wr = s.sb("wr", [P, KD, NR])
        rbias = s.sb("rbias", [P, NR])
        eps = s.sb("eps", [P, 1])
        ms, root, rstd = s.sb("ms", [P, 4]), s.sb("root", [P, 4]), s.sb("rstd", [P, 4])
        y = s.ps("y", [P, 2, D])
        turned_h = s.ps("turned_h", [P, D])
        p_logit = s.ps("p_logit", [P, 2, 512])
        w_loaded = [s.sem(f"w_loaded{i}") for i in range(2)]
        m_loaded = [s.sem(f"m_loaded{i}") for i in range(2)]
        x_loaded = [s.sem(f"x_loaded{i}") for i in range(2)]
        x1_stored = [s.sem(f"x1_stored{i}") for i in range(3)]
        h_stored = [s.sem(f"h_stored{i}") for i in range(2)]
        (small_loaded, eps_ready, w_hi_ready, w_lo_ready, m_hi_ready, m_lo_ready, y_half, y_squared, y_rooted, x_squared,
         x_rooted, recips, y_scaled, x1_ready, h_scaled, h_ready, h_turned, hT_ready, logit_summed, logit_taken) = (
             s.sem(n) for n in (
                 "small_loaded", "eps_ready", "w_hi_ready", "w_lo_ready", "m_hi_ready", "m_lo_ready", "y_half",
                 "y_squared", "y_rooted", "x_squared", "x_rooted", "recips", "y_scaled", "x1_ready", "h_scaled",
                 "h_ready", "h_turned", "hT_ready", "logit_summed", "logit_taken"))
        with nc.Block() as block:
            @block.sync
            def _(sp):
                for k in range(KD):
                    if k >= 2:
                        sp.wait_ge(w_lo_ready, k - 1)
                    sp.dma_start(w_raw[:, k % 2, :], w_out[0, ds(k * P, P), :]).then_inc(w_loaded[k % 2], 16)
                    if k == 1:
                        sp.dma_start(mod[:, :, :].rearrange("p m d -> p (m d)"),
                                     mod_dram[0:1, 2 * D:5 * D].partition_broadcast(P)).then_inc(small_loaded, 16)
                        sp.dma_start(wr[:, :, 0:EG], w_group_router[0].rearrange("(k p) e -> p k e", p=P)).then_inc(small_loaded, 16)
                        sp.dma_start(wr[:, :, EG:NR], w_expert_router[0].rearrange("(k p) e -> p k e", p=P)).then_inc(small_loaded, 16)
                        sp.dma_start(rbias[:, 0:EG], b_group_router[0:1, :].partition_broadcast(P)).then_inc(small_loaded, 16)
                        sp.dma_start(rbias[:, EG:NR], b_expert_router[0:1, :].partition_broadcast(P)).then_inc(small_loaded, 16)
                for t in range(TILES + 1):
                    if t < TILES:
                        if t >= 2:
                            sp.wait_ge(m_lo_ready, t - 1)
                        sp.dma_start(mT[:, t % 2, :, :], merged.rearrange("(k p) t -> p k t", p=P)[:, :, ds(t * P, P)]
                                     ).then_inc(m_loaded[t % 2], 16)
                        if t >= 2:
                            sp.wait_ge(x1_ready, t - 1)
                        sp.dma_start(xt[:, t % 2, :], x[0, ds(t * P, P), :]).then_inc(x_loaded[t % 2], 16)

            @block.scalar
            def _(act):
                act.wait_ge(eps_ready, 1)

                def split(t):
                    if t >= 2:
                        act.wait_ge(y_half, 2 * (t - 1))
                    act.wait_ge(m_loaded[t % 2], 16 * (t // 2 + 1))
                    nc.scalar.activation(m_hi[:, t % 2, :, :], mT[:, t % 2, :, :], ACT.Copy).then_inc(m_hi_ready, 1)

                def squares(src, wait, col, squared, rooted, count):
                    act.wait_ge(*wait)
                    if count >= 2:
                        act.wait_ge(recips, 2 * (count - 2) + 1)
                    nc.scalar.activation(sq[:, :], src, ACT.Square, accum_out=ms[:, col:col + 1]).then_inc(squared, 1)
                    act.wait_ge(squared, count)
                    nc.scalar.activation(root[:, col:col + 1], ms[:, col:col + 1], ACT.Sqrt, scale=1.0 / D,
                                         bias=eps[:, 0:1]).then_inc(rooted, 1)

                for k in range(KD):
                    act.wait_ge(w_loaded[k % 2], 16 * (k // 2 + 1))
                    nc.scalar.activation(w_hi[:, k, :], w_raw[:, k % 2, :], ACT.Copy).then_inc(w_hi_ready, 1)
                split(0)
                split(1)
                for t in range(TILES + 1):
                    if t < TILES:
                        squares(y[:, t % 2, :], (y_half, 2 * t + 2), t % 2, y_squared, y_rooted, t + 1)
                    if t >= 1:
                        if t >= 3:
                            act.wait_ge(h_scaled, t - 2)
                        squares(x1[:, (t - 1) % 3, :], (x1_ready, t), 2 + (t - 1) % 2, x_squared, x_rooted, t)
                    if t + 2 < TILES:
                        split(t + 2)

            @block.gpsimd
            def _(pool):
                pool.memset(eps[:, :], EPS).then_inc(eps_ready, 1)

                def low(t):
                    pool.wait_ge(m_hi_ready, t + 1)
                    pool.tensor_tensor(m_lo[:, t % 2, :, :], mT[:, t % 2, :, :], m_hi[:, t % 2, :, :], ALU.subtract
                                       ).then_inc(m_lo_ready, 1)

                def store_h(t):
                    pool.wait_ge(h_ready, t + 1)
                    pool.dma_start(h_dram[ds(t * P, P), :], h[:, t % 2, :]).then_inc(h_stored[t % 2], 16)

                for k in range(KD):
                    pool.wait_ge(w_hi_ready, k + 1)
                    pool.tensor_tensor(w_lo[:, k, :], w_raw[:, k % 2, :], w_hi[:, k, :], ALU.subtract).then_inc(w_lo_ready, 1)
                low(0)
                low(1)
                pool.wait_ge(small_loaded, 80)
                for t in range(TILES + 1):
                    if t < TILES:
                        pool.wait_ge(y_scaled, t + 1)
                        pool.wait_ge(x_loaded[t % 2], 16 * (t // 2 + 1))
                        pool.tensor_tensor(x1[:, t % 3, :], x1[:, t % 3, :], xt[:, t % 2, :], ALU.add).then_inc(x1_ready, 1)
                    if t >= 1:
                        pool.wait_ge(h_scaled, t)
                        pool.tensor_tensor(h[:, (t - 1) % 2, :], h[:, (t - 1) % 2, :], mod[:, 1, :], ALU.add).then_inc(h_ready, 1)
                    if t < TILES:
                        pool.wait_ge(x1_ready, t + 1)
                        pool.dma_start(x1_dram[ds(t * P, P), :], x1[:, t % 3, :]).then_inc(x1_stored[t % 3], 16)
                    if t >= 1:
                        store_h(t - 1)
                    if t + 2 < TILES:
                        low(t + 2)
                for i in range(3):
                    pool.wait_ge(x1_stored[i], 16 * len(range(i, TILES, 3)))
                for i in range(2):
                    pool.wait_ge(h_stored[i], 16 * TILES // 2)

            @block.tensor
            def _(pe):
                def product(t, half):
                    bank = y[:, t % 2, ds(half * 512, 512)]
                    cols = ds(half * 512, 512)
                    if half == 0:
                        pe.wait_ge(m_lo_ready, t + 1)
                        if t >= 2:
                            pe.wait_ge(y_scaled, t - 1)
                    for k in range(KD):
                        pe.matmul(bank, m_hi[:, t % 2, k, :], w_hi[:, k, cols], start=(k == 0), stop=False)
                        pe.matmul(bank, m_hi[:, t % 2, k, :], w_lo[:, k, cols], start=False, stop=False)
                        mm = pe.matmul(bank, m_lo[:, t % 2, k, :], w_hi[:, k, cols], start=False, stop=(k == KD - 1))
                    mm.then_inc(y_half, 1)

                def turn(t):
                    pe.wait_ge(h_ready, t + 1)
                    if t >= 1:
                        pe.wait_ge(hT_ready, t)
                    for k in range(KD):
                        tr = pe.transpose(turned_h[:, ds(k * P, P)], h[:, t % 2, ds(k * P, P)], ident[:, :])
                    tr.then_inc(h_turned, 1)

                def route(t):
                    pe.wait_ge(hT_ready, t + 1)
                    if t >= 2:
                        pe.wait_ge(logit_taken, t - 1)
                    for k in range(KD):
                        mm = pe.matmul(p_logit[:, t % 2, 0:NR], hT[:, k, :], wr[:, k, :], start=(k == 0), stop=(k == KD - 1))
                    mm.then_inc(logit_summed, 1)

                pe.wait_ge(w_lo_ready, KD)
                pe.wait_ge(small_loaded, 80)
                product(0, 0)
                product(0, 1)
                for t in range(TILES + 1):
                    if t + 1 < TILES:
                        product(t + 1, 0)
                    if t >= 1:
                        turn(t - 1)
                    if t + 1 < TILES:
                        product(t + 1, 1)
                    if t >= 1:
                        route(t - 1)

            @block.vector
            def _(dve):
                dve.wait_ge(small_loaded, 80)
                for t in range(TILES + 1):
                    if t < TILES:
                        dve.wait_ge(y_rooted, t + 1)
                        dve.reciprocal(rstd[:, t % 2:t % 2 + 1], root[:, t % 2:t % 2 + 1]).then_inc(recips, 1)
                        dve.wait_ge(recips, 2 * t if t else 1)
                        if t >= 3:
                            dve.wait_ge(x1_stored[t % 3], 16 * (t // 3))
                            dve.wait_ge(h_scaled, t - 2)
                        dve.scalar_tensor_tensor(out=x1[:, t % 3, :], in0=y[:, t % 2, :], scalar=rstd[:, t % 2:t % 2 + 1],
                                                 in1=mod[:, 0, :], op0=ALU.mult, op1=ALU.mult).then_inc(y_scaled, 1)
                    if t >= 1:
                        u = t - 1
                        col = 2 + u % 2
                        dve.wait_ge(x_rooted, t)
                        if u >= 2:
                            dve.wait_ge(h_stored[u % 2], 16 * (u // 2))
                            dve.wait_ge(h_turned, u - 1)
                        dve.reciprocal(rstd[:, col:col + 1], root[:, col:col + 1]).then_inc(recips, 1)
                        dve.wait_ge(recips, 2 * t + 1 if t < TILES else 2 * TILES)
                        dve.scalar_tensor_tensor(out=h[:, u % 2, :], in0=x1[:, u % 3, :], scalar=rstd[:, col:col + 1],
                                                 in1=mod[:, 2, :], op0=ALU.mult, op1=ALU.mult).then_inc(h_scaled, 1)
                        dve.wait_ge(h_turned, t)
                        if u >= 1:
                            dve.wait_ge(logit_summed, u)
                        dve.tensor_copy(hT[:, :, :].rearrange("p k c -> p (k c)"), turned_h[:, :]).then_inc(hT_ready, 1)
                        dve.wait_ge(logit_summed, t)
                        dve.tensor_tensor(logits[:, u, :], p_logit[:, u % 2, 0:NR], rbias[:, :], ALU.add).then_inc(logit_taken, 1)


def route(nc, logits, slot_token, dest, share, table, slot_rows):
    L, T2 = TILES, 2
    with ExitStack() as ctx:
        s = Scope(nc, ctx, "route")
        iota_e, iota_b = s.sb("iota_e", [P, NE]), s.sb("iota_b", [P, NB + 1])
        thr = s.sb("thr", [P, L])
        upper, ones = s.sb("upper", [P, P]), s.sb("ones", [P, P])
        token = s.sb("token", [P, L], I32)
        none = s.sb("none", [P, NB], I32)
        gmax, gsum, gsel = s.sb("gmax", [P, L]), s.sb("gsum", [P, L]), s.sb("gsel", [P, L])
        gexp, gtmp = s.sb("gexp", [P, L, EG]), s.sb("gtmp", [P, L, EG])
        el, etmp = s.sb("el", [P, L, NE]), s.sb("etmp", [P, L, NE])
        pick = s.sb("pick", [P, T2, L, NE])
        both = s.sb("both", [P, L, NE])
        top, sel = s.sb("top", [P, T2, L]), s.sb("sel", [P, L])
        d, ex = s.sb("d", [P, L]), s.sb("ex", [P, L])
        count = s.sb("count", [P, NE])
        over = s.sb("over", [P, NE, L])
        nblk, end = s.sb("nblk", [P, NE]), s.sb("end", [P, 2, NE])
        start = s.sb("start", [P, L, NE])
        pos = s.sb("pos", [P, L, NE])
        where = s.sb("where", [P, T2, L])
        index, index2 = s.sb("index", [P, T2 * L], I32), s.sb("index2", [P, T2 * L], I32)
        cmp = s.sb("cmp", [1, NB + 1, NE])
        before = s.sb("before", [1, NB + 1, NB + 1])
        blk, tabf = s.sb("blk", [1, NB + 1]), s.sb("tabf", [1, 4, NB + 1])
        p_rank, p_total = s.ps("p_rank", [P, 512]), s.ps("p_total", [P, 512])
        (made, consts, steps, shifted, exped, picked, ranked, index_ready, cleared, scattered, slots_read, table_ready) = (
            s.sem(n) for n in ("made", "consts", "steps", "shifted", "exped", "picked", "ranked", "index_ready",
                               "cleared", "scattered", "slots_read", "table_ready"))
        def over_experts(a, n=NE):
            return a.unsqueeze(2).to_broadcast([P, L, n])

        def over_tiles(a, n=NE):
            return a.unsqueeze(1).to_broadcast([P, L, n])

        with nc.Block() as block:
            @block.gpsimd
            def _(pool):
                chain = Chain(pool, made)
                pool.iota(iota_e[:, :], pattern=[[1, NE]], base=0, channel_multiplier=0, allow_small_or_imprecise_dtypes=True)
                pool.iota(iota_b[:, :], pattern=[[1, NB + 1]], base=0, channel_multiplier=0, allow_small_or_imprecise_dtypes=True)
                pool.iota(thr[:, :], pattern=[[P, L]], base=0, channel_multiplier=0, allow_small_or_imprecise_dtypes=True)
                pool.iota(token[:, :], pattern=[[P, L]], base=0, channel_multiplier=1)
                pool.memset(none[:, :], 0)
                chain.link(pool.memset(ones[:, :], 1.0))
                pool.affine_select(out=upper[:, :], in_=ones[:, :], compare_op=ALU.is_gt, fill=0.0, base=0,
                                   pattern=[[1, P]], channel_multiplier=-1).then_inc(consts, 1)
                pool.wait_ge(consts, 1)
                pool.dma_start(slot_token.rearrange("(p b) o -> p (b o)", b=NB), none[:, :]).then_inc(cleared, 16)
                pool.wait_ge(index_ready, 1)
                pool.wait_ge(cleared, 16)
                for n in range(T2 * L):
                    pool.indirect_dma_start(out=slot_token, out_offset=bass.IndirectOffsetOnAxis(ap=index[:, n:n + 1], axis=0),
                                            in_=token[:, n % L:n % L + 1], in_offset=None).then_inc(scattered, 16)
                pool.wait_ge(scattered, 16 * T2 * L)
                pool.dma_start(slot_rows[:, 0:NB], slot_token.rearrange("(p b) o -> p (b o)", b=NB)).then_inc(slots_read, 16)
                pool.memset(slot_rows[:, NB:NB + 2], 0).then_inc(made, 1)
                pool.wait_ge(slots_read, 16)
                pool.wait_ge(made, 2)

            @block.tensor
            def _(pe):
                pe.wait_ge(picked, 1)
                pe.wait_ge(consts, 1)
                pe.matmul(p_rank[:, :], upper[:, :], both[:, :, :].rearrange("p t e -> p (t e)"), start=True, stop=True)
                pe.matmul(p_total[:, :], ones[:, :], both[:, :, :].rearrange("p t e -> p (t e)"), start=True, stop=True
                          ).then_inc(ranked, 1)

            @block.scalar
            def _(act):
                act.wait_ge(shifted, 1)
                nc.scalar.activation(gexp[:, :, :], gexp[:, :, :], ACT.Exp).then_inc(exped, 1)
                act.wait_ge(shifted, 2)
                nc.scalar.activation(ex[:, :], d[:, :], ACT.Exp).then_inc(exped, 1)

            @block.vector
            def _(dve):
                chain = Chain(dve, steps)
                tt = dve.tensor_tensor
                gl = logits[:, :, 0:EG]
                chain.link(dve.tensor_reduce(gmax[:, :], gl, AX.X, ALU.max))
                tt(gexp[:, :, :], gl, over_experts(gmax[:, :], EG), ALU.subtract).then_inc(shifted, 1)
                dve.wait_ge(consts, 1)

                def first_highest(out, one_hot, tmp, values, highest, n):
                    chain.link(tt(tmp, values, over_experts(highest, n), ALU.is_equal))
                    chain.link(dve.scalar_tensor_tensor(out=tmp, in0=tmp, scalar=-float(NE), in1=over_tiles(iota_e[:, 0:n], n),
                                                        op0=ALU.mult, op1=ALU.add))
                    chain.link(dve.tensor_reduce(out, tmp, AX.X, ALU.min))
                    chain.link(dve.tensor_scalar(out, out, float(NE), None, ALU.add))
                    chain.link(tt(one_hot, over_tiles(iota_e[:, 0:n], n), over_experts(out, n), ALU.is_equal))

                first_highest(gsel[:, :], gtmp[:, :, :], gtmp[:, :, :], gl, gmax[:, :], EG)
                chain.link(dve.tensor_scalar(gtmp[:, :, :], gtmp[:, :, :], MASKED, -MASKED, ALU.mult, ALU.add))
                chain.link(tt(el[:, :, :].rearrange("p t (g e) -> p t g e", g=EG),
                              logits[:, :, EG:NR].rearrange("p t (g e) -> p t g e", g=EG),
                              gtmp[:, :, :].unsqueeze(3).to_broadcast([P, L, EG, EPG]), ALU.add))
                chain.link(dve.tensor_reduce(top[:, 0, :], el[:, :, :], AX.X, ALU.max))
                first_highest(sel[:, :], pick[:, 0, :, :], etmp[:, :, :], el[:, :, :], top[:, 0, :], NE)
                chain.link(dve.scalar_tensor_tensor(out=el[:, :, :], in0=pick[:, 0, :, :], scalar=-3.0 * MASKED, in1=el[:, :, :],
                                                    op0=ALU.mult, op1=ALU.add))
                chain.link(dve.tensor_reduce(top[:, 1, :], el[:, :, :], AX.X, ALU.max))
                tt(d[:, :], top[:, 1, :], top[:, 0, :], ALU.subtract).then_inc(shifted, 1)
                first_highest(sel[:, :], pick[:, 1, :, :], etmp[:, :, :], el[:, :, :], top[:, 1, :], NE)
                tt(both[:, :, :], pick[:, 0, :, :], pick[:, 1, :, :], ALU.add).then_inc(picked, 1)
                dve.wait_ge(exped, 2)
                chain.link(dve.tensor_reduce(gsum[:, :], gexp[:, :, :], AX.X, ALU.add))
                chain.link(dve.tensor_scalar(d[:, :], ex[:, :], 1.0, None, ALU.add))
                chain.link(tt(gsum[:, :], gsum[:, :], d[:, :], ALU.mult))
                chain.link(dve.reciprocal(share[:, 0, :], gsum[:, :]))
                chain.link(tt(share[:, 1, :], share[:, 0, :], ex[:, :], ALU.mult))
                dve.wait_ge(ranked, 1)
                total = p_total[:, :].rearrange("p (t e) -> p t e", e=NE)
                chain.link(dve.tensor_reduce(count[:, :], p_total[:, :].rearrange("p (t e) -> p e t", e=NE), AX.X, ALU.add))
                chain.link(tt(over[:, :, :], count[:, :].unsqueeze(2).to_broadcast([P, NE, L]),
                              thr[:, :].unsqueeze(1).to_broadcast([P, NE, L]), ALU.is_gt))
                chain.link(dve.tensor_reduce(nblk[:, :], over[:, :, :], AX.X, ALU.add))
                reach, now = 1, nblk[:, :]
                while reach < NE:
                    new = end[:, reach.bit_length() % 2, :]
                    dve.tensor_copy(new[:, :reach], now[:, :reach])
                    chain.link(tt(new[:, reach:], now[:, reach:], now[:, :NE - reach], ALU.add))
                    reach, now = 2 * reach, new
                chain.link(tt(start[:, 0, :], now, nblk[:, :], ALU.subtract))
                chain.link(dve.tensor_scalar(start[:, 0, :], start[:, 0, :], float(P), None, ALU.mult))
                for t in range(1, L):
                    chain.link(tt(start[:, t, :], start[:, t - 1, :], total[:, t - 1, :], ALU.add))
                chain.link(tt(pos[:, :, :], start[:, :, :], p_rank[:, :].rearrange("p (t e) -> p t e", e=NE), ALU.add))
                for choice in range(T2):
                    chain.link(tt(etmp[:, :, :], pick[:, choice, :, :], pos[:, :, :], ALU.mult))
                    chain.link(dve.tensor_reduce(where[:, choice, :], etmp[:, :, :], AX.X, ALU.add))
                chain.link(dve.tensor_copy(dest[:, :, :], where[:, :, :]))
                flat = dest[:, :, :].rearrange("p c t -> p (c t)")
                chain.link(dve.tensor_scalar(index[:, :], flat, P - 1, 6, ALU.bitwise_and, ALU.logical_shift_left))
                chain.link(dve.tensor_scalar(index2[:, :], flat, 7, None, ALU.logical_shift_right))
                tt(index[:, :], index[:, :], index2[:, :], ALU.bitwise_or).then_inc(index_ready, 1)
                last = now[0:1, NE - 1:NE]
                chain.link(dve.tensor_scalar(blk[:, 0:1], last, -1.0, None, ALU.add))
                chain.link(tt(blk[:, 1:], iota_b[0:1, 1:], blk[:, 0:1].to_broadcast([1, NB]), ALU.min))
                chain.link(dve.memset(blk[:, 0:1], 0.0))
                chain.link(tt(cmp[:, :, :], blk[:, :].unsqueeze(2).to_broadcast([1, NB + 1, NE]),
                              now[0:1, :].unsqueeze(1).to_broadcast([1, NB + 1, NE]), ALU.is_ge))
                chain.link(dve.tensor_reduce(tabf[:, 0, :], cmp[:, :, :], AX.X, ALU.add))
                chain.link(dve.memset(tabf[:, 1, 0:1], 0.0))
                chain.link(tt(tabf[:, 1, 1:], tabf[:, 0, 1:], tabf[:, 0, 0:NB], ALU.is_gt))
                reach, src = 1, tabf[:, 1, :]
                spare = (tabf[:, 2, :], tabf[:, 3, :])
                turn = 0
                while reach < NB + 1:
                    new = spare[turn % 2]
                    dve.tensor_copy(new[:, :reach], src[:, :reach])
                    chain.link(tt(new[:, reach:], src[:, reach:], src[:, :NB + 1 - reach], ALU.add))
                    reach, src, turn = 2 * reach, new, turn + 1
                spot = spare[turn % 2]
                chain.link(dve.tensor_scalar(spot, src, -1.0, None, ALU.add))
                chain.link(tt(before[:, :, :], spot.unsqueeze(2).to_broadcast([1, NB + 1, NB + 1]),
                              src.unsqueeze(1).to_broadcast([1, NB + 1, NB + 1]), ALU.is_gt))
                chain.link(dve.tensor_reduce(spot, before[:, :, :], AX.X, ALU.add))
                dve.tensor_copy(table[:, 4, :], spot)
                dve.tensor_copy(table[:, 2, :], src)
                dve.tensor_copy(table[:, 0, :], tabf[:, 0, :])
                dve.tensor_copy(table[:, 1, :], tabf[:, 1, :])
                dve.tensor_copy(table[:, 3, 0:1], last).then_inc(table_ready, 1)
                dve.wait_ge(table_ready, 1)


def experts(nc, table, slot_rows, ident, h_dram, w_gate, w_up, w_down, y_dram):
    with ExitStack() as ctx:
        s = Scope(nc, ctx, "moe")
        wg = s.sb("wg", [P, 2, KD, DE])
        wu = s.sb("wu", [P, 2, KD, DE])
        wd = s.sb("wd", [P, 2, KE, D])
        row = s.sb("row", [P, 2], I32)
        xg = s.sb("xg", [P, 2, D])
        xT = s.sb("xT", [P, 2, KD, P])
        act_g = s.sb("act_g", [P, 2, DE])
        hid = s.sb("hid", [P, 2, DE])
        hT = s.sb("hT", [P, 2, KE, P])
        ys = s.sb("ys", [P, 2, D])
        p_x = s.ps("p_x", [P, D])
        p_gate, p_up = s.ps("p_gate", [P, DE]), s.ps("p_up", [P, DE])
        p_h = s.ps("p_h", [P, DE])
        p_y = s.ps("p_y", [P, D])
        w_loaded = [[s.sem(f"{n}_loaded{i}") for i in range(2)] for n in ("gate", "up", "down")]
        gathered = [s.sem(f"gathered{i}") for i in range(2)]
        y_stored = [s.sem(f"y_stored{i}") for i in range(2)]
        zero = s.sb("zero", [P, D])
        row_seen, all_stored, zeroed, rest_zeroed = s.sem("row_seen"), s.sem("all_stored"), s.sem("zeroed"), s.sem("rest_zeroed")
        (row_ready, x_turned, xT_ready, gate_summed, up_summed, silu_ready, hid_ready, h_turned, hT_ready, block_done,
         y_ready) = (s.sem(n) for n in ("row_ready", "x_turned", "xT_ready", "gate_summed", "up_summed", "silu_ready",
                                        "hid_ready", "h_turned", "hT_ready", "block_done", "y_ready"))

        def entry(eng, r, b, top):
            return eng.value_load(table[0:1, r, ds(b, 1)], min_val=0, max_val=top)

        def by_twos(eng, body):
            count = entry(eng, 3, 0, NB)
            with eng.Fori(0, NB // 2) as i:
                with eng.If(2 * i < count):
                    body(i)
            return count

        with nc.Block() as block:
            @block.sync
            def _(sp):
                def load(e, slot):
                    for (dst, src), loaded in zip(((wg, w_gate), (wu, w_up), (wd, w_down)), w_loaded):
                        sp.dma_start(dst[:, slot, :, :], src[0, ds(e, 1), :, :].rearrange("e (k p) f -> p (e k) f", p=P)
                                     ).then_inc(loaded[slot], 16)

                load(entry(sp, 0, 0, NE - 1), 0)

                def body(i):
                    for u in range(2):
                        b = 2 * i + u
                        if u == 0:
                            with sp.If(i > 0):
                                reload(b)
                        else:
                            reload(b)

                def reload(b):
                    with sp.If(entry(sp, 1, b, 1) > 0):
                        sp.wait_ge(block_done, entry(sp, 4, b, NB) + 1)
                        e = entry(sp, 0, b, NE - 1)
                        odd = entry(sp, 2, b, NE) & 1
                        with sp.If(odd > 0):
                            load(e, 1)
                        with sp.Else():
                            load(e, 0)
                count = by_twos(sp, body)
                sp.wait_ge(zeroed, 1)
                with sp.Fori(0, NB // 2) as i:
                    with sp.If(2 * i >= count):
                        for u in range(2):
                            sp.dma_start(y_dram[ds((2 * i + u) * P, P), :], zero[:, :]).then_inc(rest_zeroed, 16)
                    with sp.Else():
                        sp.sem_inc(rest_zeroed, 32)
                sp.wait_ge(rest_zeroed, 16 * NB)

            @block.gpsimd
            def _(pool):
                def gather(b, u):
                    pool.wait_ge(x_turned, b + 1)
                    pool.tensor_copy(row[:, u:u + 1], slot_rows[:, ds(b, 1)]).then_inc(row_ready, 1)
                    pool.wait_ge(row_ready, b + 1)
                    pool.sem_inc(row_seen, 1)
                    pool.indirect_dma_start(out=xg[:, u, :], out_offset=None, in_=h_dram,
                                            in_offset=bass.IndirectOffsetOnAxis(ap=row[:, u:u + 1], axis=0)
                                            ).then_inc(gathered[u], 16)

                pool.memset(zero[:, :], 0.0).then_inc(zeroed, 1)
                gather(0, 0)
                gather(1, 1)
                by_twos(pool, lambda i: [gather(2 * i + 2, 0), gather(2 * i + 3, 1)])

            @block.tensor
            def _(pe):
                pe.sem_inc(x_turned, 2)
                pe.sem_inc(block_done, 1)
                for n in range(3):
                    pe.sem_inc(w_loaded[n][1], 16)

                def turn_x(b, u):
                    pe.wait_ge(gathered[u], 16 * ((b + 2) // 2) if isinstance(b, int) else 8 * b + (16 - 8 * u))
                    pe.wait_ge(xT_ready, b + 1)
                    for k in range(KD):
                        tr = pe.transpose(p_x[:, ds(k * P, P)], xg[:, u, ds(k * P, P)], ident[:, :])
                    tr.then_inc(x_turned, 1)

                def block_of(b, u):
                    n = entry(pe, 2, b, NE)
                    slot = n & 1
                    even, odd = 16 * ((n >> 1) + 1), 16 * (((n + 1) >> 1) + 1)

                    def weights_of(which):
                        pe.wait_ge(w_loaded[which][0], even)
                        pe.wait_ge(w_loaded[which][1], odd)

                    pe.wait_ge(xT_ready, b + 2)
                    pe.wait_ge(silu_ready, b + 1)
                    pe.wait_ge(hid_ready, b + 1)
                    for which, (bank, w, summed) in enumerate(((p_gate, wg, gate_summed), (p_up, wu, up_summed))):
                        weights_of(which)
                        for k in range(KD):
                            mm = pe.matmul(bank[:, :], xT[:, u, k, :], w[:, ds(slot, 1), k, :].rearrange("p a f -> p (a f)"),
                                           start=(k == 0), stop=(k == KD - 1))
                        mm.then_inc(summed, 1)
                    turn_x(b + 1, 1 - u)
                    pe.wait_ge(hid_ready, b + 2)
                    pe.wait_ge(hT_ready, b + 1)
                    for k in range(KE):
                        tr = pe.transpose(p_h[:, ds(k * P, P)], hid[:, u, ds(k * P, P)], ident[:, :])
                    tr.then_inc(h_turned, 1)
                    weights_of(2)
                    pe.wait_ge(hT_ready, b + 2)
                    pe.wait_ge(y_ready, b + 1)
                    for half in range(2):
                        for k in range(KE):
                            mm = pe.matmul(p_y[:, ds(half * 512, 512)], hT[:, u, k, :],
                                           wd[:, ds(slot, 1), k, ds(half * 512, 512)].rearrange("p a f -> p (a f)"),
                                           start=(k == 0), stop=(k == KE - 1))
                    mm.then_inc(block_done, 1)

                turn_x(0, 0)
                by_twos(pe, lambda i: [block_of(2 * i, 0), block_of(2 * i + 1, 1)])

            @block.scalar
            def _(act):
                def take_x(b, u):
                    act.wait_ge(x_turned, b + 3)
                    act.wait_ge(up_summed, b + 1)
                    nc.scalar.activation(xT[:, u, :, :].rearrange("p k c -> p (k c)"), p_x[:, :], ACT.Copy).then_inc(xT_ready, 1)

                def block_of(b, u):
                    act.wait_ge(gate_summed, b + 1)
                    nc.scalar.activation(act_g[:, u, :], p_gate[:, :], ACT.Silu).then_inc(silu_ready, 1)
                    take_x(b + 1, 1 - u)
                    act.wait_ge(y_ready, b + 2)
                    act.dma_start(y_dram[ds(b * P, P), :], ys[:, u, :]).then_inc(y_stored[u], 16)

                act.sem_inc(xT_ready, 1)
                act.sem_inc(silu_ready, 1)
                take_x(0, 0)
                count = by_twos(act, lambda i: [block_of(2 * i, 0), block_of(2 * i + 1, 1)])
                for u in range(2):
                    act.wait_ge(y_stored[u], 16 * ((count + 1) >> 1) + 16)
                    act.sem_inc(all_stored, 1)

            @block.vector
            def _(dve):
                dve.sem_inc(up_summed, 2)
                for sem in (hid_ready, hT_ready, y_ready):
                    dve.sem_inc(sem, 1)
                for u in range(2):
                    dve.sem_inc(y_stored[u], 16)

                def block_of(b, u):
                    dve.wait_ge(silu_ready, b + 2)
                    dve.wait_ge(up_summed, b + 3)
                    dve.tensor_tensor(hid[:, u, :], p_up[:, :], act_g[:, u, :], ALU.mult).then_inc(hid_ready, 1)
                    dve.wait_ge(h_turned, b + 1)
                    dve.tensor_copy(hT[:, u, :, :].rearrange("p k c -> p (k c)"), p_h[:, :]).then_inc(hT_ready, 1)
                    dve.wait_ge(block_done, b + 2)
                    dve.wait_ge(y_stored[u], 8 * b + (16 - 8 * u))
                    dve.tensor_copy(ys[:, u, :], p_y[:, :]).then_inc(y_ready, 1)

                by_twos(dve, lambda i: [block_of(2 * i, 0), block_of(2 * i + 1, 1)])


def combine(nc, dest, share, y_dram, x1_dram, mod_dram, out):
    BUF = 3
    with ExitStack() as ctx:
        s = Scope(nc, ctx, "comb")
        yy = s.sb("yy", [P, BUF, 2, D])
        x1 = s.sb("x1", [P, BUF, D])
        y = s.sb("y", [P, BUF, D])
        sq = s.sb("sq", [P, D])
        mod = s.sb("mod", [P, D])
        eps = s.sb("eps", [P, 1])
        ms, root, rstd = s.sb("ms", [P, 2]), s.sb("root", [P, 2]), s.sb("rstd", [P, 2])
        gathered = [s.sem(f"gathered{i}") for i in range(BUF)]
        x_loaded = [s.sem(f"x_loaded{i}") for i in range(BUF)]
        stored = [s.sem(f"stored{i}") for i in range(BUF)]
        mod_loaded, eps_ready, first, mixed, squared, rooted, recips, scaled, summed = (s.sem(n) for n in (
            "mod_loaded", "eps_ready", "first", "mixed", "squared", "rooted", "recips", "scaled", "summed"))
        with nc.Block() as block:
            @block.gpsimd
            def _(pool):
                pool.memset(eps[:, :], EPS).then_inc(eps_ready, 1)

                for t in range(TILES):
                    if t >= BUF:
                        pool.wait_ge(mixed, t - BUF + 1)
                    for c in range(2):
                        pool.indirect_dma_start(out=yy[:, t % BUF, c, :], out_offset=None, in_=y_dram,
                                                in_offset=bass.IndirectOffsetOnAxis(ap=dest[:, c, t:t + 1], axis=0)
                                                ).then_inc(gathered[t % BUF], 16)

            @block.sync
            def _(sp):
                sp.dma_start(mod[:, :], mod_dram[0:1, 5 * D:6 * D].partition_broadcast(P)).then_inc(mod_loaded, 16)

                def load(t):
                    if t >= BUF:
                        sp.wait_ge(stored[t % BUF], 16 * (t // BUF))
                    sp.dma_start(x1[:, t % BUF, :], x1_dram[ds(t * P, P), :]).then_inc(x_loaded[t % BUF], 16)

                load(0)
                load(1)
                for t in range(TILES):
                    if t + 2 < TILES:
                        load(t + 2)
                    sp.wait_ge(summed, t + 1)
                    sp.dma_start(out[0, ds(t * P, P), :], x1[:, t % BUF, :]).then_inc(stored[t % BUF], 16)
                for i in range(BUF):
                    sp.wait_ge(stored[i], 16 * len(range(i, TILES, BUF)))

            @block.scalar
            def _(act):
                act.wait_ge(eps_ready, 1)
                for t in range(TILES):
                    act.wait_ge(mixed, t + 1)
                    if t >= 2:
                        act.wait_ge(recips, t - 1)
                    nc.scalar.activation(sq[:, :], y[:, t % BUF, :], ACT.Square, accum_out=ms[:, t % 2:t % 2 + 1]).then_inc(squared, 1)
                    act.wait_ge(squared, t + 1)
                    nc.scalar.activation(root[:, t % 2:t % 2 + 1], ms[:, t % 2:t % 2 + 1], ACT.Sqrt, scale=1.0 / D,
                                         bias=eps[:, 0:1]).then_inc(rooted, 1)

            @block.vector
            def _(dve):
                def mix(t):
                    dve.wait_ge(gathered[t % BUF], 32 * (t // BUF + 1))
                    dve.tensor_scalar(y[:, t % BUF, :], yy[:, t % BUF, 0, :], share[:, 0, t:t + 1], None, ALU.mult).then_inc(first, 1)
                    dve.wait_ge(first, t + 1)
                    dve.scalar_tensor_tensor(out=y[:, t % BUF, :], in0=yy[:, t % BUF, 1, :], scalar=share[:, 1, t:t + 1],
                                             in1=y[:, t % BUF, :], op0=ALU.mult, op1=ALU.add).then_inc(mixed, 1)

                dve.wait_ge(mod_loaded, 16)
                mix(0)
                for t in range(TILES):
                    if t + 1 < TILES:
                        mix(t + 1)
                    dve.wait_ge(rooted, t + 1)
                    dve.reciprocal(rstd[:, t % 2:t % 2 + 1], root[:, t % 2:t % 2 + 1]).then_inc(recips, 1)
                    dve.wait_ge(recips, t + 1)
                    dve.scalar_tensor_tensor(out=y[:, t % BUF, :], in0=y[:, t % BUF, :], scalar=rstd[:, t % 2:t % 2 + 1],
                                             in1=mod[:, :], op0=ALU.mult, op1=ALU.mult).then_inc(scaled, 1)
                    dve.wait_ge(scaled, t + 1)
                    dve.wait_ge(x_loaded[t % BUF], 16 * (t // BUF + 1))
                    dve.tensor_tensor(x1[:, t % BUF, :], y[:, t % BUF, :], x1[:, t % BUF, :], ALU.add).then_inc(summed, 1)


def build(nc, x, c, w_ada, b_ada, g_pre_mix, g_post_mix, g_pre_ffn, g_post_ffn, w_in, w_pool_group, pool_scale,
          w_branch_pool, w_branch_att, w_out, w_group_router, b_group_router, w_expert_router, b_expert_router,
          w_exp_gate, w_exp_up, w_exp_down, out):
    def dram(name, shape, dt=F32):
        return nc.dram_tensor(name, shape, dt).ap()

    mod_dram = dram("mod_rows", (1, 6 * D))
    proj = dram("projected", (IN_TILES * P, SEQ))
    att = dram("attended", (len(DILATIONS), SEQ, HPG * ROW))
    merged = dram("merged", (D, SEQ))
    x1_dram = dram("x_mixed", (SEQ, D))
    h_dram = dram("h_moe", (SEQ, D))
    slot_token = dram("slot_token", (NB * P, 1), I32)
    y_dram = dram("y_slots", (NB * P, D))
    with ExitStack() as ctx:
        def top(name, shape, dt=F32):
            return ctx.enter_context(nc.sbuf_tensor(name, shape, dt))

        ident = top("ident", [P, P])
        constants(nc, ident)
        condition(nc, c, w_ada, b_ada, (g_pre_mix, g_post_mix, g_pre_ffn, g_post_ffn), mod_dram)
        with ExitStack() as mixer:
            h_hi = mixer.enter_context(nc.sbuf_tensor("h_hi", [P, KD, SEQ], F32R))
            h_lo = mixer.enter_context(nc.sbuf_tensor("h_lo", [P, KD, SEQ], F32R))
            normalise(nc, x, mod_dram, ident, h_hi, h_lo)
            project(nc, w_in, h_hi, h_lo, proj)
        attend(nc, proj, ident, att)
        merge(nc, proj, att, ident, w_pool_group, pool_scale, w_branch_pool, w_branch_att, merged)
        dest, share = top("dest", [P, 2, TILES], I32), top("share", [P, 2, TILES])
        table, slot_rows = top("table", [1, 5, NB + 1], I32), top("slot_rows", [P, NB + 2], I32)
        with nc.sbuf_tensor("logits", [P, TILES, NR], F32) as logits:
            mix_out(nc, x, merged, w_out, mod_dram, ident, w_group_router, w_expert_router, b_group_router,
                    b_expert_router, x1_dram, h_dram, logits)
            route(nc, logits, slot_token, dest, share, table, slot_rows)
        experts(nc, table, slot_rows, ident, h_dram, w_exp_gate, w_exp_up, w_exp_down, y_dram)
        combine(nc, dest, share, y_dram, x1_dram, mod_dram, out)


_INS = ["x", "c", "w_ada", "b_ada", "g_pre_mix", "g_post_mix", "g_pre_ffn", "g_post_ffn", "w_in", "w_pool_group",
        "pool_scale", "w_branch_pool", "w_branch_att", "w_out", "w_group_router", "b_group_router", "w_expert_router",
        "b_expert_router", "w_exp_gate", "w_exp_up", "w_exp_down"]


def kernel(**inputs):
    import numpy as np
    import concourse.bacc as bacc
    from concourse.bass_utils import run_bass_kernel_spmd

    nc = bacc.Bacc("TRN2", target_bir_lowering=False, num_devices=1)
    arrays, args = {}, {}
    for name in _INS:
        a = np.ascontiguousarray(inputs[name])
        arrays[f"in_{name}"] = a
        args[name] = nc.dram_tensor(f"in_{name}", a.shape, mybir.dt.from_np(a.dtype), kind="ExternalInput").ap()
    args["out"] = nc.dram_tensor("out_0", (1, SEQ, D), F32, kind="ExternalOutput").ap()
    build(nc, **args)
    r = run_bass_kernel_spmd(nc, [arrays], core_ids=[0])
    return r.results[0]["out_0"]
```

```python
from contextlib import ExitStack

import concourse.bass as bass
from concourse import mybir

P = 128
D = 1024
SEQ = 2048
KD = D // P
TILES = SEQ // P
TG = SEQ // 512
POOL_WINDOWS = (2, 4, 8, 16)
POOL_TILES = len(POOL_WINDOWS)
HEADS = 12
HPG = 4
DILATIONS = (1, 4, 16)
PAIRS_OF_GROUP = HPG // 2
IN_TILES = (4 * P + 3 * HEADS * 64 + 2 * D) // P
Q_TILE, K_TILE, V_TILE, GATE_TILE = 4, 10, 16, 22
EG, EPG = 4, 8
NE = EG * EPG
DE = 512
KE = DE // P
NB = 64
EPS = 1e-6

F32 = mybir.dt.float32
F32R = mybir.dt.float32r
I32 = mybir.dt.int32
ALU = mybir.AluOpType
ACT = mybir.ActivationFunctionType
AX = mybir.AxisListType
ds = bass.ds


class Chain:

    def __init__(self, eng, sem):
        self.eng, self.sem, self.at, self.n = eng, sem, 0, 0

    def link(self, ins):
        self.n += 1
        ins.then_inc(self.sem, 1)
        self.eng.wait_ge(self.sem, self.at + self.n)

    def turn(self, at):
        self.at, self.n = at, 0


class Scope:

    def __init__(self, nc, ctx, name):
        self.nc, self.ctx, self.name, self.sems = nc, ctx, name, []
        ctx.callback(self.clear)

    def sb(self, name, shape, dt=F32):
        return self.ctx.enter_context(self.nc.sbuf_tensor(f"{self.name}_{name}", shape, dt))

    def ps(self, name, shape, dt=F32):
        return self.ctx.enter_context(self.nc.psum_tensor(f"{self.name}_{name}", shape, dt))

    def sem(self, name):
        self.sems.append(self.nc.alloc_semaphore(f"{self.name}_{name}"))
        return self.sems[-1]

    def clear(self):
        self.nc.clear_and_free_semaphores(self.sems)
        self.nc.all_engine_barrier()


def condition(nc, c, w_ada, b_ada, gains, mod_dram):
    with ExitStack() as ctx:
        s = Scope(nc, ctx, "cond")
        RING, COLS = 4, 2048
        PARTS = 6 * D // COLS
        mod = s.sb("mod", [P, 6, D])
        ccol = s.sb("ccol", [P, KD])
        cexp = s.sb("cexp", [P, KD])
        cact = s.sb("cact", [P, KD])
        ring = s.sb("ring", [P, RING, COLS])
        acc = s.sb("acc", [P, 6 * D])
        ones = s.sb("ones", [P, P])
        gain = s.sb("gain", [P, 4, D])
        psum = s.ps("psum", [P, 2, 512])
        c_loaded, b_loaded, gain_loaded = s.sem("c_loaded"), s.sem("b_loaded"), s.sem("gain_loaded")
        chunk_loaded = [s.sem(f"chunk_loaded{r}") for r in range(RING)]
        chunk_used, act_ready, acc_zero = s.sem("chunk_used"), s.sem("act_ready"), s.sem("acc_zero")
        ones_ready, part_summed, sum_taken, mod_done, mod_stored = (
            s.sem("ones_ready"), s.sem("part_summed"), s.sem("sum_taken"), s.sem("mod_done"), s.sem("mod_stored"))
        steps = s.sem("steps")
        w = w_ada[0].rearrange("(p k) n -> p k n", k=KD)
        with nc.Block() as block:
            @block.sync
            def _(sp):
                sp.dma_start(ccol[:, :], c.rearrange("b (p k) -> (b p) k", k=KD)).then_inc(c_loaded, 16)
                for n in range(PARTS * KD):
                    part, k = divmod(n, KD)
                    if n >= RING:
                        sp.wait_ge(chunk_used, n - RING + 1)
                    sp.dma_start(ring[:, n % RING, :], w[:, k, ds(part * COLS, COLS)]).then_inc(chunk_loaded[n % RING], 16)
                sp.wait_ge(mod_done, 6)
                sp.dma_start(mod_dram, mod[0:1, :, :].rearrange("a m d -> a (m d)")).then_inc(mod_stored, 16)
                sp.wait_ge(mod_stored, 16)

            @block.scalar
            def _(act):
                act.wait_ge(acc_zero, 1)
                act.dma_start(acc[0:1, :], b_ada).then_inc(b_loaded, 16)
                for n, g in enumerate(gains):
                    act.dma_start(gain[:, n, :], g[0:1, :].partition_broadcast(P)).then_inc(gain_loaded, 16)
                act.wait_ge(c_loaded, 16)
                nc.scalar.activation(cexp[:, :], ccol[:, :], ACT.Exp, scale=-1.0).then_inc(act_ready, 1)

            @block.tensor
            def _(pe):
                pe.wait_ge(ones_ready, 1)
                for n in range(12):
                    if n % 4 == 0:
                        pe.wait_ge(chunk_used, (n // 4 + 1) * KD)
                    if n >= 2:
                        pe.wait_ge(sum_taken, n - 1)
                    pe.matmul(psum[:, n % 2, :], ones[:, :], acc[:, ds(n * 512, 512)], start=True, stop=True).then_inc(part_summed, 1)

            @block.gpsimd
            def _(pool):
                pool.memset(ones[:, :], 1.0).then_inc(ones_ready, 1)

            @block.vector
            def _(dve):
                chain = Chain(dve, steps)
                dve.memset(acc[:, :], 0.0).then_inc(acc_zero, 1)
                dve.wait_ge(act_ready, 1)
                chain.link(dve.tensor_scalar(cexp[:, :], cexp[:, :], 1.0, None, ALU.add))
                chain.link(dve.reciprocal(cexp[:, :], cexp[:, :]))
                chain.link(dve.tensor_tensor(cact[:, :], cexp[:, :], ccol[:, :], ALU.mult))
                dve.wait_ge(b_loaded, 16)
                mod_flat = mod[:, :, :].rearrange("p m d -> p (m d)")

                def take(n):
                    dve.wait_ge(part_summed, n + 1)
                    dve.tensor_copy(mod_flat[:, ds(n * 512, 512)], psum[:, n % 2, :]).then_inc(sum_taken, 1)

                for n in range(PARTS * KD):
                    part, k = divmod(n, KD)
                    dve.wait_ge(chunk_loaded[n % RING], 16 * (n // RING + 1))
                    if n:
                        dve.wait_ge(chunk_used, n)
                    sums = acc[:, ds(part * COLS, COLS)]
                    dve.scalar_tensor_tensor(out=sums, in0=ring[:, n % RING, :], scalar=cact[:, k:k + 1], in1=sums,
                                             op0=ALU.mult, op1=ALU.add).then_inc(chunk_used, 1)
                    if part and k == 1:
                        for m in range(4):
                            take((part - 1) * 4 + m)
                for m in range(4):
                    take((PARTS - 1) * 4 + m)
                dve.wait_ge(sum_taken, 12)
                dve.wait_ge(gain_loaded, 64)
                for half in range(2):
                    row = mod[:, 3 * half + 1, :]
                    dve.scalar_tensor_tensor(out=row, in0=row, scalar=1.0, in1=gain[:, 2 * half, :],
                                             op0=ALU.add, op1=ALU.mult).then_inc(mod_done, 2)
                    row = mod[:, 3 * half + 2, :]
                    dve.tensor_tensor(row, row, gain[:, 2 * half + 1, :], ALU.mult).then_inc(mod_done, 1)


def normalise(nc, x, mod_dram, ident, h_hi, h_lo):
    with ExitStack() as ctx:
        s = Scope(nc, ctx, "norm")
        mod = s.sb("mod", [P, 2, D])
        eps = s.sb("eps", [P, 1])
        root = s.sb("root", [P, 2])
        mod_loaded, eps_ready, root_ready = s.sem("mod_loaded"), s.sem("eps_ready"), s.sem("root_ready")
        xt = s.sb("xt", [P, 2, D])
        sq = s.sb("sq", [P, 2, D])
        h = s.sb("h", [P, 2, D])
        ms = s.sb("ms", [P, 2])
        rstd = s.sb("rstd", [P, 2])
        psum = s.ps("psum", [P, 2, D])
        loaded = [s.sem(f"loaded{i}") for i in range(2)]
        summed, rstd_ready, scaled, h_ready, turned, hi_ready, lo_ready, steps = (s.sem(n) for n in (
            "summed", "rstd_ready", "scaled", "h_ready", "turned", "hi_ready", "lo_ready", "steps"))
        hT_hi = h_hi[:, :, :].rearrange("p k (t c) -> p k t c", c=P)
        hT_lo = h_lo[:, :, :].rearrange("p k (t c) -> p k t c", c=P)
        with nc.Block() as block:
            @block.sync
            def _(sp):
                sp.dma_start(mod[:, :, :].rearrange("p m d -> p (m d)"),
                             mod_dram[0:1, 0:2 * D].partition_broadcast(P)).then_inc(mod_loaded, 16)
                for t in range(TILES):
                    if t >= 2:
                        sp.wait_ge(scaled, t - 1)
                    sp.dma_start(xt[:, t % 2, :], x[0, ds(t * P, P), :]).then_inc(loaded[t % 2], 16)

            @block.scalar
            def _(act):
                def split(t):
                    act.wait_ge(turned, t + 1)
                    nc.scalar.activation(hT_hi[:, :, t, :], psum[:, t % 2, :].rearrange("p (k c) -> p k c", c=P),
                                         ACT.Copy).then_inc(hi_ready, 1)

                act.wait_ge(eps_ready, 1)
                for t in range(TILES):
                    act.wait_ge(loaded[t % 2], 16 * (t // 2 + 1))
                    if t >= 2:
                        act.wait_ge(scaled, t - 1)
                    nc.scalar.activation(sq[:, t % 2, :], xt[:, t % 2, :], ACT.Square,
                                         accum_out=ms[:, t % 2:t % 2 + 1]).then_inc(summed, 1)
                    act.wait_ge(summed, t + 1)
                    nc.scalar.activation(root[:, t % 2:t % 2 + 1], ms[:, t % 2:t % 2 + 1], ACT.Sqrt, scale=1.0 / D,
                                         bias=eps[:, 0:1]).then_inc(root_ready, 1)
                    if t >= 1:
                        split(t - 1)
                split(TILES - 1)

            @block.gpsimd
            def _(pool):
                pool.memset(eps[:, :], EPS).then_inc(eps_ready, 1)
                pool.wait_ge(mod_loaded, 16)
                for t in range(TILES):
                    pool.wait_ge(scaled, t + 1)
                    pool.tensor_tensor(h[:, t % 2, :], h[:, t % 2, :], mod[:, 0, :], ALU.add).then_inc(h_ready, 1)

            @block.tensor
            def _(pe):
                for t in range(TILES):
                    pe.wait_ge(h_ready, t + 1)
                    if t >= 2:
                        pe.wait_ge(lo_ready, t - 1)
                    for k in range(KD):
                        mm = pe.transpose(psum[:, t % 2, ds(k * P, P)], h[:, t % 2, ds(k * P, P)], ident[:, :])
                    mm.then_inc(turned, 1)

            @block.vector
            def _(dve):
                dve.wait_ge(mod_loaded, 16)

                def low(t):
                    dve.wait_ge(hi_ready, t + 1)
                    dve.tensor_tensor(hT_lo[:, :, t, :], psum[:, t % 2, :].rearrange("p (k c) -> p k c", c=P),
                                      hT_hi[:, :, t, :], ALU.subtract).then_inc(lo_ready, 1)

                for t in range(TILES):
                    dve.wait_ge(root_ready, t + 1)
                    dve.reciprocal(rstd[:, t % 2:t % 2 + 1], root[:, t % 2:t % 2 + 1]).then_inc(rstd_ready, 1)
                    dve.wait_ge(rstd_ready, t + 1)
                    if t >= 2:
                        dve.wait_ge(turned, t - 1)
                    dve.scalar_tensor_tensor(out=h[:, t % 2, :], in0=xt[:, t % 2, :], scalar=rstd[:, t % 2:t % 2 + 1],
                                             in1=mod[:, 1, :], op0=ALU.mult, op1=ALU.mult).then_inc(scaled, 1)
                    if t >= 1:
                        low(t - 1)
                low(TILES - 1)


def project(nc, w_in, h_hi, h_lo, proj):
    with ExitStack() as ctx:
        s = Scope(nc, ctx, "proj")
        raw = s.sb("raw", [P, 2, KD, P])
        w_hi = s.sb("w_hi", [P, 2, KD, P], F32R)
        w_lo = s.sb("w_lo", [P, 2, KD, P], F32R)
        out = s.sb("out", [P, 2, SEQ])
        sums = s.sb("sums", [P, 2, SEQ])
        inv = s.sb("inv", [P, 16])
        psum = s.ps("psum", [P, 2, TG, 512])
        loaded = [s.sem(f"loaded{i}") for i in range(2)]
        hi_ready = [s.sem(f"hi_ready{i}") for i in range(2)]
        lo_ready = [s.sem(f"lo_ready{i}") for i in range(2)]
        summed = [s.sem(f"summed{i}") for i in range(2)]
        taken = [s.sem(f"taken{i}") for i in range(2)]
        tile_done = [s.sem(f"tile_done{i}") for i in range(2)]
        stored = [s.sem(f"stored{i}") for i in range(2)]
        steps = s.sem("steps")
        PAIRS = IN_TILES // 2
        with nc.Block() as block:
            @block.sync
            def _(sp):
                def load(j, u):
                    sp.dma_start(raw[:, u, :, :], w_in[0, :, ds((2 * j + u) * P, P)].rearrange("(k p) f -> p k f", p=P)
                                 ).then_inc(loaded[u], 16)

                def store(j, u):
                    sp.wait_ge(tile_done[u], j + 1)
                    sp.dma_start(proj[ds((2 * j + u) * P, P), :], out[:, u, :]).then_inc(stored[u], 16)

                for u in range(2):
                    load(0, u)
                with sp.Fori(1, PAIRS) as j:
                    for u in range(2):
                        sp.wait_ge(lo_ready[u], j)
                        load(j, u)
                    for u in range(2):
                        store(j - 1, u)
                for u in range(2):
                    store(PAIRS - 1, u)
                for u in range(2):
                    sp.wait_ge(stored[u], 16 * PAIRS)

            @block.scalar
            def _(act):
                with act.Fori(0, PAIRS) as j:
                    for u in range(2):
                        act.wait_ge(loaded[u], 16 * j + 16)
                        act.wait_ge(summed[u], TG * j + TG)
                        nc.scalar.activation(w_hi[:, u, :, :], raw[:, u, :, :], ACT.Copy).then_inc(hi_ready[u], 1)

            @block.gpsimd
            def _(pool):
                with pool.Fori(0, PAIRS) as j:
                    for u in range(2):
                        pool.wait_ge(hi_ready[u], j + 1)
                        pool.tensor_tensor(w_lo[:, u, :, :], raw[:, u, :, :], w_hi[:, u, :, :], ALU.subtract
                                           ).then_inc(lo_ready[u], 1)

            @block.tensor
            def _(pe):
                for u in range(2):
                    pe.sem_inc(summed[u], TG)
                with pe.Fori(0, PAIRS) as j:
                    for u in range(2):
                        pe.wait_ge(lo_ready[u], j + 1)
                        for tg in range(TG):
                            pe.wait_ge(taken[u], TG * j + tg + 1)
                            for k in range(KD):
                                tok = ds(tg * 512, 512)
                                bank = psum[:, u, tg, :]
                                pe.matmul(bank, w_hi[:, u, k, :], h_hi[:, k, tok], start=(k == 0), stop=False)
                                pe.matmul(bank, w_hi[:, u, k, :], h_lo[:, k, tok], start=False, stop=False)
                                mm = pe.matmul(bank, w_lo[:, u, k, :], h_hi[:, k, tok], start=False, stop=(k == KD - 1))
                            mm.then_inc(summed[u], 1)

            @block.vector
            def _(dve):
                chain = Chain(dve, steps)
                for u in range(2):
                    dve.sem_inc(taken[u], TG)
                for t in range(15):
                    last = dve.memset(inv[:, t:t + 1], 1.0 / (t + 1))
                chain.link(last)

                def take(j, u, dilation):
                    view = out[:, u, :].rearrange("p (r m) -> p m r", r=dilation)
                    per = 512 // dilation
                    for tg in range(TG):
                        dve.wait_ge(summed[u], TG * j + TG + tg + 1)
                        ins = dve.tensor_copy(view[:, ds(tg * per, per), :],
                                              psum[:, u, tg, :].rearrange("p (m r) -> p m r", r=dilation))
                        ins.then_inc(taken[u], 1)

                for j in range(POOL_TILES // 2):
                    for u in range(2):
                        window = POOL_WINDOWS[2 * j + u]
                        if j:
                            dve.wait_ge(stored[u], 16 * j)
                        take(j, u, 1)
                        dve.wait_ge(taken[u], TG * (j + 2))
                        chan = out[:, u, :]
                        reach, now = 1, chan
                        while reach < window:
                            new = sums[:, reach.bit_length() % 2, :]
                            dve.tensor_copy(new[:, :reach], now[:, :reach])
                            chain.link(dve.tensor_tensor(new[:, reach:], now[:, reach:], now[:, :SEQ - reach], ALU.add))
                            reach, now = 2 * reach, new
                        head = window - 1
                        chain.link(dve.tensor_tensor(now[:, :head], now[:, :head], inv[:, :head], ALU.mult))
                        chain.link(dve.tensor_tensor(chan[:, :head], now[:, :head], chan[:, :head], ALU.subtract))
                        chain.link(dve.scalar_tensor_tensor(out=chan[:, head:], in0=now[:, head:], scalar=1.0 / window,
                                                            in1=chan[:, head:], op0=ALU.mult, op1=ALU.subtract))
                        dve.sem_inc(tile_done[u], 1)
                first = POOL_TILES // 2
                groups = len(DILATIONS)
                with dve.Fori(0, 3) as part:
                    for g, dilation in enumerate(DILATIONS):
                        j = part * groups + (first + g)
                        for u in range(2):
                            dve.wait_ge(stored[u], 16 * j)
                            take(j, u, dilation)
                            dve.wait_ge(taken[u], TG * j + 2 * TG)
                            dve.sem_inc(tile_done[u], 1)
                with dve.Fori(first + 3 * groups, PAIRS) as j:
                    for u in range(2):
                        dve.wait_ge(stored[u], 16 * j)
                        take(j, u, 1)
                        dve.wait_ge(taken[u], TG * j + 2 * TG)
                        dve.sem_inc(tile_done[u], 1)


def constants(nc, ident):
    with ExitStack() as ctx:
        s = Scope(nc, ctx, "const")
        zeroed, ready = s.sem("zeroed"), s.sem("ready")
        with nc.Block() as block:
            @block.gpsimd
            def _(pool):
                pool.memset(ident[:, :], 0.0).then_inc(zeroed, 1)
                pool.wait_ge(zeroed, 1)
                pool.affine_select(out=ident[:, :], in_=ident[:, :], compare_op=ALU.not_equal, fill=1.0,
                                   base=0, pattern=[[-1, P]], channel_multiplier=1).then_inc(ready, 1)
                pool.wait_ge(ready, 1)


ROW = 66
MASKED = 1e38


def attend(nc, proj, ident, att):
    units = []
    for g, dilation in enumerate(DILATIONS):
        blocks_of_residue = TILES // dilation
        width = P if blocks_of_residue == 1 else 2 * P
        step = 512 // width
        for pair in range(PAIRS_OF_GROUP):
            for b in range(0, TILES, step):
                units.append((g, pair, b, step, width))
    N = len(units)
    pair_of = [PAIRS_OF_GROUP * g + pair for g, pair, *_ in units]
    first_of = [n == 0 or pair_of[n] != pair_of[n - 1] for n in range(N)]
    last_of = [max(n for n in range(N) if pair_of[n] == q) for q in range(6)]
    turn_of = [n + 2 * (pair_of[n] + 1) for n in range(N)]
    VP = nc_bufs = 2
    with ExitStack() as ctx:
        s = Scope(nc, ctx, "att")
        qkv = s.sb("qkv", [P, 2, 3, SEQ])
        v = s.sb("v", [P, 2, TILES, P])
        dist = s.sb("dist", [P, 3 * 2 * P])
        dist_own = s.sb("dist_own", [P, 4 * P])
        bias = s.sb("bias", [P, 2, 2, 3 * 2 * P])
        score = s.sb("score", [P, 2, 2, 512])
        prob = s.sb("prob", [P, 2, 2, 512])
        probT = s.sb("probT", [P, 2, 2, 512])
        neg = s.sb("neg", [P, 2, 2, 4])
        res = s.sb("res", [P, 4, 4, 2, ROW])
        p_score = s.ps("p_score", [P, 2, 2, 512])
        p_turn = s.ps("p_turn", [P, 2, 512])
        p_out = s.ps("p_out", [P, 2, 512])
        loaded = [s.sem(f"loaded{i}") for i in range(2)]
        stored = [s.sem(f"stored{i}") for i in range(4)]
        names = ("dist_ready", "biased", "bias_ready", "scored", "maxed", "negated", "exped", "turned0", "turned1",
                 "copied0", "copied1", "weighed", "res_ready", "made")
        (dist_ready, biased, bias_ready, scored, maxed, negated, exped, turned0, turned1, copied0, copied1,
         weighed, res_ready, made) = (s.sem(n) for n in names)
        turned, copied = (turned0, turned1), (copied0, copied1)

        def probs_dst(n, a):
            return probT[:, n % 2, a, :]

        def copy_turn(eng, copy, turn, a, dst):
            eng.wait_ge(turned[a], turn + 1)
            copy(dst, p_turn[:, a, :]).then_inc(copied[a], 1)

        def v_dst(q, half, a):
            return v[:, q % 2, ds(8 * half + 4 * a, 4), :].rearrange("p b f -> p (b f)")

        def copies(eng, copy, n, a):
            q = pair_of[n]
            if first_of[n]:
                if q >= 2:
                    eng.wait_ge(weighed, last_of[q - 2] + 1)
                for half in range(2):
                    copy_turn(eng, copy, turn_of[n] - 2 + half, a, v_dst(q, half, a))
            if n >= 2:
                eng.wait_ge(weighed, n - 1)
            copy_turn(eng, copy, turn_of[n], a, probs_dst(n, a))

        with nc.Block() as block:
            @block.sync
            def _(sp):
                def load(q):
                    g, pair = divmod(q, PAIRS_OF_GROUP)
                    if q >= 2:
                        sp.wait_ge(scored, last_of[q - 2] + 1)
                        sp.wait_ge(turned1, turn_of[last_of[q - 2]] + 1)
                    for part, tile0 in enumerate((Q_TILE, K_TILE, V_TILE)):
                        sp.dma_start(qkv[:, q % 2, part, :], proj[ds((tile0 + 2 * g + pair) * P, P), :]).then_inc(loaded[q % 2], 16)

                load(0)
                load(1)
                for n, (g, pair, b, step, width) in enumerate(units):
                    if first_of[n] and 2 <= pair_of[n] + 1 < 6:
                        load(pair_of[n] + 1)
                    dilation = DILATIONS[g]
                    rows = att[g].rearrange("(n i r) f -> r n i f", r=dilation, i=P)
                    per = TILES // dilation
                    if width == P:
                        dst = rows[b:b + step, 0, :, ds(2 * pair * ROW, 2 * ROW)].rearrange("r i f -> i r f")
                    else:
                        dst = rows[b // per, b % per:b % per + step, :, ds(2 * pair * ROW, 2 * ROW)].rearrange("n i f -> i n f")
                    sp.wait_ge(res_ready, n + 1)
                    sp.dma_start(dst, res[:, n % 4, 0:step, :, :].rearrange("p b a f -> p b (a f)")).then_inc(stored[n % 4], 16)
                for i in range(4):
                    sp.wait_ge(stored[i], 16 * len(range(i, N, 4)))

            @block.gpsimd
            def _(pool):
                chain = Chain(pool, made)
                own = dist[:, 256:512]
                chain.link(pool.iota(own, pattern=[[-1, 256]], base=P, channel_multiplier=1,
                                     allow_small_or_imprecise_dtypes=True))
                chain.link(pool.affine_select(out=own, in_=own, compare_op=ALU.is_ge, fill=MASKED, base=P,
                                              pattern=[[-1, 256]], channel_multiplier=1))
                chain.link(pool.affine_select(out=own, in_=own, compare_op=ALU.is_ge, fill=MASKED, base=0,
                                              pattern=[[1, 256]], channel_multiplier=-1))
                pool.memset(dist[:, 0:P], MASKED)
                pool.tensor_copy(dist[:, P:2 * P], own[:, P:2 * P])
                pool.tensor_copy(dist[:, 512:768], own)
                for m in range(4):
                    last = pool.tensor_copy(dist_own[:, ds(m * P, P)], own[:, P:2 * P])
                chain.link(last)
                for q in range(6):
                    g, pair = divmod(q, PAIRS_OF_GROUP)
                    if q >= 2:
                        pool.wait_ge(biased, 2 * (last_of[q - 2] + 1))
                    for a in range(2):
                        head = HPG * g + 2 * pair + a
                        slope = 2.0 ** (-8.0 * (head + 1) / HEADS) * DILATIONS[g]
                        src = dist_own if DILATIONS[g] == TILES else dist
                        w = src.shape[1]
                        pool.tensor_scalar(bias[:, q % 2, a, 0:w], src[:, :], -slope, None, ALU.mult).then_inc(bias_ready, 1)

            @block.tensor
            def _(pe):
                def scores(n):
                    g, pair, b, step, width = units[n]
                    q = pair_of[n]
                    pe.wait_ge(loaded[q % 2], 48 * (q // 2 + 1))
                    if n >= 2:
                        pe.wait_ge(biased, 2 * (n - 1))
                    for a in range(2):
                        part = ds(64 * a, 64)
                        for m in range(step):
                            blk = b + m
                            before = max(blk - 1, 0) if width == 2 * P else blk
                            if width == 2 * P and blk == 0:
                                for half in range(2):
                                    mm = pe.matmul(p_score[:, n % 2, a, ds(half * P, P)], qkv[part, q % 2, 0, 0:P],
                                                   qkv[part, q % 2, 1, 0:P], start=True, stop=True)
                                continue
                            mm = pe.matmul(p_score[:, n % 2, a, ds(m * width, width)],
                                           qkv[part, q % 2, 0, ds(blk * P, P)],
                                           qkv[part, q % 2, 1, ds(before * P, width)], start=True, stop=True)
                    mm.then_inc(scored, 1)

                def turns(n):
                    q = pair_of[n]

                    def turn(index, tile):
                        for a in range(2):
                            if index:
                                pe.wait_ge(copied[a], index)
                            for m in range(4):
                                tr = pe.transpose(p_turn[:, a, ds(m * P, P)], tile(a, m), ident[:, :])
                            tr.then_inc(turned[a], 1)

                    if first_of[n]:
                        for half in range(2):
                            turn(turn_of[n] - 2 + half, lambda a, m: qkv[:, q % 2, 2, ds((8 * half + 4 * a + m) * P, P)])
                    pe.wait_ge(exped, n + 1)
                    turn(turn_of[n], lambda a, m: prob[:, n % 2, a, ds(m * P, P)])

                def weigh(n):
                    g, pair, b, step, width = units[n]
                    q = pair_of[n]
                    for a in range(2):
                        pe.wait_ge(copied[a], turn_of[n] + 1)
                    if n >= 2:
                        pe.wait_ge(res_ready, n - 1)
                    halves = width // P
                    for a in range(2):
                        for m in range(step):
                            for half in range(halves):
                                blk = max(b + m + half + 1 - halves, 0)
                                mm = pe.matmul(p_out[:, n % 2, ds((m * 2 + a) * 64, 64)],
                                               probT[:, n % 2, a, ds((m * halves + half) * P, P)],
                                               v[:, q % 2, blk, ds(64 * a, 64)], start=(half == 0), stop=(half == halves - 1))
                    mm.then_inc(weighed, 1)

                scores(0)
                scores(1)
                for n in range(N):
                    turns(n)
                    if n + 2 < N:
                        scores(n + 2)
                    weigh(n)

            @block.scalar
            def _(act):
                def exps(n):
                    step, width = units[n][3:]
                    act.wait_ge(negated, n + 1)
                    if n >= 2:
                        act.wait_ge(turned[1], turn_of[n - 2] + 1)
                    for a in range(2):
                        for m in range(step):
                            ins = nc.scalar.activation(prob[:, n % 2, a, ds(m * width, width)],
                                                       score[:, n % 2, a, ds(m * width, width)], ACT.Exp,
                                                       bias=neg[:, n % 2, a, m:m + 1],
                                                       accum_out=res[:, n % 4, m, a, 65:66])
                    ins.then_inc(exped, 1)

                exps(0)
                for n in range(N):
                    if n + 1 < N:
                        exps(n + 1)
                    copies(act, lambda d, x: nc.scalar.activation(d, x, ACT.Copy), n, 0)

            @block.vector
            def _(dve):
                def soft(n):
                    g, pair, b, step, width = units[n]
                    q = pair_of[n]
                    dve.wait_ge(scored, n + 1)
                    dve.wait_ge(bias_ready, 2 * (q + 1))
                    if n >= 2:
                        dve.wait_ge(exped, n - 1)
                    if n >= 4:
                        dve.wait_ge(stored[n % 4], 16 * (n // 4))
                    first = width == P or b % (TILES // DILATIONS[g]) == 0
                    for a in range(2):
                        dve.scalar_tensor_tensor(out=score[:, n % 2, a, :], in0=p_score[:, n % 2, a, :], scalar=64 ** -0.5,
                                                 in1=bias[:, q % 2, a, ds(0 if first else 256, 512)],
                                                 op0=ALU.mult, op1=ALU.add).then_inc(biased, 1)
                    dve.wait_ge(biased, 2 * n + 2)
                    top = res[:, n % 4, 0:step, :, 64].rearrange("p b a -> p a b")
                    dve.tensor_reduce(top, score[:, n % 2, :, :].rearrange("p a (b w) -> p a b w", w=width), AX.X, ALU.max
                                      ).then_inc(maxed, 1)
                    dve.wait_ge(maxed, n + 1)
                    dve.tensor_scalar(neg[:, n % 2, :, 0:step], top, -1.0, None, ALU.mult).then_inc(negated, 1)

                def take(n):
                    step = units[n][3]
                    dve.wait_ge(weighed, n + 1)
                    dve.tensor_copy(res[:, n % 4, 0:step, :, 0:64],
                                    p_out[:, n % 2, 0:step * P].rearrange("p (b a f) -> p b a f", a=2, f=64)
                                    ).then_inc(res_ready, 1)

                soft(0)
                for n in range(N):
                    if n + 1 < N:
                        soft(n + 1)
                    if n >= 1:
                        take(n - 1)
                    copies(dve, dve.tensor_copy, n, 1)
                take(N - 1)


def merge(nc, proj, att, ident, w_pool_group, pool_scale, w_branch_pool, w_branch_att, merged):
    HALF = SEQ // 2
    KP, KA = POOL_TILES, 2
    with ExitStack() as ctx:
        s = Scope(nc, ctx, "merge")
        z_hi, z_lo = s.sb("z_hi", [P, KP, SEQ], F32R), s.sb("z_lo", [P, KP, SEQ], F32R)
        o_hi, o_lo = s.sb("o_hi", [P, KA, SEQ], F32R), s.sb("o_lo", [P, KA, SEQ], F32R)
        w_hi, w_lo = s.sb("w_hi", [P, KP + KA, D], F32R), s.sb("w_lo", [P, KP + KA, D], F32R)
        w_raw = s.sb("w_raw", [P, 2, D])
        pooled = s.sb("pooled", [P, 2, HALF])
        wg = s.sb("wg", [P, KP, P])
        scale = s.sb("scale", [P, KP])
        heads = s.sb("heads", [P, 2, 3, HPG, ROW])
        top = s.sb("top", [P, HPG])
        coef = s.sb("coef", [P, 3, HPG])
        part = s.sb("part", [P, 3, HPG])
        total = s.sb("total", [P, HPG])
        term = s.sb("term", [P, 3, HPG, 64])
        o = s.sb("o", [P, 2, KA * P])
        gate = s.sb("gate", [P, 2, 2, HALF])
        m = s.sb("m", [P, 2, HALF])
        psum = s.ps("psum", [P, 8, 512])
        w_loaded = [s.sem(f"w_loaded{i}") for i in range(2)]
        pooled_loaded = [s.sem(f"pooled_loaded{i}") for i in range(2)]
        heads_loaded = [s.sem(f"heads_loaded{i}") for i in range(2)]
        gate_loaded = [s.sem(f"gate_loaded{i}") for i in range(2)]
        m_stored = [s.sem(f"m_stored{i}") for i in range(2)]
        (small_loaded, w_hi_ready, w_lo_ready, z_summed, z_hi_ready, z_lo_ready, steps, shifted, coef_exp, o_ready,
         o_turned, o_hi_ready, o_lo_ready, gated, y_summed, gate_applied, m_ready) = (s.sem(n) for n in (
             "small_loaded", "w_hi_ready", "w_lo_ready", "z_summed", "z_hi_ready", "z_lo_ready", "steps", "shifted",
             "coef_exp", "o_ready", "o_turned", "o_hi_ready", "o_lo_ready", "gated", "y_summed", "gate_applied", "m_ready"))
        UNITS = KD * 2
        z_bank = lambda n: 2 * (n % 2)
        with nc.Block() as block:
            @block.sync
            def _(sp):
                sp.dma_start(wg[:, :, :], w_pool_group[0].rearrange("g c d -> c g d")).then_inc(small_loaded, 16)
                sp.dma_start(scale[:, :], pool_scale[0].rearrange("(g p) -> p g", p=P),
                             allow_slow_non_contiguous=True).then_inc(small_loaded, 16)
                for n in range(2 * KP):
                    g, half = divmod(n, 2)
                    if n >= 2:
                        sp.wait_ge(z_summed, n - 1)
                    sp.dma_start(pooled[:, n % 2, :], proj[ds(g * P, P), ds(half * HALF, HALF)]).then_inc(pooled_loaded[n % 2], 16)
                for t in range(TILES):
                    if t >= 2:
                        sp.wait_ge(o_ready, t - 1)
                    sp.dma_start(heads[:, t % 2, :, :, :].rearrange("p g h f -> p g (h f)"),
                                 att[:, ds(t * P, P), :].rearrange("g p f -> p g f")).then_inc(heads_loaded[t % 2], 16)
                    if t < KP + KA:
                        if t >= 2:
                            sp.wait_ge(w_lo_ready, t - 1)
                        rows = w_branch_pool[0, ds(t * P, P), :] if t < KP else w_branch_att[0, ds((t - KP) * P, P), :]
                        sp.dma_start(w_raw[:, t % 2, :], rows).then_inc(w_loaded[t % 2], 16)

                def load_gates(n):
                    d, half = divmod(n, 2)
                    if n >= 2:
                        sp.wait_ge(gate_applied, 4 * (n - 1))
                    for b in range(2):
                        sp.dma_start(gate[:, n % 2, b, :], proj[ds((GATE_TILE + b * KD + d) * P, P), ds(half * HALF, HALF)]
                                     ).then_inc(gate_loaded[n % 2], 16)

                load_gates(0)
                for n in range(UNITS):
                    if n + 1 < UNITS:
                        load_gates(n + 1)
                    d, half = divmod(n, 2)
                    sp.wait_ge(m_ready, 2 * (n + 1))
                    sp.dma_start(merged[ds(d * P, P), ds(half * HALF, HALF)], m[:, n % 2, :]).then_inc(m_stored[n % 2], 16)
                for i in range(2):
                    sp.wait_ge(m_stored[i], 16 * UNITS // 2)

            @block.scalar
            def _(act):
                for n in range(2 * KP):
                    g, half = divmod(n, 2)
                    act.wait_ge(z_summed, n + 1)
                    nc.scalar.activation(z_hi[:, g, ds(half * HALF, HALF)],
                                         psum[:, z_bank(n):z_bank(n) + 2, :].rearrange("p b c -> p (b c)"),
                                         ACT.Copy, scale=scale[:, g:g + 1]).then_inc(z_hi_ready, 1)
                for t in range(TILES):
                    if t < KP + KA:
                        act.wait_ge(w_loaded[t % 2], 16 * (t // 2 + 1))
                        nc.scalar.activation(w_hi[:, t, :], w_raw[:, t % 2, :], ACT.Copy).then_inc(w_hi_ready, 1)
                    act.wait_ge(shifted, t + 1)
                    nc.scalar.activation(coef[:, :, :], coef[:, :, :], ACT.Exp).then_inc(coef_exp, 1)
                    act.wait_ge(o_turned, t + 1)
                    nc.scalar.activation(o_hi[:, :, ds(t * P, P)],
                                         psum[:, 4 + t % 2, 0:KA * P].rearrange("p (k c) -> p k c", c=P),
                                         ACT.Copy).then_inc(o_hi_ready, 1)
                for n in range(UNITS):
                    act.wait_ge(gate_loaded[n % 2], 32 * (n // 2 + 1))
                    nc.scalar.activation(gate[:, n % 2, :, :], gate[:, n % 2, :, :], ACT.Sigmoid).then_inc(gated, 1)

            @block.gpsimd
            def _(pool):
                for t in range(KP + KA):
                    pool.wait_ge(w_hi_ready, t + 1)
                    pool.tensor_tensor(w_lo[:, t, :], w_raw[:, t % 2, :], w_hi[:, t, :], ALU.subtract).then_inc(w_lo_ready, 1)
                for n in range(UNITS):
                    for q in range(2):
                        pool.wait_ge(gate_applied, 4 * n + 2 * q + 2)
                        if n >= 2:
                            pool.wait_ge(m_stored[n % 2], 16 * (n // 2))
                        tok = ds(q * 512, 512)
                        pool.tensor_tensor(m[:, n % 2, tok], gate[:, n % 2, 0, tok], gate[:, n % 2, 1, tok], ALU.add
                                           ).then_inc(m_ready, 1)

            @block.tensor
            def _(pe):
                pe.wait_ge(small_loaded, 32)
                for n in range(2 * KP):
                    pe.wait_ge(pooled_loaded[n % 2], 16 * (n // 2 + 1))
                    if n >= 2:
                        pe.wait_ge(z_lo_ready, n - 1)
                    for q in range(2):
                        mm = pe.matmul(psum[:, z_bank(n) + q, :], wg[:, n // 2, :], pooled[:, n % 2, ds(q * 512, 512)],
                                       start=True, stop=True)
                    mm.then_inc(z_summed, 1)
                for t in range(TILES):
                    pe.wait_ge(o_ready, t + 1)
                    if t >= 2:
                        pe.wait_ge(o_lo_ready, t - 1)
                    for k in range(KA):
                        tr = pe.transpose(psum[:, 4 + t % 2, ds(k * P, P)], o[:, t % 2, ds(k * P, P)], ident[:, :])
                    tr.then_inc(o_turned, 1)
                pe.wait_ge(z_lo_ready, 2 * KP)
                pe.wait_ge(w_lo_ready, KP + KA)
                pe.wait_ge(o_lo_ready, TILES)
                for n in range(UNITS):
                    d, half = divmod(n, 2)
                    cols = ds(d * P, P)
                    for q in range(2):
                        turn = 2 * n + q
                        if turn >= 4:
                            pe.wait_ge(gate_applied, 2 * (turn - 3))
                        tok = ds(half * HALF + q * 512, 512)
                        for b, (k0, k1, in_hi, in_lo) in enumerate(((0, KP, z_hi, z_lo), (KP, KP + KA, o_hi, o_lo))):
                            bank = psum[:, 2 * (turn % 4) + b, :]
                            for k in range(k0, k1):
                                pe.matmul(bank, w_hi[:, k, cols], in_hi[:, k - k0, tok], start=(k == k0), stop=False)
                                pe.matmul(bank, w_hi[:, k, cols], in_lo[:, k - k0, tok], start=False, stop=False)
                                mm = pe.matmul(bank, w_lo[:, k, cols], in_hi[:, k - k0, tok], start=False, stop=(k == k1 - 1))
                            mm.then_inc(y_summed, 1)

            @block.vector
            def _(dve):
                chain = Chain(dve, steps)
                for n in range(2 * KP):
                    g, half = divmod(n, 2)
                    dve.wait_ge(z_hi_ready, n + 1)
                    tok = ds(half * HALF, HALF)
                    dve.scalar_tensor_tensor(out=z_lo[:, g, tok],
                                             in0=psum[:, z_bank(n):z_bank(n) + 2, :].rearrange("p b c -> p (b c)"),
                                             scalar=scale[:, g:g + 1], in1=z_hi[:, g, tok],
                                             op0=ALU.mult, op1=ALU.subtract).then_inc(z_lo_ready, 1)

                def low(t):
                    dve.wait_ge(o_hi_ready, t + 1)
                    dve.tensor_tensor(o_lo[:, :, ds(t * P, P)], psum[:, 4 + t % 2, 0:KA * P].rearrange("p (k c) -> p k c", c=P),
                                      o_hi[:, :, ds(t * P, P)], ALU.subtract).then_inc(o_lo_ready, 1)

                for t in range(TILES):
                    hd = heads[:, t % 2, :, :, :]
                    dve.wait_ge(heads_loaded[t % 2], 16 * (t // 2 + 1))
                    chain.link(dve.tensor_tensor(top[:, :], hd[:, 0, :, 64], hd[:, 1, :, 64], ALU.max))
                    chain.link(dve.tensor_tensor(top[:, :], top[:, :], hd[:, 2, :, 64], ALU.max))
                    dve.tensor_tensor(coef[:, :, :], hd[:, :, :, 64], top[:, :].unsqueeze(1).to_broadcast([P, 3, HPG]),
                                      ALU.subtract).then_inc(shifted, 1)
                    if t:
                        low(t - 1)
                    dve.wait_ge(coef_exp, t + 1)
                    chain.link(dve.tensor_tensor(part[:, :, :], coef[:, :, :], hd[:, :, :, 65], ALU.mult))
                    chain.link(dve.tensor_reduce(total[:, :], part[:, :, :].rearrange("p g h -> p h g"), AX.X, ALU.add))
                    chain.link(dve.reciprocal(total[:, :], total[:, :]))
                    chain.link(dve.tensor_tensor(coef[:, :, :], coef[:, :, :],
                                                 total[:, :].unsqueeze(1).to_broadcast([P, 3, HPG]), ALU.mult))
                    chain.link(dve.tensor_tensor(term[:, :, :, :], hd[:, :, :, 0:64],
                                                 coef[:, :, :].unsqueeze(3).to_broadcast([P, 3, HPG, 64]), ALU.mult))
                    if t >= 2:
                        dve.wait_ge(o_turned, t - 1)
                    flat = term[:, :, :, :].rearrange("p g h f -> p g (h f)")
                    chain.link(dve.tensor_tensor(o[:, t % 2, :], flat[:, 0, :], flat[:, 1, :], ALU.add))
                    dve.tensor_tensor(o[:, t % 2, :], o[:, t % 2, :], flat[:, 2, :], ALU.add).then_inc(o_ready, 1)
                low(TILES - 1)
                for n in range(UNITS):
                    dve.wait_ge(gated, n + 1)
                    for q in range(2):
                        turn = 2 * n + q
                        tok = ds(q * 512, 512)
                        for b in range(2):
                            dve.wait_ge(y_summed, 2 * turn + b + 1)
                            dve.tensor_tensor(gate[:, n % 2, b, tok], psum[:, 2 * (turn % 4) + b, :],
                                              gate[:, n % 2, b, tok], ALU.mult).then_inc(gate_applied, 1)


NR = EG + NE


def mix_out(nc, x, merged, w_out, mod_dram, ident, w_group_router, w_expert_router, b_group_router, b_expert_router,
            x1_dram, h_dram, logits):
    with ExitStack() as ctx:
        s = Scope(nc, ctx, "out")
        w_hi, w_lo = s.sb("w_hi", [P, KD, D], F32R), s.sb("w_lo", [P, KD, D], F32R)
        w_raw = s.sb("w_raw", [P, 2, D])
        mT = s.sb("mT", [P, 2, KD, P])
        m_hi, m_lo = s.sb("m_hi", [P, 2, KD, P], F32R), s.sb("m_lo", [P, 2, KD, P], F32R)
        mod = s.sb("mod", [P, 3, D])
        xt = s.sb("xt", [P, 2, D])
        sq = s.sb("sq", [P, D])
        x1 = s.sb("x1", [P, 3, D])
        h = s.sb("h", [P, 2, D])
        hT = s.sb("hT", [P, KD, P])
        wr = s.sb("wr", [P, KD, NR])
        rbias = s.sb("rbias", [P, NR])
        eps = s.sb("eps", [P, 1])
        ms, root, rstd = s.sb("ms", [P, 4]), s.sb("root", [P, 4]), s.sb("rstd", [P, 4])
        y = s.ps("y", [P, 2, D])
        turned_h = s.ps("turned_h", [P, D])
        p_logit = s.ps("p_logit", [P, 2, 512])
        w_loaded = [s.sem(f"w_loaded{i}") for i in range(2)]
        m_loaded = [s.sem(f"m_loaded{i}") for i in range(2)]
        x_loaded = [s.sem(f"x_loaded{i}") for i in range(2)]
        x1_stored = [s.sem(f"x1_stored{i}") for i in range(3)]
        h_stored = [s.sem(f"h_stored{i}") for i in range(2)]
        (small_loaded, eps_ready, w_hi_ready, w_lo_ready, m_hi_ready, m_lo_ready, y_half, y_squared, y_rooted, x_squared,
         x_rooted, recips, y_scaled, x1_ready, h_scaled, h_ready, h_turned, hT_ready, logit_summed, logit_taken) = (
             s.sem(n) for n in (
                 "small_loaded", "eps_ready", "w_hi_ready", "w_lo_ready", "m_hi_ready", "m_lo_ready", "y_half",
                 "y_squared", "y_rooted", "x_squared", "x_rooted", "recips", "y_scaled", "x1_ready", "h_scaled",
                 "h_ready", "h_turned", "hT_ready", "logit_summed", "logit_taken"))
        with nc.Block() as block:
            @block.sync
            def _(sp):
                for k in range(KD):
                    if k >= 2:
                        sp.wait_ge(w_lo_ready, k - 1)
                    sp.dma_start(w_raw[:, k % 2, :], w_out[0, ds(k * P, P), :]).then_inc(w_loaded[k % 2], 16)
                    if k == 1:
                        sp.dma_start(mod[:, :, :].rearrange("p m d -> p (m d)"),
                                     mod_dram[0:1, 2 * D:5 * D].partition_broadcast(P)).then_inc(small_loaded, 16)
                        sp.dma_start(wr[:, :, 0:EG], w_group_router[0].rearrange("(k p) e -> p k e", p=P)).then_inc(small_loaded, 16)
                        sp.dma_start(wr[:, :, EG:NR], w_expert_router[0].rearrange("(k p) e -> p k e", p=P)).then_inc(small_loaded, 16)
                        sp.dma_start(rbias[:, 0:EG], b_group_router[0:1, :].partition_broadcast(P)).then_inc(small_loaded, 16)
                        sp.dma_start(rbias[:, EG:NR], b_expert_router[0:1, :].partition_broadcast(P)).then_inc(small_loaded, 16)
                for t in range(TILES + 1):
                    if t < TILES:
                        if t >= 2:
                            sp.wait_ge(m_lo_ready, t - 1)
                        sp.dma_start(mT[:, t % 2, :, :], merged.rearrange("(k p) t -> p k t", p=P)[:, :, ds(t * P, P)]
                                     ).then_inc(m_loaded[t % 2], 16)
                        if t >= 2:
                            sp.wait_ge(x1_ready, t - 1)
                        sp.dma_start(xt[:, t % 2, :], x[0, ds(t * P, P), :]).then_inc(x_loaded[t % 2], 16)

            @block.scalar
            def _(act):
                act.wait_ge(eps_ready, 1)

                def split(t):
                    if t >= 2:
                        act.wait_ge(y_half, 2 * (t - 1))
                    act.wait_ge(m_loaded[t % 2], 16 * (t // 2 + 1))
                    nc.scalar.activation(m_hi[:, t % 2, :, :], mT[:, t % 2, :, :], ACT.Copy).then_inc(m_hi_ready, 1)

                def squares(src, wait, col, squared, rooted, count):
                    act.wait_ge(*wait)
                    if count >= 2:
                        act.wait_ge(recips, 2 * (count - 2) + 1)
                    nc.scalar.activation(sq[:, :], src, ACT.Square, accum_out=ms[:, col:col + 1]).then_inc(squared, 1)
                    act.wait_ge(squared, count)
                    nc.scalar.activation(root[:, col:col + 1], ms[:, col:col + 1], ACT.Sqrt, scale=1.0 / D,
                                         bias=eps[:, 0:1]).then_inc(rooted, 1)

                for k in range(KD):
                    act.wait_ge(w_loaded[k % 2], 16 * (k // 2 + 1))
                    nc.scalar.activation(w_hi[:, k, :], w_raw[:, k % 2, :], ACT.Copy).then_inc(w_hi_ready, 1)
                split(0)
                split(1)
                for t in range(TILES + 1):
                    if t < TILES:
                        squares(y[:, t % 2, :], (y_half, 2 * t + 2), t % 2, y_squared, y_rooted, t + 1)
                    if t >= 1:
                        if t >= 3:
                            act.wait_ge(h_scaled, t - 2)
                        squares(x1[:, (t - 1) % 3, :], (x1_ready, t), 2 + (t - 1) % 2, x_squared, x_rooted, t)
                    if t + 2 < TILES:
                        split(t + 2)

            @block.gpsimd
            def _(pool):
                pool.memset(eps[:, :], EPS).then_inc(eps_ready, 1)

                def low(t):
                    pool.wait_ge(m_hi_ready, t + 1)
                    pool.tensor_tensor(m_lo[:, t % 2, :, :], mT[:, t % 2, :, :], m_hi[:, t % 2, :, :], ALU.subtract
                                       ).then_inc(m_lo_ready, 1)

                def store_h(t):
                    pool.wait_ge(h_ready, t + 1)
                    pool.dma_start(h_dram[ds(t * P, P), :], h[:, t % 2, :]).then_inc(h_stored[t % 2], 16)

                for k in range(KD):
                    pool.wait_ge(w_hi_ready, k + 1)
                    pool.tensor_tensor(w_lo[:, k, :], w_raw[:, k % 2, :], w_hi[:, k, :], ALU.subtract).then_inc(w_lo_ready, 1)
                low(0)
                low(1)
                pool.wait_ge(small_loaded, 80)
                for t in range(TILES + 1):
                    if t < TILES:
                        pool.wait_ge(y_scaled, t + 1)
                        pool.wait_ge(x_loaded[t % 2], 16 * (t // 2 + 1))
                        pool.tensor_tensor(x1[:, t % 3, :], x1[:, t % 3, :], xt[:, t % 2, :], ALU.add).then_inc(x1_ready, 1)
                    if t >= 1:
                        pool.wait_ge(h_scaled, t)
                        pool.tensor_tensor(h[:, (t - 1) % 2, :], h[:, (t - 1) % 2, :], mod[:, 1, :], ALU.add).then_inc(h_ready, 1)
                    if t < TILES:
                        pool.wait_ge(x1_ready, t + 1)
                        pool.dma_start(x1_dram[ds(t * P, P), :], x1[:, t % 3, :]).then_inc(x1_stored[t % 3], 16)
                    if t >= 1:
                        store_h(t - 1)
                    if t + 2 < TILES:
                        low(t + 2)
                for i in range(3):
                    pool.wait_ge(x1_stored[i], 16 * len(range(i, TILES, 3)))
                for i in range(2):
                    pool.wait_ge(h_stored[i], 16 * TILES // 2)

            @block.tensor
            def _(pe):
                def product(t, half):
                    bank = y[:, t % 2, ds(half * 512, 512)]
                    cols = ds(half * 512, 512)
                    if half == 0:
                        pe.wait_ge(m_lo_ready, t + 1)
                        if t >= 2:
                            pe.wait_ge(y_scaled, t - 1)
                    for k in range(KD):
                        pe.matmul(bank, m_hi[:, t % 2, k, :], w_hi[:, k, cols], start=(k == 0), stop=False)
                        pe.matmul(bank, m_hi[:, t % 2, k, :], w_lo[:, k, cols], start=False, stop=False)
                        mm = pe.matmul(bank, m_lo[:, t % 2, k, :], w_hi[:, k, cols], start=False, stop=(k == KD - 1))
                    mm.then_inc(y_half, 1)

                def turn(t):
                    pe.wait_ge(h_ready, t + 1)
                    if t >= 1:
                        pe.wait_ge(hT_ready, t)
                    for k in range(KD):
                        tr = pe.transpose(turned_h[:, ds(k * P, P)], h[:, t % 2, ds(k * P, P)], ident[:, :])
                    tr.then_inc(h_turned, 1)

                def route(t):
                    pe.wait_ge(hT_ready, t + 1)
                    if t >= 2:
                        pe.wait_ge(logit_taken, t - 1)
                    for k in range(KD):
                        mm = pe.matmul(p_logit[:, t % 2, 0:NR], hT[:, k, :], wr[:, k, :], start=(k == 0), stop=(k == KD - 1))
                    mm.then_inc(logit_summed, 1)

                pe.wait_ge(w_lo_ready, KD)
                pe.wait_ge(small_loaded, 80)
                product(0, 0)
                product(0, 1)
                for t in range(TILES + 1):
                    if t + 1 < TILES:
                        product(t + 1, 0)
                    if t >= 1:
                        turn(t - 1)
                    if t + 1 < TILES:
                        product(t + 1, 1)
                    if t >= 1:
                        route(t - 1)

            @block.vector
            def _(dve):
                dve.wait_ge(small_loaded, 80)
                for t in range(TILES + 1):
                    if t < TILES:
                        dve.wait_ge(y_rooted, t + 1)
                        dve.reciprocal(rstd[:, t % 2:t % 2 + 1], root[:, t % 2:t % 2 + 1]).then_inc(recips, 1)
                        dve.wait_ge(recips, 2 * t if t else 1)
                        if t >= 3:
                            dve.wait_ge(x1_stored[t % 3], 16 * (t // 3))
                            dve.wait_ge(h_scaled, t - 2)
                        dve.scalar_tensor_tensor(out=x1[:, t % 3, :], in0=y[:, t % 2, :], scalar=rstd[:, t % 2:t % 2 + 1],
                                                 in1=mod[:, 0, :], op0=ALU.mult, op1=ALU.mult).then_inc(y_scaled, 1)
                    if t >= 1:
                        u = t - 1
                        col = 2 + u % 2
                        dve.wait_ge(x_rooted, t)
                        if u >= 2:
                            dve.wait_ge(h_stored[u % 2], 16 * (u // 2))
                            dve.wait_ge(h_turned, u - 1)
                        dve.reciprocal(rstd[:, col:col + 1], root[:, col:col + 1]).then_inc(recips, 1)
                        dve.wait_ge(recips, 2 * t + 1 if t < TILES else 2 * TILES)
                        dve.scalar_tensor_tensor(out=h[:, u % 2, :], in0=x1[:, u % 3, :], scalar=rstd[:, col:col + 1],
                                                 in1=mod[:, 2, :], op0=ALU.mult, op1=ALU.mult).then_inc(h_scaled, 1)
                        dve.wait_ge(h_turned, t)
                        if u >= 1:
                            dve.wait_ge(logit_summed, u)
                        dve.tensor_copy(hT[:, :, :].rearrange("p k c -> p (k c)"), turned_h[:, :]).then_inc(hT_ready, 1)
                        dve.wait_ge(logit_summed, t)
                        dve.tensor_tensor(logits[:, u, :], p_logit[:, u % 2, 0:NR], rbias[:, :], ALU.add).then_inc(logit_taken, 1)


def route(nc, logits, slot_token, dest, share, table, slot_rows):
    L, T2 = TILES, 2
    with ExitStack() as ctx:
        s = Scope(nc, ctx, "route")
        iota_e, iota_b = s.sb("iota_e", [P, NE]), s.sb("iota_b", [P, NB + 1])
        thr = s.sb("thr", [P, L])
        upper, ones = s.sb("upper", [P, P]), s.sb("ones", [P, P])
        token = s.sb("token", [P, L], I32)
        none = s.sb("none", [P, NB], I32)
        gmax, gsum, gsel = s.sb("gmax", [P, L]), s.sb("gsum", [P, L]), s.sb("gsel", [P, L])
        gexp, gtmp = s.sb("gexp", [P, L, EG]), s.sb("gtmp", [P, L, EG])
        el, etmp = s.sb("el", [P, L, NE]), s.sb("etmp", [P, L, NE])
        pick = s.sb("pick", [P, T2, L, NE])
        both = s.sb("both", [P, L, NE])
        top, sel = s.sb("top", [P, T2, L]), s.sb("sel", [P, L])
        d, ex = s.sb("d", [P, L]), s.sb("ex", [P, L])
        count = s.sb("count", [P, NE])
        over = s.sb("over", [P, NE, L])
        nblk, end = s.sb("nblk", [P, NE]), s.sb("end", [P, 2, NE])
        start = s.sb("start", [P, L, NE])
        pos = s.sb("pos", [P, L, NE])
        where = s.sb("where", [P, T2, L])
        index, index2 = s.sb("index", [P, T2 * L], I32), s.sb("index2", [P, T2 * L], I32)
        cmp = s.sb("cmp", [1, NB + 1, NE])
        before = s.sb("before", [1, NB + 1, NB + 1])
        blk, tabf = s.sb("blk", [1, NB + 1]), s.sb("tabf", [1, 4, NB + 1])
        p_rank, p_total = s.ps("p_rank", [P, 512]), s.ps("p_total", [P, 512])
        (made, consts, steps, shifted, exped, picked, ranked, index_ready, cleared, scattered, slots_read, table_ready) = (
            s.sem(n) for n in ("made", "consts", "steps", "shifted", "exped", "picked", "ranked", "index_ready",
                               "cleared", "scattered", "slots_read", "table_ready"))
        def over_experts(a, n=NE):
            return a.unsqueeze(2).to_broadcast([P, L, n])

        def over_tiles(a, n=NE):
            return a.unsqueeze(1).to_broadcast([P, L, n])

        with nc.Block() as block:
            @block.gpsimd
            def _(pool):
                chain = Chain(pool, made)
                pool.iota(iota_e[:, :], pattern=[[1, NE]], base=0, channel_multiplier=0, allow_small_or_imprecise_dtypes=True)
                pool.iota(iota_b[:, :], pattern=[[1, NB + 1]], base=0, channel_multiplier=0, allow_small_or_imprecise_dtypes=True)
                pool.iota(thr[:, :], pattern=[[P, L]], base=0, channel_multiplier=0, allow_small_or_imprecise_dtypes=True)
                pool.iota(token[:, :], pattern=[[P, L]], base=0, channel_multiplier=1)
                pool.memset(none[:, :], 0)
                chain.link(pool.memset(ones[:, :], 1.0))
                pool.affine_select(out=upper[:, :], in_=ones[:, :], compare_op=ALU.is_gt, fill=0.0, base=0,
                                   pattern=[[1, P]], channel_multiplier=-1).then_inc(consts, 1)
                pool.wait_ge(consts, 1)
                pool.dma_start(slot_token.rearrange("(p b) o -> p (b o)", b=NB), none[:, :]).then_inc(cleared, 16)
                pool.wait_ge(index_ready, 1)
                pool.wait_ge(cleared, 16)
                for n in range(T2 * L):
                    pool.indirect_dma_start(out=slot_token, out_offset=bass.IndirectOffsetOnAxis(ap=index[:, n:n + 1], axis=0),
                                            in_=token[:, n % L:n % L + 1], in_offset=None).then_inc(scattered, 16)
                pool.wait_ge(scattered, 16 * T2 * L)
                pool.dma_start(slot_rows[:, 0:NB], slot_token.rearrange("(p b) o -> p (b o)", b=NB)).then_inc(slots_read, 16)
                pool.memset(slot_rows[:, NB:NB + 2], 0).then_inc(made, 1)
                pool.wait_ge(slots_read, 16)
                pool.wait_ge(made, 2)

            @block.tensor
            def _(pe):
                pe.wait_ge(picked, 1)
                pe.wait_ge(consts, 1)
                pe.matmul(p_rank[:, :], upper[:, :], both[:, :, :].rearrange("p t e -> p (t e)"), start=True, stop=True)
                pe.matmul(p_total[:, :], ones[:, :], both[:, :, :].rearrange("p t e -> p (t e)"), start=True, stop=True
                          ).then_inc(ranked, 1)

            @block.scalar
            def _(act):
                act.wait_ge(shifted, 1)
                nc.scalar.activation(gexp[:, :, :], gexp[:, :, :], ACT.Exp).then_inc(exped, 1)
                act.wait_ge(shifted, 2)
                nc.scalar.activation(ex[:, :], d[:, :], ACT.Exp).then_inc(exped, 1)

            @block.vector
            def _(dve):
                chain = Chain(dve, steps)
                tt = dve.tensor_tensor
                gl = logits[:, :, 0:EG]
                chain.link(dve.tensor_reduce(gmax[:, :], gl, AX.X, ALU.max))
                tt(gexp[:, :, :], gl, over_experts(gmax[:, :], EG), ALU.subtract).then_inc(shifted, 1)
                dve.wait_ge(consts, 1)

                def first_highest(out, one_hot, tmp, values, highest, n):
                    chain.link(tt(tmp, values, over_experts(highest, n), ALU.is_equal))
                    chain.link(dve.scalar_tensor_tensor(out=tmp, in0=tmp, scalar=-float(NE), in1=over_tiles(iota_e[:, 0:n], n),
                                                        op0=ALU.mult, op1=ALU.add))
                    chain.link(dve.tensor_reduce(out, tmp, AX.X, ALU.min))
                    chain.link(dve.tensor_scalar(out, out, float(NE), None, ALU.add))
                    chain.link(tt(one_hot, over_tiles(iota_e[:, 0:n], n), over_experts(out, n), ALU.is_equal))

                first_highest(gsel[:, :], gtmp[:, :, :], gtmp[:, :, :], gl, gmax[:, :], EG)
                chain.link(dve.tensor_scalar(gtmp[:, :, :], gtmp[:, :, :], MASKED, -MASKED, ALU.mult, ALU.add))
                chain.link(tt(el[:, :, :].rearrange("p t (g e) -> p t g e", g=EG),
                              logits[:, :, EG:NR].rearrange("p t (g e) -> p t g e", g=EG),
                              gtmp[:, :, :].unsqueeze(3).to_broadcast([P, L, EG, EPG]), ALU.add))
                chain.link(dve.tensor_reduce(top[:, 0, :], el[:, :, :], AX.X, ALU.max))
                first_highest(sel[:, :], pick[:, 0, :, :], etmp[:, :, :], el[:, :, :], top[:, 0, :], NE)
                chain.link(dve.scalar_tensor_tensor(out=el[:, :, :], in0=pick[:, 0, :, :], scalar=-3.0 * MASKED, in1=el[:, :, :],
                                                    op0=ALU.mult, op1=ALU.add))
                chain.link(dve.tensor_reduce(top[:, 1, :], el[:, :, :], AX.X, ALU.max))
                tt(d[:, :], top[:, 1, :], top[:, 0, :], ALU.subtract).then_inc(shifted, 1)
                first_highest(sel[:, :], pick[:, 1, :, :], etmp[:, :, :], el[:, :, :], top[:, 1, :], NE)
                tt(both[:, :, :], pick[:, 0, :, :], pick[:, 1, :, :], ALU.add).then_inc(picked, 1)
                dve.wait_ge(exped, 2)
                chain.link(dve.tensor_reduce(gsum[:, :], gexp[:, :, :], AX.X, ALU.add))
                chain.link(dve.tensor_scalar(d[:, :], ex[:, :], 1.0, None, ALU.add))
                chain.link(tt(gsum[:, :], gsum[:, :], d[:, :], ALU.mult))
                chain.link(dve.reciprocal(share[:, 0, :], gsum[:, :]))
                chain.link(tt(share[:, 1, :], share[:, 0, :], ex[:, :], ALU.mult))
                dve.wait_ge(ranked, 1)
                total = p_total[:, :].rearrange("p (t e) -> p t e", e=NE)
                chain.link(dve.tensor_reduce(count[:, :], p_total[:, :].rearrange("p (t e) -> p e t", e=NE), AX.X, ALU.add))
                chain.link(tt(over[:, :, :], count[:, :].unsqueeze(2).to_broadcast([P, NE, L]),
                              thr[:, :].unsqueeze(1).to_broadcast([P, NE, L]), ALU.is_gt))
                chain.link(dve.tensor_reduce(nblk[:, :], over[:, :, :], AX.X, ALU.add))
                reach, now = 1, nblk[:, :]
                while reach < NE:
                    new = end[:, reach.bit_length() % 2, :]
                    dve.tensor_copy(new[:, :reach], now[:, :reach])
                    chain.link(tt(new[:, reach:], now[:, reach:], now[:, :NE - reach], ALU.add))
                    reach, now = 2 * reach, new
                chain.link(tt(start[:, 0, :], now, nblk[:, :], ALU.subtract))
                chain.link(dve.tensor_scalar(start[:, 0, :], start[:, 0, :], float(P), None, ALU.mult))
                for t in range(1, L):
                    chain.link(tt(start[:, t, :], start[:, t - 1, :], total[:, t - 1, :], ALU.add))
                chain.link(tt(pos[:, :, :], start[:, :, :], p_rank[:, :].rearrange("p (t e) -> p t e", e=NE), ALU.add))
                for choice in range(T2):
                    chain.link(tt(etmp[:, :, :], pick[:, choice, :, :], pos[:, :, :], ALU.mult))
                    chain.link(dve.tensor_reduce(where[:, choice, :], etmp[:, :, :], AX.X, ALU.add))
                chain.link(dve.tensor_copy(dest[:, :, :], where[:, :, :]))
                flat = dest[:, :, :].rearrange("p c t -> p (c t)")
                chain.link(dve.tensor_scalar(index[:, :], flat, P - 1, 6, ALU.bitwise_and, ALU.logical_shift_left))
                chain.link(dve.tensor_scalar(index2[:, :], flat, 7, None, ALU.logical_shift_right))
                tt(index[:, :], index[:, :], index2[:, :], ALU.bitwise_or).then_inc(index_ready, 1)
                last = now[0:1, NE - 1:NE]
                chain.link(dve.tensor_scalar(blk[:, 0:1], last, -1.0, None, ALU.add))
                chain.link(tt(blk[:, 1:], iota_b[0:1, 1:], blk[:, 0:1].to_broadcast([1, NB]), ALU.min))
                chain.link(dve.memset(blk[:, 0:1], 0.0))
                chain.link(tt(cmp[:, :, :], blk[:, :].unsqueeze(2).to_broadcast([1, NB + 1, NE]),
                              now[0:1, :].unsqueeze(1).to_broadcast([1, NB + 1, NE]), ALU.is_ge))
                chain.link(dve.tensor_reduce(tabf[:, 0, :], cmp[:, :, :], AX.X, ALU.add))
                chain.link(dve.memset(tabf[:, 1, 0:1], 0.0))
                chain.link(tt(tabf[:, 1, 1:], tabf[:, 0, 1:], tabf[:, 0, 0:NB], ALU.is_gt))
                reach, src = 1, tabf[:, 1, :]
                spare = (tabf[:, 2, :], tabf[:, 3, :])
                turn = 0
                while reach < NB + 1:
                    new = spare[turn % 2]
                    dve.tensor_copy(new[:, :reach], src[:, :reach])
                    chain.link(tt(new[:, reach:], src[:, reach:], src[:, :NB + 1 - reach], ALU.add))
                    reach, src, turn = 2 * reach, new, turn + 1
                spot = spare[turn % 2]
                chain.link(dve.tensor_scalar(spot, src, -1.0, None, ALU.add))
                chain.link(tt(before[:, :, :], spot.unsqueeze(2).to_broadcast([1, NB + 1, NB + 1]),
                              src.unsqueeze(1).to_broadcast([1, NB + 1, NB + 1]), ALU.is_gt))
                chain.link(dve.tensor_reduce(spot, before[:, :, :], AX.X, ALU.add))
                dve.tensor_copy(table[:, 4, :], spot)
                dve.tensor_copy(table[:, 2, :], src)
                dve.tensor_copy(table[:, 0, :], tabf[:, 0, :])
                dve.tensor_copy(table[:, 1, :], tabf[:, 1, :])
                dve.tensor_copy(table[:, 3, 0:1], last).then_inc(table_ready, 1)
                dve.wait_ge(table_ready, 1)


def experts(nc, table, slot_rows, ident, h_dram, w_gate, w_up, w_down, y_dram):
    H2 = DE // 2
    GU, PARTS = 8, 12
    BY_POOL = (1, 4, 7, 10)
    HI_BY_DVE = (3, 9)
    with ExitStack() as ctx:
        s = Scope(nc, ctx, "moe")
        raw_gu = s.sb("raw_gu", [P, 4, 2, 2, DE])
        raw_d = s.sb("raw_d", [P, KE, D])
        hi_gu, lo_gu = s.sb("hi_gu", [P, GU, 2, 2, H2], F32R), s.sb("lo_gu", [P, GU, 2, 2, H2], F32R)
        hi_d, lo_d = s.sb("hi_d", [P, KE, D], F32R), s.sb("lo_d", [P, KE, D], F32R)
        row = s.sb("row", [P, 2], I32)
        xg = s.sb("xg", [P, 2, D])
        xT_hi, xT_lo = s.sb("xT_hi", [P, 2, KD, P], F32R), s.sb("xT_lo", [P, 2, KD, P], F32R)
        act_g = s.sb("act_g", [P, 2, H2])
        hid = s.sb("hid", [P, 2, H2])
        hT_hi, hT_lo = s.sb("hT_hi", [P, KE, P], F32R), s.sb("hT_lo", [P, KE, P], F32R)
        ys = s.sb("ys", [P, 2, D])
        zero = s.sb("zero", [P, D])
        p_turn = s.ps("p_turn", [P, 2, 512])
        p_gu = s.ps("p_gu", [P, 2, 2, 512])
        p_y = s.ps("p_y", [P, 2, 512])
        part_loaded = [s.sem(f"part_loaded{i}") for i in range(8)]
        hi_ready = [s.sem(f"hi_ready{g}") for g in range(PARTS)]
        lo_ready = [s.sem(f"lo_ready{g}") for g in range(PARTS)]
        used = [s.sem(f"used{g}") for g in range(PARTS)]
        gathered = [s.sem(f"gathered{i}") for i in range(2)]
        y_stored = [s.sem(f"y_stored{i}") for i in range(2)]
        turned = [s.sem(f"turned{i}") for i in range(2)]
        hi_taken = [s.sem(f"hi_taken{i}") for i in range(2)]
        lo_taken = [s.sem(f"lo_taken{i}") for i in range(2)]
        silu_ready = [s.sem(f"silu_ready{i}") for i in range(2)]
        hid_ready = [s.sem(f"hid_ready{i}") for i in range(2)]
        row_ready, row_seen, all_stored, zeroed, rest_zeroed, y_ready = (s.sem(n) for n in (
            "row_ready", "row_seen", "all_stored", "zeroed", "rest_zeroed", "y_ready"))

        def entry(eng, r, b, top):
            return eng.value_load(table[0:1, r, ds(b, 1)], min_val=0, max_val=top)

        def by_twos(eng, body):
            count = entry(eng, 3, 0, NB)
            with eng.Fori(0, NB // 2) as i:
                with eng.If(2 * i < count):
                    body(i)
            return count

        def raw_part(g):
            return raw_gu[:, g % 4, :, :, ds((g // 4) * H2, H2)] if g < GU else raw_d[:, g - GU, :]

        def hi_part(g):
            return hi_gu[:, g, :, :, :] if g < GU else hi_d[:, g - GU, :]

        def lo_part(g):
            return lo_gu[:, g, :, :, :] if g < GU else lo_d[:, g - GU, :]

        def source(g):
            return (part_loaded[g % 4], 32) if g < GU else (part_loaded[4 + g - GU], 16)

        def cut_high(eng, copy, g, n, b):
            loaded, per = source(g)
            eng.wait_ge(loaded, per * n)
            if b is not None:
                eng.wait_ge(used[g], b + 1)
            copy(hi_part(g), raw_part(g)).then_inc(hi_ready[g], 1)

        def cut_low(eng, g, n, b):
            eng.wait_ge(hi_ready[g], n)
            if b is not None:
                eng.wait_ge(used[g], b + 1)
            eng.tensor_tensor(lo_part(g), raw_part(g), hi_part(g), ALU.subtract).then_inc(lo_ready[g], 1)

        with nc.Block() as block:
            @block.sync
            def _(sp):
                def load(e, before):
                    for kp in range(4):
                        if before is not None:
                            sp.wait_ge(lo_ready[kp], before)
                            sp.wait_ge(lo_ready[4 + kp], before)
                        for m, w in enumerate((w_gate, w_up)):
                            sp.dma_start(raw_gu[:, kp, m, :, :],
                                         w[0, ds(e, 1), ds(kp * 2 * P, 2 * P), :].rearrange("e (k p) f -> p (e k) f", p=P)
                                         ).then_inc(part_loaded[kp], 16)
                    for k in range(KE):
                        if before is not None:
                            sp.wait_ge(lo_ready[GU + k], before)
                        sp.dma_start(raw_d[:, k, :], w_down[0, ds(e, 1), ds(k * P, P), :].rearrange("e p f -> p (e f)")
                                     ).then_inc(part_loaded[4 + k], 16)

                load(entry(sp, 0, 0, NE - 1), None)

                def reload(b):
                    with sp.If(entry(sp, 1, b, 1) > 0):
                        load(entry(sp, 0, b, NE - 1), entry(sp, 2, b, NE))

                count = by_twos(sp, lambda i: [reload(2 * i), reload(2 * i + 1)])
                sp.wait_ge(zeroed, 1)
                with sp.Fori(0, NB // 2) as i:
                    with sp.If(2 * i >= count):
                        for u in range(2):
                            sp.dma_start(y_dram[ds((2 * i + u) * P, P), :], zero[:, :]).then_inc(rest_zeroed, 16)
                    with sp.Else():
                        sp.sem_inc(rest_zeroed, 32)
                sp.wait_ge(rest_zeroed, 16 * NB)

            @block.gpsimd
            def _(pool):
                def gather(b, u):
                    pool.wait_ge(turned[1], 2 * b + 1)
                    pool.tensor_copy(row[:, u:u + 1], slot_rows[:, ds(b, 1)]).then_inc(row_ready, 1)
                    pool.wait_ge(row_ready, b + 1)
                    pool.sem_inc(row_seen, 1)
                    pool.indirect_dma_start(out=xg[:, u, :], out_offset=None, in_=h_dram,
                                            in_offset=bass.IndirectOffsetOnAxis(ap=row[:, u:u + 1], axis=0)
                                            ).then_inc(gathered[u], 16)

                def block_of(b, u):
                    gather(b + 2, u)
                    with pool.If(entry(pool, 1, b + 1, 1) > 0):
                        n = entry(pool, 2, b + 1, NE) + 1
                        for g in BY_POOL:
                            cut_low(pool, g, n, b)

                gather(0, 0)
                gather(1, 1)
                pool.memset(zero[:, :], 0.0).then_inc(zeroed, 1)
                for g in BY_POOL:
                    cut_low(pool, g, 1, None)
                by_twos(pool, lambda i: [block_of(2 * i, 0), block_of(2 * i + 1, 1)])

            @block.tensor
            def _(pe):
                pe.sem_inc(turned[1], 4)

                def turn(half, tiles, src, count):
                    pe.wait_ge(lo_taken[half], count)
                    for m in range(tiles):
                        tr = pe.transpose(p_turn[:, half, ds(m * P, P)], src(m), ident[:, :])
                    tr.then_inc(turned[half], 1)

                def turn_x(u, gathers, count):
                    pe.wait_ge(gathered[u], gathers)
                    for half in range(2):
                        turn(half, 4, lambda m: xg[:, u, ds((4 * half + m) * P, P)], count)

                def three(bank, x_hi, x_lo, w_hi, w_lo, first, last):
                    pe.matmul(bank, x_hi, w_hi, start=first, stop=False)
                    pe.matmul(bank, x_hi, w_lo, start=False, stop=False)
                    return pe.matmul(bank, x_lo, w_hi, start=False, stop=last)

                def block_of(b, u):
                    n = entry(pe, 2, b, NE) + 1

                    def gate_up(half, kp):
                        g = 4 * half + kp
                        pe.wait_ge(lo_ready[g], n)
                        for k in range(2):
                            for m in range(2):
                                mm = three(p_gu[:, half, m, 0:H2], xT_hi[:, u, 2 * kp + k, :], xT_lo[:, u, 2 * kp + k, :],
                                           hi_gu[:, g, m, k, :], lo_gu[:, g, m, k, :], kp + k == 0, kp == 3 and k == 1)
                        mm.then_inc(used[g], 1)

                    def down(k):
                        pe.wait_ge(lo_ready[GU + k], n)
                        for half in range(2):
                            cols = ds(half * 512, 512)
                            mm = three(p_y[:, half, :], hT_hi[:, k, :], hT_lo[:, k, :], hi_d[:, k, cols], lo_d[:, k, cols],
                                       k == 0, k == KE - 1)
                        mm.then_inc(used[GU + k], 1)

                    def turn_h(half):
                        pe.wait_ge(hid_ready[half], b + 2)
                        turn(half, 2, lambda m: hid[:, half, ds(m * P, P)], 2 * b + 3)

                    for half in range(2):
                        pe.wait_ge(lo_taken[half], 2 * b + 2)
                    pe.wait_ge(hid_ready[0], b + 1)
                    for kp in range(4):
                        gate_up(0, kp)
                    turn_x(1 - u, 8 * b + 16 + 8 * u, 2 * b + 2)
                    pe.wait_ge(hid_ready[1], b + 1)
                    gate_up(1, 0)
                    gate_up(1, 1)
                    turn_h(0)
                    gate_up(1, 2)
                    gate_up(1, 3)
                    pe.wait_ge(lo_taken[0], 2 * b + 4)
                    pe.wait_ge(y_ready, b + 1)
                    down(0)
                    turn_h(1)
                    down(1)
                    pe.wait_ge(lo_taken[1], 2 * b + 4)
                    down(2)
                    down(3)

                turn_x(0, 16, 1)
                by_twos(pe, lambda i: [block_of(2 * i, 0), block_of(2 * i + 1, 1)])

            @block.scalar
            def _(act):
                copy = lambda dst, src: nc.scalar.activation(dst, src, ACT.Copy)

                def take_high(half, dst, n_tiles, count):
                    act.wait_ge(turned[half], count + (4 if half else 0))
                    copy(dst, p_turn[:, half, 0:n_tiles * P]).then_inc(hi_taken[half], 1)

                def take_x(u, count):
                    for half in range(2):
                        take_high(half, xT_hi[:, u, ds(4 * half, 4), :].rearrange("p k c -> p (k c)"), 4, count)

                def block_of(b, u):
                    new = entry(act, 1, b + 1, 1)
                    n = entry(act, 2, b + 1, NE) + 1

                    def cuts(parts):
                        with act.If(new > 0):
                            for g in parts:
                                if g not in HI_BY_DVE:
                                    cut_high(act, copy, g, n, b)

                    def silu(half):
                        act.wait_ge(used[4 * half + 3], b + 1)
                        nc.scalar.activation(act_g[:, half, :], p_gu[:, half, 0, 0:H2], ACT.Silu).then_inc(silu_ready[half], 1)

                    def take_h(half):
                        take_high(half, hT_hi[:, ds(2 * half, 2), :].rearrange("p k c -> p (k c)"), 2, 2 * b + 3)

                    cuts(range(0, 4))
                    silu(0)
                    take_x(1 - u, 2 * b + 2)
                    cuts(range(4, 6))
                    take_h(0)
                    cuts(range(6, 7))
                    silu(1)
                    take_h(1)
                    cuts(range(7, PARTS))
                    act.wait_ge(y_ready, b + 2)
                    act.dma_start(y_dram[ds(b * P, P), :], ys[:, u, :]).then_inc(y_stored[u], 16)

                for g in range(PARTS):
                    if g not in HI_BY_DVE:
                        cut_high(act, copy, g, 1, None)
                    if g == 1:
                        take_x(0, 1)
                count = by_twos(act, lambda i: [block_of(2 * i, 0), block_of(2 * i + 1, 1)])
                for u in range(2):
                    act.wait_ge(y_stored[u], 16 * ((count + 1) >> 1) + 16)
                    act.sem_inc(all_stored, 1)

            @block.vector
            def _(dve):
                dve.sem_inc(y_ready, 1)
                for u in range(2):
                    dve.sem_inc(y_stored[u], 16)
                    dve.sem_inc(hid_ready[u], 1)
                    dve.sem_inc(lo_taken[u], 1)

                def take_low(half, dst, hi, n_tiles, count):
                    dve.wait_ge(hi_taken[half], count)
                    dve.tensor_tensor(dst, p_turn[:, half, 0:n_tiles * P], hi, ALU.subtract).then_inc(lo_taken[half], 1)

                def flat(t, k, n):
                    return t[:, ds(k, n), :].rearrange("p k c -> p (k c)")

                def take_x(u, count):
                    for half in range(2):
                        take_low(half, flat(xT_lo[:, u, :, :], 4 * half, 4), flat(xT_hi[:, u, :, :], 4 * half, 4), 4, count)

                def cut(g, n, b):
                    if g in HI_BY_DVE:
                        cut_high(dve, dve.tensor_copy, g, n, b)
                    if g not in BY_POOL:
                        cut_low(dve, g, n, b)

                def block_of(b, u):
                    new = entry(dve, 1, b + 1, 1)
                    n = entry(dve, 2, b + 1, NE) + 1

                    def cuts(parts):
                        with dve.If(new > 0):
                            for g in parts:
                                cut(g, n, b)

                    def multiply(half):
                        dve.wait_ge(silu_ready[half], b + 1)
                        dve.wait_ge(used[4 * half + 3], b + 1)
                        dve.tensor_tensor(hid[:, half, :], p_gu[:, half, 1, 0:H2], act_g[:, half, :], ALU.mult
                                          ).then_inc(hid_ready[half], 1)

                    def take_h(half):
                        take_low(half, flat(hT_lo, 2 * half, 2), flat(hT_hi, 2 * half, 2), 2, 2 * b + 3)

                    cuts(range(0, 4))
                    multiply(0)
                    take_x(1 - u, 2 * b + 2)
                    cuts(range(4, 6))
                    take_h(0)
                    cuts(range(6, 7))
                    multiply(1)
                    take_h(1)
                    cuts(range(7, PARTS))
                    dve.wait_ge(used[PARTS - 1], b + 1)
                    dve.wait_ge(y_stored[u], 8 * b + (16 - 8 * u))
                    dve.tensor_copy(ys[:, u, :], p_y[:, :, :].rearrange("p a c -> p (a c)")).then_inc(y_ready, 1)

                for g in range(PARTS):
                    cut(g, 1, None)
                    if g == 1:
                        take_x(0, 1)
                by_twos(dve, lambda i: [block_of(2 * i, 0), block_of(2 * i + 1, 1)])


def combine(nc, dest, share, y_dram, x1_dram, mod_dram, out):
    BUF = 3
    with ExitStack() as ctx:
        s = Scope(nc, ctx, "comb")
        yy = s.sb("yy", [P, BUF, 2, D])
        x1 = s.sb("x1", [P, BUF, D])
        y = s.sb("y", [P, BUF, D])
        sq = s.sb("sq", [P, D])
        mod = s.sb("mod", [P, D])
        eps = s.sb("eps", [P, 1])
        ms, root, rstd = s.sb("ms", [P, 2]), s.sb("root", [P, 2]), s.sb("rstd", [P, 2])
        gathered = [s.sem(f"gathered{i}") for i in range(BUF)]
        x_loaded = [s.sem(f"x_loaded{i}") for i in range(BUF)]
        stored = [s.sem(f"stored{i}") for i in range(BUF)]
        mod_loaded, eps_ready, first, mixed, squared, rooted, recips, scaled, summed = (s.sem(n) for n in (
            "mod_loaded", "eps_ready", "first", "mixed", "squared", "rooted", "recips", "scaled", "summed"))
        with nc.Block() as block:
            @block.gpsimd
            def _(pool):
                pool.memset(eps[:, :], EPS).then_inc(eps_ready, 1)

                for t in range(TILES):
                    if t >= BUF:
                        pool.wait_ge(mixed, t - BUF + 1)
                    for c in range(2):
                        pool.indirect_dma_start(out=yy[:, t % BUF, c, :], out_offset=None, in_=y_dram,
                                                in_offset=bass.IndirectOffsetOnAxis(ap=dest[:, c, t:t + 1], axis=0)
                                                ).then_inc(gathered[t % BUF], 16)

            @block.sync
            def _(sp):
                sp.dma_start(mod[:, :], mod_dram[0:1, 5 * D:6 * D].partition_broadcast(P)).then_inc(mod_loaded, 16)

                def load(t):
                    if t >= BUF:
                        sp.wait_ge(stored[t % BUF], 16 * (t // BUF))
                    sp.dma_start(x1[:, t % BUF, :], x1_dram[ds(t * P, P), :]).then_inc(x_loaded[t % BUF], 16)

                load(0)
                load(1)
                for t in range(TILES):
                    if t + 2 < TILES:
                        load(t + 2)
                    sp.wait_ge(summed, t + 1)
                    sp.dma_start(out[0, ds(t * P, P), :], x1[:, t % BUF, :]).then_inc(stored[t % BUF], 16)
                for i in range(BUF):
                    sp.wait_ge(stored[i], 16 * len(range(i, TILES, BUF)))

            @block.scalar
            def _(act):
                act.wait_ge(eps_ready, 1)
                for t in range(TILES):
                    act.wait_ge(mixed, t + 1)
                    if t >= 2:
                        act.wait_ge(recips, t - 1)
                    nc.scalar.activation(sq[:, :], y[:, t % BUF, :], ACT.Square, accum_out=ms[:, t % 2:t % 2 + 1]).then_inc(squared, 1)
                    act.wait_ge(squared, t + 1)
                    nc.scalar.activation(root[:, t % 2:t % 2 + 1], ms[:, t % 2:t % 2 + 1], ACT.Sqrt, scale=1.0 / D,
                                         bias=eps[:, 0:1]).then_inc(rooted, 1)

            @block.vector
            def _(dve):
                def mix(t):
                    dve.wait_ge(gathered[t % BUF], 32 * (t // BUF + 1))
                    dve.tensor_scalar(y[:, t % BUF, :], yy[:, t % BUF, 0, :], share[:, 0, t:t + 1], None, ALU.mult).then_inc(first, 1)
                    dve.wait_ge(first, t + 1)
                    dve.scalar_tensor_tensor(out=y[:, t % BUF, :], in0=yy[:, t % BUF, 1, :], scalar=share[:, 1, t:t + 1],
                                             in1=y[:, t % BUF, :], op0=ALU.mult, op1=ALU.add).then_inc(mixed, 1)

                dve.wait_ge(mod_loaded, 16)
                mix(0)
                for t in range(TILES):
                    if t + 1 < TILES:
                        mix(t + 1)
                    dve.wait_ge(rooted, t + 1)
                    dve.reciprocal(rstd[:, t % 2:t % 2 + 1], root[:, t % 2:t % 2 + 1]).then_inc(recips, 1)
                    dve.wait_ge(recips, t + 1)
                    dve.scalar_tensor_tensor(out=y[:, t % BUF, :], in0=y[:, t % BUF, :], scalar=rstd[:, t % 2:t % 2 + 1],
                                             in1=mod[:, :], op0=ALU.mult, op1=ALU.mult).then_inc(scaled, 1)
                    dve.wait_ge(scaled, t + 1)
                    dve.wait_ge(x_loaded[t % BUF], 16 * (t // BUF + 1))
                    dve.tensor_tensor(x1[:, t % BUF, :], y[:, t % BUF, :], x1[:, t % BUF, :], ALU.add).then_inc(summed, 1)


def build(nc, x, c, w_ada, b_ada, g_pre_mix, g_post_mix, g_pre_ffn, g_post_ffn, w_in, w_pool_group, pool_scale,
          w_branch_pool, w_branch_att, w_out, w_group_router, b_group_router, w_expert_router, b_expert_router,
          w_exp_gate, w_exp_up, w_exp_down, out):
    def dram(name, shape, dt=F32):
        return nc.dram_tensor(name, shape, dt).ap()

    mod_dram = dram("mod_rows", (1, 6 * D))
    proj = dram("projected", (IN_TILES * P, SEQ))
    att = dram("attended", (len(DILATIONS), SEQ, HPG * ROW))
    merged = dram("merged", (D, SEQ))
    x1_dram = dram("x_mixed", (SEQ, D))
    h_dram = dram("h_moe", (SEQ, D))
    slot_token = dram("slot_token", (NB * P, 1), I32)
    y_dram = dram("y_slots", (NB * P, D))
    with ExitStack() as ctx:
        def top(name, shape, dt=F32):
            return ctx.enter_context(nc.sbuf_tensor(name, shape, dt))

        ident = top("ident", [P, P])
        constants(nc, ident)
        condition(nc, c, w_ada, b_ada, (g_pre_mix, g_post_mix, g_pre_ffn, g_post_ffn), mod_dram)
        with ExitStack() as mixer:
            h_hi = mixer.enter_context(nc.sbuf_tensor("h_hi", [P, KD, SEQ], F32R))
            h_lo = mixer.enter_context(nc.sbuf_tensor("h_lo", [P, KD, SEQ], F32R))
            normalise(nc, x, mod_dram, ident, h_hi, h_lo)
            project(nc, w_in, h_hi, h_lo, proj)
        attend(nc, proj, ident, att)
        merge(nc, proj, att, ident, w_pool_group, pool_scale, w_branch_pool, w_branch_att, merged)
        dest, share = top("dest", [P, 2, TILES], I32), top("share", [P, 2, TILES])
        table, slot_rows = top("table", [1, 5, NB + 1], I32), top("slot_rows", [P, NB + 2], I32)
        with nc.sbuf_tensor("logits", [P, TILES, NR], F32) as logits:
            mix_out(nc, x, merged, w_out, mod_dram, ident, w_group_router, w_expert_router, b_group_router,
                    b_expert_router, x1_dram, h_dram, logits)
            route(nc, logits, slot_token, dest, share, table, slot_rows)
        experts(nc, table, slot_rows, ident, h_dram, w_exp_gate, w_exp_up, w_exp_down, y_dram)
        combine(nc, dest, share, y_dram, x1_dram, mod_dram, out)


_INS = ["x", "c", "w_ada", "b_ada", "g_pre_mix", "g_post_mix", "g_pre_ffn", "g_post_ffn", "w_in", "w_pool_group",
        "pool_scale", "w_branch_pool", "w_branch_att", "w_out", "w_group_router", "b_group_router", "w_expert_router",
        "b_expert_router", "w_exp_gate", "w_exp_up", "w_exp_down"]


def kernel(**inputs):
    import numpy as np
    import concourse.bacc as bacc
    from concourse.bass_utils import run_bass_kernel_spmd

    nc = bacc.Bacc("TRN2", target_bir_lowering=False, num_devices=1)
    arrays, args = {}, {}
    for name in _INS:
        a = np.ascontiguousarray(inputs[name])
        arrays[f"in_{name}"] = a
        args[name] = nc.dram_tensor(f"in_{name}", a.shape, mybir.dt.from_np(a.dtype), kind="ExternalInput").ap()
    args["out"] = nc.dram_tensor("out_0", (1, SEQ, D), F32, kind="ExternalOutput").ap()
    build(nc, **args)
    r = run_bass_kernel_spmd(nc, [arrays], core_ids=[0])
    return r.results[0]["out_0"]
```

```python
from contextlib import ExitStack

import concourse.bass as bass
from concourse import mybir

P = 128
D = 1024
SEQ = 2048
KD = D // P
TILES = SEQ // P
TG = SEQ // 512
POOL_WINDOWS = (2, 4, 8, 16)
POOL_TILES = len(POOL_WINDOWS)
HEADS = 12
HPG = 4
DILATIONS = (1, 4, 16)
PAIRS_OF_GROUP = HPG // 2
IN_TILES = (4 * P + 3 * HEADS * 64 + 2 * D) // P
Q_TILE, K_TILE, V_TILE, GATE_TILE = 4, 10, 16, 22
EG, EPG = 4, 8
NE = EG * EPG
DE = 512
KE = DE // P
NB = 64
EPS = 1e-6

F32 = mybir.dt.float32
F32R = mybir.dt.float32r
I32 = mybir.dt.int32
ALU = mybir.AluOpType
ACT = mybir.ActivationFunctionType
AX = mybir.AxisListType
ds = bass.ds


class Chain:

    def __init__(self, eng, sem):
        self.eng, self.sem, self.at, self.n = eng, sem, 0, 0

    def link(self, ins):
        self.n += 1
        ins.then_inc(self.sem, 1)
        self.eng.wait_ge(self.sem, self.at + self.n)

    def turn(self, at):
        self.at, self.n = at, 0


class Scope:

    def __init__(self, nc, ctx, name):
        self.nc, self.ctx, self.name, self.sems = nc, ctx, name, []
        ctx.callback(self.clear)

    def sb(self, name, shape, dt=F32):
        return self.ctx.enter_context(self.nc.sbuf_tensor(f"{self.name}_{name}", shape, dt))

    def ps(self, name, shape, dt=F32):
        return self.ctx.enter_context(self.nc.psum_tensor(f"{self.name}_{name}", shape, dt))

    def sem(self, name):
        self.sems.append(self.nc.alloc_semaphore(f"{self.name}_{name}"))
        return self.sems[-1]

    def clear(self):
        self.nc.clear_and_free_semaphores(self.sems)
        self.nc.all_engine_barrier()


def normalise(nc, x, c, w_ada, b_ada, g_pre_mix, ident, act_c, h_hi, h_lo):
    COLS, RING, XBUF, G = 2 * D, 3, 4, 2
    GROUPS = TILES // G
    with ExitStack() as ctx:
        s = Scope(nc, ctx, "norm")
        ccol, cexp = s.sb("ccol", [P, KD]), s.sb("cexp", [P, KD])
        w_ring = s.sb("w_ring", [P, RING, COLS])
        acc = s.sb("acc", [P, COLS])
        ones = s.sb("ones", [P, 1])
        rows = s.sb("rows", [3 * KD, P])
        cols = s.sb("cols", [P, 3 * KD])
        shift, scale = s.sb("shift", [P, KD]), s.sb("scale", [P, KD])
        eps = s.sb("eps", [P, 1])
        ms, root, rstd = s.sb("ms", [P, TILES]), s.sb("root", [P, TILES]), s.sb("rstd", [P, TILES])
        xt = s.sb("xt", [P, XBUF, D])
        sq = s.sb("sq", [P, D])
        h = s.sb("h", [P, 2, KD, G * P])
        psum = s.ps("psum", [P, 2, KD, G * P])
        c_loaded, rows_loaded = s.sem("c_loaded"), s.sem("rows_loaded")
        chunk_loaded = [s.sem(f"chunk_loaded{r}") for r in range(RING)]
        x_loaded = [s.sem(f"x_loaded{i}") for i in range(XBUF)]
        (exp_ready, acc_zero, chunk_used, set_up, cols_turned, mod_summed, mod_taken, steps, squared, rooted, recips,
         scaled, turned, taken, h_ready, hi_ready, lo_ready, last_hi_ready) = (s.sem(n) for n in (
             "exp_ready", "acc_zero", "chunk_used", "set_up", "cols_turned", "mod_summed", "mod_taken", "steps", "squared",
             "rooted", "recips", "scaled", "turned", "taken", "h_ready", "hi_ready", "lo_ready", "last_hi_ready"))
        w = w_ada[0].rearrange("(p k) n -> p k n", k=KD)

        def group(t, g):
            return t[:, :, ds(g * G * P, G * P)]

        def half_of(t, part):
            return t[:, ds(4 * part, 4), ds((GROUPS - 1) * G * P, G * P)]

        with nc.Block() as block:
            @block.sync
            def _(sp):
                def load_x(t):
                    if t >= XBUF:
                        sp.wait_ge(turned, t - XBUF + 1)
                    sp.dma_start(xt[:, t % XBUF, :], x[0, ds(t * P, P), :]).then_inc(x_loaded[t % XBUF], 16)

                sp.dma_start(ccol[:, :], c.rearrange("b (p k) -> (b p) k", k=KD)).then_inc(c_loaded, 16)
                for k in range(KD):
                    if k >= RING:
                        sp.wait_ge(chunk_used, k - RING + 1)
                    sp.dma_start(w_ring[:, k % RING, :], w[:, k, 0:COLS]).then_inc(chunk_loaded[k % RING], 16)
                    if k == 0:
                        sp.dma_start(rows[0:2 * KD, :], b_ada[0, 0:COLS].rearrange("(k p) -> k p", p=P)).then_inc(rows_loaded, 16)
                        sp.dma_start(rows[2 * KD:3 * KD, :], g_pre_mix[0].rearrange("(k p) -> k p", p=P)).then_inc(rows_loaded, 16)
                    if k % 2:
                        load_x(k // 2)
                for t in range(KD // 2, TILES):
                    load_x(t)

            @block.gpsimd
            def _(pool):
                pool.memset(eps[:, :], EPS).then_inc(set_up, 1)
                pool.memset(ones[:, :], 1.0).then_inc(set_up, 1)
                for g in range(GROUPS - 1):
                    pool.wait_ge(h_ready, KD * (g + 1))
                    pool.wait_ge(hi_ready, g + 1)
                    pool.tensor_tensor(group(h_lo, g), h[:, g % 2, :, :], group(h_hi, g), ALU.subtract).then_inc(lo_ready, 1)

            @block.scalar
            def _(act):
                def squares(t):
                    act.wait_ge(x_loaded[t % XBUF], 16 * (t // XBUF + 1))
                    if t:
                        act.wait_ge(squared, t)
                    nc.scalar.activation(sq[:, :], xt[:, t % XBUF, :], ACT.Square, accum_out=ms[:, t:t + 1]).then_inc(squared, 1)

                def roots(t):
                    act.wait_ge(squared, t + 1)
                    nc.scalar.activation(root[:, t:t + 1], ms[:, t:t + 1], ACT.Sqrt, scale=1.0 / D,
                                         bias=eps[:, 0:1]).then_inc(rooted, 1)

                def high(g):
                    act.wait_ge(h_ready, KD * (g + 1))
                    nc.scalar.activation(group(h_hi, g), h[:, g % 2, :, :], ACT.Copy).then_inc(hi_ready, 1)

                act.wait_ge(c_loaded, 16)
                nc.scalar.activation(cexp[:, :], ccol[:, :], ACT.Exp, scale=-1.0).then_inc(exp_ready, 1)
                act.wait_ge(set_up, 2)
                squares(0)
                for t in range(TILES):
                    if t + 1 < TILES:
                        squares(t + 1)
                    roots(t)
                    if t >= 5 and t % G:
                        high(t // G - 2)
                high(GROUPS - 2)
                for part in range(2):
                    act.wait_ge(h_ready, KD * (GROUPS - 1) + 4 * (part + 1))
                    nc.scalar.activation(half_of(h_hi, part), h[:, (GROUPS - 1) % 2, ds(4 * part, 4), :], ACT.Copy).then_inc(last_hi_ready, 1)

            @block.tensor
            def _(pe):
                pe.wait_ge(rows_loaded, 32)
                pe.transpose(psum[:, 1, 0, 0:3 * KD], rows[:, :], ident[0:3 * KD, 0:3 * KD]).then_inc(cols_turned, 1)
                pe.wait_ge(set_up, 2)

                def turn(t):
                    g, m = divmod(t, G)
                    pe.wait_ge(scaled, t + 1)
                    if g >= 2 and m == 0:
                        pe.wait_ge(h_ready, KD * (g - 1))
                    for k in range(KD):
                        tr = pe.transpose(psum[:, g % 2, k, ds(m * P, P)], xt[:, t % XBUF, ds(k * P, P)], ident[:, :])
                    tr.then_inc(turned, 1)

                for t in range(G):
                    turn(t)
                pe.wait_ge(chunk_used, KD)
                pe.wait_ge(mod_taken, 1)
                for n in range(2 * KD):
                    mm = pe.matmul(psum[:, 1, 0, n:n + 1], acc[:, ds(n * P, P)], ones[:, :], start=True, stop=True)
                mm.then_inc(mod_summed, 1)
                pe.wait_ge(mod_taken, 3)
                for t in range(G, TILES):
                    turn(t)

            @block.vector
            def _(dve):
                chain = Chain(dve, steps)
                dve.memset(acc[:, :], 0.0).then_inc(acc_zero, 1)
                dve.wait_ge(exp_ready, 1)
                chain.link(dve.tensor_scalar(cexp[:, :], cexp[:, :], 1.0, None, ALU.add))
                chain.link(dve.reciprocal(cexp[:, :], cexp[:, :]))
                chain.link(dve.tensor_tensor(act_c[:, :], cexp[:, :], ccol[:, :], ALU.mult))
                dve.wait_ge(acc_zero, 1)

                def scale_x(t):
                    dve.wait_ge(rooted, t + 1)
                    dve.reciprocal(rstd[:, t:t + 1], root[:, t:t + 1]).then_inc(recips, 1)
                    dve.wait_ge(recips, t + 1)
                    dve.wait_ge(x_loaded[t % XBUF], 16 * (t // XBUF + 1))
                    dve.tensor_scalar(xt[:, t % XBUF, :], xt[:, t % XBUF, :], rstd[:, t:t + 1], None, ALU.mult).then_inc(scaled, 1)

                for k in range(KD):
                    dve.wait_ge(chunk_loaded[k % RING], 16 * (k // RING + 1))
                    if k:
                        dve.wait_ge(chunk_used, k)
                    dve.scalar_tensor_tensor(out=acc[:, :], in0=w_ring[:, k % RING, :], scalar=act_c[:, k:k + 1], in1=acc[:, :],
                                             op0=ALU.mult, op1=ALU.add).then_inc(chunk_used, 1)
                    if k % 2 and k > 1:
                        scale_x(k // 2 - 1)
                dve.wait_ge(cols_turned, 1)
                dve.tensor_copy(cols[:, :], psum[:, 1, 0, 0:3 * KD]).then_inc(mod_taken, 1)
                dve.wait_ge(mod_summed, 1)
                dve.wait_ge(mod_taken, 1)
                dve.tensor_tensor(shift[:, :], psum[:, 1, 0, 0:KD], cols[:, 0:KD], ALU.add).then_inc(mod_taken, 1)
                dve.tensor_tensor(scale[:, :], psum[:, 1, 0, KD:2 * KD], cols[:, KD:2 * KD], ALU.add).then_inc(mod_taken, 1)
                dve.wait_ge(mod_taken, 3)
                chain.link(dve.scalar_tensor_tensor(out=scale[:, :], in0=scale[:, :], scalar=1.0, in1=cols[:, 2 * KD:3 * KD],
                                                    op0=ALU.add, op1=ALU.mult))
                ahead = KD // 2 - 1
                for g in range(GROUPS):
                    if ahead < TILES:
                        scale_x(ahead)
                        ahead += 1
                    dve.wait_ge(turned, G * (g + 1))
                    if g >= 2:
                        dve.wait_ge(lo_ready, g - 1)
                    for k in range(KD):
                        dve.tensor_scalar(h[:, g % 2, k, :], psum[:, g % 2, k, :], scale[:, k:k + 1], shift[:, k:k + 1], ALU.mult, ALU.add
                                          ).then_inc(h_ready, 1)
                    if ahead < TILES:
                        scale_x(ahead)
                        ahead += 1
                for part in range(2):
                    dve.wait_ge(last_hi_ready, part + 1)
                    dve.tensor_tensor(half_of(h_lo, part), h[:, (GROUPS - 1) % 2, ds(4 * part, 4), :], half_of(h_hi, part),
                                      ALU.subtract).then_inc(lo_ready, 1)


def project(nc, w_in, w_ada, act_c, h_hi, h_lo, proj, ada_part):
    FIRST_GATE = GATE_TILE // 2
    assert IN_TILES // 2 - FIRST_GATE == KD
    with ExitStack() as ctx:
        s = Scope(nc, ctx, "proj")
        w_rest = s.sb("w_rest", [P, 4 * D])
        rest_loaded, rest_used, part_stored = (s.sem(n) for n in ("rest_loaded", "rest_used", "part_stored"))
        raw = s.sb("raw", [P, 2, KD, P])
        w_hi = s.sb("w_hi", [P, 2, KD, P], F32R)
        w_lo = s.sb("w_lo", [P, 2, KD, P], F32R)
        out = s.sb("out", [P, 2, SEQ])
        sums = s.sb("sums", [P, 2, SEQ])
        inv = s.sb("inv", [P, 16])
        psum = s.ps("psum", [P, 2, TG, 512])
        loaded = [s.sem(f"loaded{i}") for i in range(2)]
        hi_ready = [s.sem(f"hi_ready{i}") for i in range(2)]
        lo_ready = [s.sem(f"lo_ready{i}") for i in range(2)]
        summed = [s.sem(f"summed{i}") for i in range(2)]
        taken = [s.sem(f"taken{i}") for i in range(2)]
        tile_done = [s.sem(f"tile_done{i}") for i in range(2)]
        stored = [s.sem(f"stored{i}") for i in range(2)]
        steps = s.sem("steps")
        acc = sums[:, :, :].rearrange("p a t -> p (a t)")
        PAIRS = IN_TILES // 2
        with nc.Block() as block:
            @block.sync
            def _(sp):
                def load(j, u):
                    sp.dma_start(raw[:, u, :, :], w_in[0, :, ds((2 * j + u) * P, P)].rearrange("(k p) f -> p k f", p=P)
                                 ).then_inc(loaded[u], 16)

                def store(j, u):
                    sp.wait_ge(tile_done[u], j + 1)
                    sp.dma_start(proj[ds((2 * j + u) * P, P), :], out[:, u, :]).then_inc(stored[u], 16)

                for u in range(2):
                    load(0, u)
                def pair_of_tiles(j):
                    for u in range(2):
                        sp.wait_ge(lo_ready[u], j)
                        load(j, u)
                    for u in range(2):
                        store(j - 1, u)

                with sp.Fori(1, FIRST_GATE) as j:
                    pair_of_tiles(j)
                ada = w_ada[0].rearrange("(p k) n -> p k n", k=KD)
                with sp.Fori(0, KD) as k:
                    pair_of_tiles(k + FIRST_GATE)
                    sp.wait_ge(rest_used, k + 1)
                    sp.dma_start(w_rest[:, :], ada[:, ds(k, 1), 2 * D:6 * D].rearrange("p k n -> p (k n)")).then_inc(rest_loaded, 16)
                sp.wait_ge(rest_used, KD + 1)
                sp.dma_start(ada_part, acc).then_inc(part_stored, 16)
                for u in range(2):
                    store(PAIRS - 1, u)
                for u in range(2):
                    sp.wait_ge(stored[u], 16 * PAIRS)
                sp.wait_ge(part_stored, 16)

            @block.scalar
            def _(act):
                with act.Fori(0, PAIRS) as j:
                    for u in range(2):
                        act.wait_ge(loaded[u], 16 * j + 16)
                        act.wait_ge(summed[u], TG * j + TG)
                        nc.scalar.activation(w_hi[:, u, :, :], raw[:, u, :, :], ACT.Copy).then_inc(hi_ready[u], 1)

            @block.gpsimd
            def _(pool):
                with pool.Fori(0, PAIRS) as j:
                    for u in range(2):
                        pool.wait_ge(hi_ready[u], j + 1)
                        pool.tensor_tensor(w_lo[:, u, :, :], raw[:, u, :, :], w_hi[:, u, :, :], ALU.subtract
                                           ).then_inc(lo_ready[u], 1)

            @block.tensor
            def _(pe):
                for u in range(2):
                    pe.sem_inc(summed[u], TG)
                with pe.Fori(0, PAIRS) as j:
                    for u in range(2):
                        pe.wait_ge(lo_ready[u], j + 1)
                        for tg in range(TG):
                            pe.wait_ge(taken[u], TG * j + tg + 1)
                            for k in range(KD):
                                tok = ds(tg * 512, 512)
                                bank = psum[:, u, tg, :]
                                pe.matmul(bank, w_hi[:, u, k, :], h_hi[:, k, tok], start=(k == 0), stop=False)
                                pe.matmul(bank, w_hi[:, u, k, :], h_lo[:, k, tok], start=False, stop=False)
                                mm = pe.matmul(bank, w_lo[:, u, k, :], h_hi[:, k, tok], start=False, stop=(k == KD - 1))
                            mm.then_inc(summed[u], 1)

            @block.vector
            def _(dve):
                chain = Chain(dve, steps)
                for u in range(2):
                    dve.sem_inc(taken[u], TG)
                for t in range(15):
                    last = dve.memset(inv[:, t:t + 1], 1.0 / (t + 1))
                chain.link(last)

                def take(j, u, dilation):
                    view = out[:, u, :].rearrange("p (r m) -> p m r", r=dilation)
                    per = 512 // dilation
                    for tg in range(TG):
                        dve.wait_ge(summed[u], TG * j + TG + tg + 1)
                        ins = dve.tensor_copy(view[:, ds(tg * per, per), :],
                                              psum[:, u, tg, :].rearrange("p (m r) -> p m r", r=dilation))
                        ins.then_inc(taken[u], 1)

                for j in range(POOL_TILES // 2):
                    for u in range(2):
                        window = POOL_WINDOWS[2 * j + u]
                        if j:
                            dve.wait_ge(stored[u], 16 * j)
                        take(j, u, 1)
                        dve.wait_ge(taken[u], TG * (j + 2))
                        chan = out[:, u, :]
                        reach, now = 1, chan
                        while reach < window:
                            new = sums[:, reach.bit_length() % 2, :]
                            dve.tensor_copy(new[:, :reach], now[:, :reach])
                            chain.link(dve.tensor_tensor(new[:, reach:], now[:, reach:], now[:, :SEQ - reach], ALU.add))
                            reach, now = 2 * reach, new
                        head = window - 1
                        chain.link(dve.tensor_tensor(now[:, :head], now[:, :head], inv[:, :head], ALU.mult))
                        chain.link(dve.tensor_tensor(chan[:, :head], now[:, :head], chan[:, :head], ALU.subtract))
                        chain.link(dve.scalar_tensor_tensor(out=chan[:, head:], in0=now[:, head:], scalar=1.0 / window,
                                                            in1=chan[:, head:], op0=ALU.mult, op1=ALU.subtract))
                        dve.sem_inc(tile_done[u], 1)
                first = POOL_TILES // 2
                groups = len(DILATIONS)
                with dve.Fori(0, 3) as part:
                    for g, dilation in enumerate(DILATIONS):
                        j = part * groups + (first + g)
                        for u in range(2):
                            dve.wait_ge(stored[u], 16 * j)
                            take(j, u, dilation)
                            dve.wait_ge(taken[u], TG * j + 2 * TG)
                            dve.sem_inc(tile_done[u], 1)
                dve.memset(acc, 0.0).then_inc(rest_used, 1)
                with dve.Fori(0, KD) as k:
                    j = k + FIRST_GATE
                    for u in range(2):
                        dve.wait_ge(stored[u], 16 * j)
                        take(j, u, 1)
                        dve.wait_ge(taken[u], TG * j + 2 * TG)
                        dve.sem_inc(tile_done[u], 1)
                        if u == 0:
                            dve.wait_ge(rest_loaded, 16 * k + 16)
                            dve.wait_ge(rest_used, k + 1)
                            dve.scalar_tensor_tensor(out=acc, in0=w_rest[:, :], scalar=act_c[:, ds(k, 1)], in1=acc,
                                                     op0=ALU.mult, op1=ALU.add).then_inc(rest_used, 1)


def constants(nc, ident):
    with ExitStack() as ctx:
        s = Scope(nc, ctx, "const")
        zeroed, ready = s.sem("zeroed"), s.sem("ready")
        with nc.Block() as block:
            @block.gpsimd
            def _(pool):
                pool.memset(ident[:, :], 0.0).then_inc(zeroed, 1)
                pool.wait_ge(zeroed, 1)
                pool.affine_select(out=ident[:, :], in_=ident[:, :], compare_op=ALU.not_equal, fill=1.0,
                                   base=0, pattern=[[-1, P]], channel_multiplier=1).then_inc(ready, 1)
                pool.wait_ge(ready, 1)


ROW = 66
MASKED = 1e38


def attend(nc, proj, ident, att):
    units = []
    for g, dilation in enumerate(DILATIONS):
        blocks_of_residue = TILES // dilation
        width = P if blocks_of_residue == 1 else 2 * P
        step = 512 // width
        for pair in range(PAIRS_OF_GROUP):
            for b in range(0, TILES, step):
                units.append((g, pair, b, step, width))
    N = len(units)
    pair_of = [PAIRS_OF_GROUP * g + pair for g, pair, *_ in units]
    first_of = [n == 0 or pair_of[n] != pair_of[n - 1] for n in range(N)]
    last_of = [max(n for n in range(N) if pair_of[n] == q) for q in range(6)]
    v_half_at = {n + half: half for n in range(N) if first_of[n] for half in range(2)}
    turn_of = [n + sum(m in v_half_at for m in range(n + 1)) for n in range(N)]
    with ExitStack() as ctx:
        s = Scope(nc, ctx, "att")
        qkv = s.sb("qkv", [P, 2, 3, SEQ])
        v = s.sb("v", [P, 2, TILES, P])
        dist = s.sb("dist", [P, 3 * 2 * P])
        dist_own = s.sb("dist_own", [P, 4 * P])
        bias = s.sb("bias", [P, 2, 2, 3 * 2 * P])
        score = s.sb("score", [P, 2, 2, 512])
        prob = s.sb("prob", [P, 2, 2, 512])
        probT = s.sb("probT", [P, 2, 2, 512])
        neg = s.sb("neg", [P, 2, 2, 4])
        res = s.sb("res", [P, 4, 4, 2, ROW])
        p_score = s.ps("p_score", [P, 2, 2, 512])
        p_turn = s.ps("p_turn", [P, 2, 512])
        p_out = s.ps("p_out", [P, 2, 512])
        v_loaded = [s.sem(f"v_loaded{i}") for i in range(2)]
        loaded = [s.sem(f"loaded{i}") for i in range(2)]
        stored = [s.sem(f"stored{i}") for i in range(4)]
        names = ("dist_ready", "biased", "bias_ready", "scored", "maxed", "negated", "exped", "turned0", "turned1",
                 "copied0", "copied1", "weighed", "res_ready", "made")
        (dist_ready, biased, bias_ready, scored, maxed, negated, exped, turned0, turned1, copied0, copied1,
         weighed, res_ready, made) = (s.sem(n) for n in names)
        turned, copied = (turned0, turned1), (copied0, copied1)

        def probs_dst(n, a):
            return probT[:, n % 2, a, :]

        def copy_turn(eng, copy, turn, a, dst):
            eng.wait_ge(turned[a], turn + 1)
            copy(dst, p_turn[:, a, :]).then_inc(copied[a], 1)

        def v_dst(q, half, a):
            return v[:, q % 2, ds(8 * half + 4 * a, 4), :].rearrange("p b f -> p (b f)")

        def copy_v(eng, copy, n, a):
            q = pair_of[n]
            if n in v_half_at:
                if q >= 2:
                    eng.wait_ge(weighed, last_of[q - 2] + 1)
                copy_turn(eng, copy, turn_of[n] - 1, a, v_dst(q, v_half_at[n], a))

        def copy_probs(eng, copy, n, a):
            if n >= 2:
                eng.wait_ge(weighed, n - 1)
            copy_turn(eng, copy, turn_of[n], a, probs_dst(n, a))

        with nc.Block() as block:
            @block.sync
            def _(sp):
                def load(q):
                    g, pair = divmod(q, PAIRS_OF_GROUP)
                    if q >= 2:
                        sp.wait_ge(scored, last_of[q - 2] + 1)
                        sp.wait_ge(turned1, turn_of[last_of[q - 2]] + 1)
                    for part, tile0 in enumerate((Q_TILE, K_TILE, V_TILE)):
                        sp.dma_start(qkv[:, q % 2, part, :], proj[ds((tile0 + 2 * g + pair) * P, P), :]
                                     ).then_inc((v_loaded if part == 2 else loaded)[q % 2], 16)

                load(0)
                load(1)
                for n, (g, pair, b, step, width) in enumerate(units):
                    if first_of[n] and 2 <= pair_of[n] + 1 < 6:
                        load(pair_of[n] + 1)
                    dilation = DILATIONS[g]
                    rows = att[g].rearrange("(n i r) f -> r n i f", r=dilation, i=P)
                    per = TILES // dilation
                    if width == P:
                        dst = rows[b:b + step, 0, :, ds(2 * pair * ROW, 2 * ROW)].rearrange("r i f -> i r f")
                    else:
                        dst = rows[b // per, b % per:b % per + step, :, ds(2 * pair * ROW, 2 * ROW)].rearrange("n i f -> i n f")
                    sp.wait_ge(res_ready, n + 1)
                    sp.dma_start(dst, res[:, n % 4, 0:step, :, :].rearrange("p b a f -> p b (a f)")).then_inc(stored[n % 4], 16)
                for i in range(4):
                    sp.wait_ge(stored[i], 16 * len(range(i, N, 4)))

            @block.gpsimd
            def _(pool):
                chain = Chain(pool, made)
                own = dist[:, 256:512]
                chain.link(pool.iota(own, pattern=[[-1, 256]], base=P, channel_multiplier=1,
                                     allow_small_or_imprecise_dtypes=True))
                chain.link(pool.affine_select(out=own, in_=own, compare_op=ALU.is_ge, fill=MASKED, base=P,
                                              pattern=[[-1, 256]], channel_multiplier=1))
                chain.link(pool.affine_select(out=own, in_=own, compare_op=ALU.is_ge, fill=MASKED, base=0,
                                              pattern=[[1, 256]], channel_multiplier=-1))
                pool.memset(dist[:, 0:P], MASKED)
                pool.tensor_copy(dist[:, P:2 * P], own[:, P:2 * P])
                pool.tensor_copy(dist[:, 512:768], own)
                for m in range(4):
                    last = pool.tensor_copy(dist_own[:, ds(m * P, P)], own[:, P:2 * P])
                chain.link(last)
                for q in range(6):
                    g, pair = divmod(q, PAIRS_OF_GROUP)
                    if q >= 2:
                        pool.wait_ge(biased, 2 * (last_of[q - 2] + 1))
                    for a in range(2):
                        head = HPG * g + 2 * pair + a
                        slope = 2.0 ** (-8.0 * (head + 1) / HEADS) * DILATIONS[g]
                        src = dist_own if DILATIONS[g] == TILES else dist
                        w = src.shape[1]
                        pool.tensor_scalar(bias[:, q % 2, a, 0:w], src[:, :], -slope, None, ALU.mult).then_inc(bias_ready, 1)

            @block.tensor
            def _(pe):
                def scores(n):
                    g, pair, b, step, width = units[n]
                    q = pair_of[n]
                    pe.wait_ge(loaded[q % 2], 32 * (q // 2 + 1))
                    if n >= 2:
                        pe.wait_ge(biased, 2 * (n - 1))
                    for a in range(2):
                        part = ds(64 * a, 64)
                        for m in range(step):
                            blk = b + m
                            before = max(blk - 1, 0) if width == 2 * P else blk
                            if width == 2 * P and blk == 0:
                                for half in range(2):
                                    mm = pe.matmul(p_score[:, n % 2, a, ds(half * P, P)], qkv[part, q % 2, 0, 0:P],
                                                   qkv[part, q % 2, 1, 0:P], start=True, stop=True)
                                continue
                            mm = pe.matmul(p_score[:, n % 2, a, ds(m * width, width)],
                                           qkv[part, q % 2, 0, ds(blk * P, P)],
                                           qkv[part, q % 2, 1, ds(before * P, width)], start=True, stop=True)
                    mm.then_inc(scored, 1)

                def turn(index, tile):
                    for a in range(2):
                        if index:
                            pe.wait_ge(copied[a], index)
                        for m in range(4):
                            tr = pe.transpose(p_turn[:, a, ds(m * P, P)], tile(a, m), ident[:, :])
                        tr.then_inc(turned[a], 1)

                def turn_v(n):
                    q = pair_of[n]
                    if n in v_half_at:
                        pe.wait_ge(v_loaded[q % 2], 16 * (q // 2 + 1))
                        turn(turn_of[n] - 1, lambda a, m: qkv[:, q % 2, 2, ds((8 * v_half_at[n] + 4 * a + m) * P, P)])

                def turn_probs(n):
                    pe.wait_ge(exped, n + 1)
                    turn(turn_of[n], lambda a, m: prob[:, n % 2, a, ds(m * P, P)])

                def weigh(n):
                    g, pair, b, step, width = units[n]
                    q = pair_of[n]
                    for a in range(2):
                        pe.wait_ge(copied[a], turn_of[n] + 1)
                    if n >= 2:
                        pe.wait_ge(res_ready, n - 1)
                    halves = width // P
                    for a in range(2):
                        for m in range(step):
                            for half in range(halves):
                                blk = max(b + m + half + 1 - halves, 0)
                                mm = pe.matmul(p_out[:, n % 2, ds((m * 2 + a) * 64, 64)],
                                               probT[:, n % 2, a, ds((m * halves + half) * P, P)],
                                               v[:, q % 2, blk, ds(64 * a, 64)], start=(half == 0), stop=(half == halves - 1))
                    mm.then_inc(weighed, 1)

                scores(0)
                scores(1)
                for n in range(N):
                    turn_v(n)
                    if n + 2 < N:
                        scores(n + 2)
                    turn_probs(n)
                    if n >= 1:
                        weigh(n - 1)
                weigh(N - 1)

            @block.scalar
            def _(act):
                def exps(n):
                    step, width = units[n][3:]
                    act.wait_ge(negated, n + 1)
                    if n >= 2:
                        act.wait_ge(turned[1], turn_of[n - 2] + 1)
                    for a in range(2):
                        for m in range(step):
                            ins = nc.scalar.activation(prob[:, n % 2, a, ds(m * width, width)],
                                                       score[:, n % 2, a, ds(m * width, width)], ACT.Exp,
                                                       bias=neg[:, n % 2, a, m:m + 1],
                                                       accum_out=res[:, n % 4, m, a, 65:66])
                    ins.then_inc(exped, 1)

                copy = lambda d, x: nc.scalar.activation(d, x, ACT.Copy)
                exps(0)
                for n in range(N):
                    copy_v(act, copy, n, 0)
                    if n + 1 < N:
                        exps(n + 1)
                    copy_probs(act, copy, n, 0)

            @block.vector
            def _(dve):
                def soft(n):
                    g, pair, b, step, width = units[n]
                    q = pair_of[n]
                    dve.wait_ge(scored, n + 1)
                    dve.wait_ge(bias_ready, 2 * (q + 1))
                    if n >= 2:
                        dve.wait_ge(exped, n - 1)
                    if n >= 4:
                        dve.wait_ge(stored[n % 4], 16 * (n // 4))
                    first = width == P or b % (TILES // DILATIONS[g]) == 0
                    for a in range(2):
                        dve.scalar_tensor_tensor(out=score[:, n % 2, a, :], in0=p_score[:, n % 2, a, :], scalar=64 ** -0.5,
                                                 in1=bias[:, q % 2, a, ds(0 if first else 256, 512)],
                                                 op0=ALU.mult, op1=ALU.add).then_inc(biased, 1)
                    dve.wait_ge(biased, 2 * n + 2)
                    top = res[:, n % 4, 0:step, :, 64].rearrange("p b a -> p a b")
                    dve.tensor_reduce(top, score[:, n % 2, :, :].rearrange("p a (b w) -> p a b w", w=width), AX.X, ALU.max
                                      ).then_inc(maxed, 1)
                    dve.wait_ge(maxed, n + 1)
                    dve.tensor_scalar(neg[:, n % 2, :, 0:step], top, -1.0, None, ALU.mult).then_inc(negated, 1)

                def take(n):
                    step = units[n][3]
                    dve.wait_ge(weighed, n + 1)
                    dve.tensor_copy(res[:, n % 4, 0:step, :, 0:64],
                                    p_out[:, n % 2, 0:step * P].rearrange("p (b a f) -> p b a f", a=2, f=64)
                                    ).then_inc(res_ready, 1)

                soft(0)
                for n in range(N):
                    copy_v(dve, dve.tensor_copy, n, 1)
                    if n + 1 < N:
                        soft(n + 1)
                    copy_probs(dve, dve.tensor_copy, n, 1)
                    if n >= 1:
                        take(n - 1)
                take(N - 1)


def merge(nc, proj, att, ident, w_pool_group, pool_scale, w_branch_pool, w_branch_att, merged):
    HALF = SEQ // 2
    KP, KA = POOL_TILES, 2
    UNITS = KD * 2
    DUOS = TILES // 2
    GATES = 3
    with ExitStack() as ctx:
        s = Scope(nc, ctx, "merge")
        z_hi, z_lo = s.sb("z_hi", [P, KP, SEQ], F32R), s.sb("z_lo", [P, KP, SEQ], F32R)
        o_hi, o_lo = s.sb("o_hi", [P, KA, SEQ], F32R), s.sb("o_lo", [P, KA, SEQ], F32R)
        w_hi, w_lo = s.sb("w_hi", [P, KP + KA, D], F32R), s.sb("w_lo", [P, KP + KA, D], F32R)
        pooled = s.sb("pooled", [P, 2, HALF])
        wg = s.sb("wg", [P, KP, P])
        scale = s.sb("scale", [P, KP])
        heads = s.sb("heads", [P, 2, 2, 3, HPG, ROW])
        top = s.sb("top", [P, 2, HPG])
        coef = s.sb("coef", [P, 2, 3, HPG])
        part = s.sb("part", [P, 2, 3, HPG])
        total = s.sb("total", [P, 2, HPG])
        term = s.sb("term", [P, 2, 3, HPG, 64])
        o = s.sb("o", [P, 2, 2, KA * P])
        gate = s.sb("gate", [P, GATES, 2, HALF])
        psum = s.ps("psum", [P, 8, 512])
        pooled_loaded = [s.sem(f"pooled_loaded{i}") for i in range(2)]
        heads_loaded = [s.sem(f"heads_loaded{i}") for i in range(2)]
        w_loaded = [s.sem(f"w_loaded{i}") for i in range(KP + KA)]
        gate_loaded = [s.sem(f"gate_loaded{i}") for i in range(GATES)]
        m_stored = [s.sem(f"m_stored{i}") for i in range(GATES)]
        (small_loaded, w_hi_ready, w_lo_ready, z_summed, z_hi_ready, z_lo_ready, steps, shifted, coef_exp, o_ready,
         o_turned, o_hi_ready, o_lo_ready, gated, y_summed, gate_applied, m_ready) = (s.sem(n) for n in (
             "small_loaded", "w_hi_ready", "w_lo_ready", "z_summed", "z_hi_ready", "z_lo_ready", "steps", "shifted",
             "coef_exp", "o_ready", "o_turned", "o_hi_ready", "o_lo_ready", "gated", "y_summed", "gate_applied", "m_ready"))
        z_bank = lambda n: 2 * (n % 2)
        y_bank = lambda turn, b: (0, 2, 6)[turn % 3] + b

        def z_of(n):
            half, g = divmod(n, KP)
            return g, ds(half * HALF, HALF)

        def w_raw(t):
            return gate[:, t // 2, t % 2, :]

        def o_bank(p):
            return psum[:, 4 + p % 2, :].rearrange("p (k i c) -> p k (i c)", k=KA, c=P)

        with nc.Block() as block:
            @block.sync
            def _(sp):
                def load_heads(p):
                    if p >= 2:
                        sp.wait_ge(o_ready, p - 1)
                    for i in range(2):
                        sp.dma_start(heads[:, p % 2, i, :, :, :].rearrange("p g h f -> p g (h f)"),
                                     att[:, ds((2 * p + i) * P, P), :].rearrange("g p f -> p g f")).then_inc(heads_loaded[p % 2], 16)

                sp.dma_start(wg[:, :, :], w_pool_group[0].rearrange("g c d -> c g d")).then_inc(small_loaded, 16)
                sp.dma_start(scale[:, :], pool_scale[0].rearrange("(g p) -> p g", p=P),
                             allow_slow_non_contiguous=True).then_inc(small_loaded, 16)
                for n in range(2 * KP):
                    if n >= 2:
                        sp.wait_ge(z_summed, n - 1)
                    g, tok = z_of(n)
                    sp.dma_start(pooled[:, n % 2, :], proj[ds(g * P, P), tok]).then_inc(pooled_loaded[n % 2], 16)
                    if n % 2 == 0:
                        load_heads(n // 2)
                    if n < KP + KA:
                        rows = w_branch_pool[0, ds(n * P, P), :] if n < KP else w_branch_att[0, ds((n - KP) * P, P), :]
                        sp.dma_start(w_raw(n), rows).then_inc(w_loaded[n], 16)

                def load_gates(n):
                    half, d = divmod(n, KD)
                    if n < GATES:
                        sp.wait_ge(w_lo_ready, 2 * n + 2)
                    else:
                        sp.wait_ge(m_stored[n % GATES], 16 * (n // GATES))
                    for b in range(2):
                        sp.dma_start(gate[:, n % GATES, b, :], proj[ds((GATE_TILE + b * KD + d) * P, P), ds(half * HALF, HALF)]
                                     ).then_inc(gate_loaded[n % GATES], 16)

                load_heads(DUOS // 2)
                load_gates(0)
                load_gates(1)
                for n in range(UNITS):
                    if n + 2 < UNITS:
                        load_gates(n + 2)
                    if n < KD - 2 and n % 2 == 0:
                        load_heads((KD + n) // 2 + 1)
                    half, d = divmod(n, KD)
                    sp.wait_ge(m_ready, 2 * (n + 1))
                    sp.dma_start(merged[ds(d * P, P), ds(half * HALF, HALF)], gate[:, n % GATES, 0, :]).then_inc(m_stored[n % GATES], 16)
                for i in range(GATES):
                    sp.wait_ge(m_stored[i], 16 * len(range(i, UNITS, GATES)))

            @block.scalar
            def _(act):
                def coefficients(p):
                    act.wait_ge(shifted, p + 1)
                    nc.scalar.activation(coef[:, :, :, :], coef[:, :, :, :], ACT.Exp).then_inc(coef_exp, 1)

                def high(p):
                    act.wait_ge(o_turned, p + 1)
                    nc.scalar.activation(o_hi[:, :, ds(2 * p * P, 2 * P)], o_bank(p), ACT.Copy).then_inc(o_hi_ready, 1)

                for n in range(2 * KP):
                    if n < KP + KA:
                        act.wait_ge(w_loaded[n], 16)
                        nc.scalar.activation(w_hi[:, n, :], w_raw(n), ACT.Copy).then_inc(w_hi_ready, 1)
                    act.wait_ge(z_summed, n + 1)
                    g, tok = z_of(n)
                    nc.scalar.activation(z_hi[:, g, tok], psum[:, z_bank(n):z_bank(n) + 2, :].rearrange("p b c -> p (b c)"),
                                         ACT.Copy, scale=scale[:, g:g + 1]).then_inc(z_hi_ready, 1)
                    if n % 2:
                        coefficients(n // 2)
                        if n > 1:
                            high(n // 2 - 1)
                high(DUOS // 2 - 1)
                for n in range(UNITS):
                    if n < KD:
                        if n % 2 == 0:
                            coefficients((KD + n) // 2)
                        else:
                            high((KD + n) // 2)
                    act.wait_ge(gate_loaded[n % GATES], 32 * (n // GATES + 1))
                    nc.scalar.activation(gate[:, n % GATES, :, :], gate[:, n % GATES, :, :], ACT.Sigmoid).then_inc(gated, 1)

            @block.gpsimd
            def _(pool):
                for t in range(KP + KA):
                    pool.wait_ge(w_hi_ready, t + 1)
                    pool.tensor_tensor(w_lo[:, t, :], w_raw(t), w_hi[:, t, :], ALU.subtract).then_inc(w_lo_ready, 1)
                for n in range(UNITS):
                    for q in range(2):
                        pool.wait_ge(gate_applied, 4 * n + 2 * q + 2)
                        tok = ds(q * 512, 512)
                        pool.tensor_tensor(gate[:, n % GATES, 0, tok], gate[:, n % GATES, 0, tok], gate[:, n % GATES, 1, tok],
                                           ALU.add).then_inc(m_ready, 1)

            @block.tensor
            def _(pe):
                def turn(p):
                    pe.wait_ge(o_ready, p + 1)
                    if p >= 2:
                        pe.wait_ge(o_lo_ready, p - 1)
                    for k in range(KA):
                        for i in range(2):
                            tr = pe.transpose(psum[:, 4 + p % 2, ds((2 * k + i) * P, P)], o[:, p % 2, i, ds(k * P, P)], ident[:, :])
                    tr.then_inc(o_turned, 1)

                pe.wait_ge(small_loaded, 32)
                for n in range(2 * KP):
                    pe.wait_ge(pooled_loaded[n % 2], 16 * (n // 2 + 1))
                    if n >= 2:
                        pe.wait_ge(z_lo_ready, n - 1)
                    for q in range(2):
                        mm = pe.matmul(psum[:, z_bank(n) + q, :], wg[:, n % KP, :], pooled[:, n % 2, ds(q * 512, 512)],
                                       start=True, stop=True)
                    mm.then_inc(z_summed, 1)
                    if n % 2 and n > 1:
                        turn(n // 2 - 1)
                turn(DUOS // 2 - 1)
                pe.wait_ge(z_lo_ready, 2 * KP)
                pe.wait_ge(w_lo_ready, KP + KA)
                pe.wait_ge(o_lo_ready, DUOS // 2)
                for n in range(UNITS):
                    half, d = divmod(n, KD)
                    if n < KD and n % 2:
                        turn((KD + n) // 2)
                    if n == KD:
                        pe.wait_ge(o_lo_ready, DUOS)
                    cols = ds(d * P, P)
                    for q in range(2):
                        turn_y = 2 * n + q
                        if turn_y >= 3:
                            pe.wait_ge(gate_applied, 2 * (turn_y - 2))
                        tok = ds(half * HALF + q * 512, 512)
                        for b, (k0, k1, in_hi, in_lo) in enumerate(((0, KP, z_hi, z_lo), (KP, KP + KA, o_hi, o_lo))):
                            bank = psum[:, y_bank(turn_y, b), :]
                            for k in range(k0, k1):
                                pe.matmul(bank, w_hi[:, k, cols], in_hi[:, k - k0, tok], start=(k == k0), stop=False)
                                pe.matmul(bank, w_hi[:, k, cols], in_lo[:, k - k0, tok], start=False, stop=False)
                                mm = pe.matmul(bank, w_lo[:, k, cols], in_hi[:, k - k0, tok], start=False, stop=(k == k1 - 1))
                            mm.then_inc(y_summed, 1)

            @block.vector
            def _(dve):
                chain = Chain(dve, steps)

                def low(p):
                    dve.wait_ge(o_hi_ready, p + 1)
                    tok = ds(2 * p * P, 2 * P)
                    dve.tensor_tensor(o_lo[:, :, tok], o_bank(p), o_hi[:, :, tok], ALU.subtract).then_inc(o_lo_ready, 1)

                def add_up(p):
                    hd = heads[:, p % 2, :, :, :, :]
                    over_groups = lambda t: t[:, :, :].unsqueeze(2).to_broadcast([P, 2, 3, HPG])
                    all_heads = "p i g h f -> p (i g h) f"
                    dve.wait_ge(heads_loaded[p % 2], 32 * (p // 2 + 1))
                    chain.link(dve.tensor_tensor(top[:, :, :], hd[:, :, 0, :, 64], hd[:, :, 1, :, 64], ALU.max))
                    chain.link(dve.tensor_tensor(top[:, :, :], top[:, :, :], hd[:, :, 2, :, 64], ALU.max))
                    dve.tensor_tensor(coef[:, :, :, :], hd[:, :, :, :, 64], over_groups(top), ALU.subtract).then_inc(shifted, 1)
                    dve.wait_ge(coef_exp, p + 1)
                    chain.link(dve.tensor_tensor(part[:, :, :, :], coef[:, :, :, :], hd[:, :, :, :, 65], ALU.mult))
                    chain.link(dve.tensor_reduce(total[:, :, :], part[:, :, :, :].rearrange("p i g h -> p i h g"), AX.X, ALU.add))
                    chain.link(dve.reciprocal(total[:, :, :], total[:, :, :]))
                    chain.link(dve.tensor_tensor(coef[:, :, :, :], coef[:, :, :, :], over_groups(total), ALU.mult))
                    chain.link(dve.tensor_tensor(term[:, :, :, :, :].rearrange(all_heads), hd.rearrange(all_heads)[:, :, 0:64],
                                                 coef[:, :, :, :].rearrange("p i g h -> p (i g h)").unsqueeze(2)
                                                 .to_broadcast([P, 2 * 3 * HPG, 64]), ALU.mult))
                    if p >= 2:
                        dve.wait_ge(o_turned, p - 1)
                    flat = term[:, :, :, :, :].rearrange("p i g h f -> p i g (h f)")
                    chain.link(dve.tensor_tensor(o[:, p % 2, :, :], flat[:, :, 0, :], flat[:, :, 1, :], ALU.add))
                    dve.tensor_tensor(o[:, p % 2, :, :], o[:, p % 2, :, :], flat[:, :, 2, :], ALU.add).then_inc(o_ready, 1)

                for n in range(2 * KP):
                    dve.wait_ge(z_hi_ready, n + 1)
                    g, tok = z_of(n)
                    dve.scalar_tensor_tensor(out=z_lo[:, g, tok],
                                             in0=psum[:, z_bank(n):z_bank(n) + 2, :].rearrange("p b c -> p (b c)"),
                                             scalar=scale[:, g:g + 1], in1=z_hi[:, g, tok],
                                             op0=ALU.mult, op1=ALU.subtract).then_inc(z_lo_ready, 1)
                    if n % 2:
                        add_up(n // 2)
                        if n > 1:
                            low(n // 2 - 1)
                low(DUOS // 2 - 1)
                for n in range(UNITS):
                    if n < KD:
                        if n % 2 == 0:
                            add_up((KD + n) // 2)
                        else:
                            low((KD + n) // 2)
                    dve.wait_ge(gated, n + 1)
                    for q in range(2):
                        turn_y = 2 * n + q
                        tok = ds(q * 512, 512)
                        for b in range(2):
                            dve.wait_ge(y_summed, 2 * turn_y + b + 1)
                            dve.tensor_tensor(gate[:, n % GATES, b, tok], psum[:, y_bank(turn_y, b), :],
                                              gate[:, n % GATES, b, tok], ALU.mult).then_inc(gate_applied, 1)


NR = EG + NE


def mix_out(nc, x, merged, w_out, ada_part, b_ada, gains, ident, w_group_router, w_expert_router, b_group_router,
            b_expert_router, gate_dram, x1_dram, h_dram, logits):
    RAW = 4
    with ExitStack() as ctx:
        s = Scope(nc, ctx, "out")
        w_hi, w_lo = s.sb("w_hi", [P, KD, D], F32R), s.sb("w_lo", [P, KD, D], F32R)
        w_raw = s.sb("w_raw", [P, RAW, D])
        mT = s.sb("mT", [P, 2, KD, P])
        m_hi, m_lo = s.sb("m_hi", [P, 2, KD, P], F32R), s.sb("m_lo", [P, 2, KD, P], F32R)
        mod = s.sb("mod", [P, 4, D])
        part = s.sb("part", [P, 4 * D])
        gain = s.sb("gain", [P, 3, D])
        ones = s.sb("ones", [P, P])
        xt = s.sb("xt", [P, 2, D])
        sq = s.sb("sq", [P, D])
        x1 = s.sb("x1", [P, 3, D])
        h = s.sb("h", [P, 2, D])
        hT = s.sb("hT", [P, KD, P])
        wr = s.sb("wr", [P, KD, NR])
        rbias = s.sb("rbias", [P, NR])
        eps = s.sb("eps", [P, 1])
        ms, root, rstd = s.sb("ms", [P, 4]), s.sb("root", [P, 4]), s.sb("rstd", [P, 4])
        y = s.ps("y", [P, 2, D])
        turned_h = s.ps("turned_h", [P, D])
        p_logit = s.ps("p_logit", [P, 2, 512])
        w_loaded = [s.sem(f"w_loaded{i}") for i in range(RAW)]
        w_lo_ready = [s.sem(f"w_lo_ready{i}") for i in range(2)]
        m_loaded = [s.sem(f"m_loaded{i}") for i in range(2)]
        x_loaded = [s.sem(f"x_loaded{i}") for i in range(2)]
        x1_stored = [s.sem(f"x1_stored{i}") for i in range(3)]
        h_stored = [s.sem(f"h_stored{i}") for i in range(2)]
        part_loaded, bias_loaded, gain_loaded, ones_ready, row_summed, row_added, mod_ready, gate_stored = (s.sem(n) for n in (
            "part_loaded", "bias_loaded", "gain_loaded", "ones_ready", "row_summed", "row_added", "mod_ready", "gate_stored"))
        (small_loaded, eps_ready, w_hi_ready, m_hi_ready, m_lo_ready, y_half, y_squared, y_rooted, x_squared,
         x_rooted, recips, y_scaled, x1_ready, h_scaled, h_ready, h_turned, hT_ready, logit_summed, logit_taken) = (
             s.sem(n) for n in (
                 "small_loaded", "eps_ready", "w_hi_ready", "m_hi_ready", "m_lo_ready", "y_half",
                 "y_squared", "y_rooted", "x_squared", "x_rooted", "recips", "y_scaled", "x1_ready", "h_scaled",
                 "h_ready", "h_turned", "hT_ready", "logit_summed", "logit_taken"))
        with nc.Block() as block:
            @block.sync
            def _(sp):
                for k in range(KD):
                    if k >= RAW:
                        sp.wait_ge(w_lo_ready[k % 2], (k - RAW) // 2 + 1)
                    sp.dma_start(w_raw[:, k % RAW, :], w_out[0, ds(k * P, P), :]).then_inc(w_loaded[k % RAW], 16)
                for t in range(TILES + 1):
                    if t < TILES:
                        if t >= 2:
                            sp.wait_ge(m_lo_ready, t - 1)
                        sp.dma_start(mT[:, t % 2, :, :], merged.rearrange("(k p) t -> p k t", p=P)[:, :, ds(t * P, P)]
                                     ).then_inc(m_loaded[t % 2], 16)
                    if t == 1:
                        sp.dma_start(part[:, :], ada_part).then_inc(part_loaded, 16)
                        sp.dma_start(mod[:, :, :].rearrange("p m d -> p (m d)"),
                                     b_ada[0:1, 2 * D:6 * D].partition_broadcast(P)).then_inc(bias_loaded, 16)
                        for n, g in enumerate(gains):
                            sp.dma_start(gain[:, n, :], g[0:1, :].partition_broadcast(P)).then_inc(gain_loaded, 16)
                        sp.dma_start(wr[:, :, 0:EG], w_group_router[0].rearrange("(k p) e -> p k e", p=P)).then_inc(small_loaded, 16)
                        sp.dma_start(wr[:, :, EG:NR], w_expert_router[0].rearrange("(k p) e -> p k e", p=P)).then_inc(small_loaded, 16)
                        sp.dma_start(rbias[:, 0:EG], b_group_router[0:1, :].partition_broadcast(P)).then_inc(small_loaded, 16)
                        sp.dma_start(rbias[:, EG:NR], b_expert_router[0:1, :].partition_broadcast(P)).then_inc(small_loaded, 16)
                    if t < TILES:
                        if t >= 2:
                            sp.wait_ge(x1_ready, t - 1)
                        sp.dma_start(xt[:, t % 2, :], x[0, ds(t * P, P), :]).then_inc(x_loaded[t % 2], 16)
                    if t == 3:
                        sp.wait_ge(mod_ready, 3)
                        sp.dma_start(gate_dram, mod[0:1, 3, :]).then_inc(gate_stored, 16)
                sp.wait_ge(gate_stored, 16)

            @block.scalar
            def _(act):
                act.wait_ge(eps_ready, 1)

                def split(t):
                    if t >= 2:
                        act.wait_ge(y_half, 2 * (t - 1))
                    act.wait_ge(m_loaded[t % 2], 16 * (t // 2 + 1))
                    nc.scalar.activation(m_hi[:, t % 2, :, :], mT[:, t % 2, :, :], ACT.Copy).then_inc(m_hi_ready, 1)

                def squares(src, wait, col, squared, rooted, count):
                    act.wait_ge(*wait)
                    if count >= 2:
                        act.wait_ge(recips, 2 * (count - 2) + 1)
                    nc.scalar.activation(sq[:, :], src, ACT.Square, accum_out=ms[:, col:col + 1]).then_inc(squared, 1)
                    act.wait_ge(squared, count)
                    nc.scalar.activation(root[:, col:col + 1], ms[:, col:col + 1], ACT.Sqrt, scale=1.0 / D,
                                         bias=eps[:, 0:1]).then_inc(rooted, 1)

                for k in range(KD):
                    act.wait_ge(w_loaded[k % RAW], 16 * (k // RAW + 1))
                    nc.scalar.activation(w_hi[:, k, :], w_raw[:, k % RAW, :], ACT.Copy).then_inc(w_hi_ready, 1)
                split(0)
                split(1)
                for t in range(TILES + 2):
                    if t < TILES:
                        squares(y[:, t % 2, :], (y_half, 2 * t + 2), t % 2, y_squared, y_rooted, t + 1)
                    if 1 <= t <= TILES:
                        if t >= 3:
                            act.wait_ge(h_scaled, t - 2)
                        u = t - 1
                        squares(x1[:, u % 3, :], (x1_ready, t), 2 + u % 2, x_squared, x_rooted, t)
                        act.dma_start(x1_dram[ds(u * P, P), :], x1[:, u % 3, :]).then_inc(x1_stored[u % 3], 16)
                    if t + 2 < TILES:
                        split(t + 2)
                    if t >= 2:
                        u = t - 2
                        act.wait_ge(h_ready, u + 1)
                        act.dma_start(h_dram[ds(u * P, P), :], h[:, u % 2, :]).then_inc(h_stored[u % 2], 16)
                for i in range(3):
                    act.wait_ge(x1_stored[i], 16 * len(range(i, TILES, 3)))
                for i in range(2):
                    act.wait_ge(h_stored[i], 16 * TILES // 2)

            @block.gpsimd
            def _(pool):
                pool.memset(eps[:, :], EPS).then_inc(eps_ready, 1)
                pool.memset(ones[:, :], 1.0).then_inc(ones_ready, 1)

                def low(t):
                    pool.wait_ge(m_hi_ready, t + 1)
                    pool.tensor_tensor(m_lo[:, t % 2, :, :], mT[:, t % 2, :, :], m_hi[:, t % 2, :, :], ALU.subtract
                                       ).then_inc(m_lo_ready, 1)

                for k in range(1, KD, 2):
                    pool.wait_ge(w_hi_ready, k + 1)
                    pool.tensor_tensor(w_lo[:, k, :], w_raw[:, k % RAW, :], w_hi[:, k, :], ALU.subtract).then_inc(w_lo_ready[1], 1)
                low(0)
                low(1)
                pool.wait_ge(mod_ready, 3)
                for t in range(TILES + 1):
                    if t < TILES:
                        pool.wait_ge(y_scaled, t + 1)
                        pool.wait_ge(x_loaded[t % 2], 16 * (t // 2 + 1))
                        pool.tensor_tensor(x1[:, t % 3, :], x1[:, t % 3, :], xt[:, t % 2, :], ALU.add).then_inc(x1_ready, 1)
                    if t >= 1:
                        pool.wait_ge(h_scaled, t)
                        pool.tensor_tensor(h[:, (t - 1) % 2, :], h[:, (t - 1) % 2, :], mod[:, 1, :], ALU.add).then_inc(h_ready, 1)
                    if t + 2 < TILES:
                        low(t + 2)

            @block.tensor
            def _(pe):
                def product(t, half):
                    bank = y[:, t % 2, ds(half * 512, 512)]
                    cols = ds(half * 512, 512)
                    if half == 0:
                        pe.wait_ge(m_lo_ready, t + 1)
                        if t >= 2:
                            pe.wait_ge(y_scaled, t - 1)
                    for k in range(KD):
                        pe.matmul(bank, m_hi[:, t % 2, k, :], w_hi[:, k, cols], start=(k == 0), stop=False)
                        pe.matmul(bank, m_hi[:, t % 2, k, :], w_lo[:, k, cols], start=False, stop=False)
                        mm = pe.matmul(bank, m_lo[:, t % 2, k, :], w_hi[:, k, cols], start=False, stop=(k == KD - 1))
                    mm.then_inc(y_half, 1)

                def turn(t):
                    pe.wait_ge(h_ready, t + 1)
                    if t >= 1:
                        pe.wait_ge(hT_ready, t)
                    for k in range(KD):
                        tr = pe.transpose(turned_h[:, ds(k * P, P)], h[:, t % 2, ds(k * P, P)], ident[:, :])
                    tr.then_inc(h_turned, 1)

                def route(t):
                    pe.wait_ge(hT_ready, t + 1)
                    if t >= 2:
                        pe.wait_ge(logit_taken, t - 1)
                    for k in range(KD):
                        mm = pe.matmul(p_logit[:, t % 2, 0:NR], hT[:, k, :], wr[:, k, :], start=(k == 0), stop=(k == KD - 1))
                    mm.then_inc(logit_summed, 1)

                for i in range(2):
                    pe.wait_ge(w_lo_ready[i], KD // 2)
                product(0, 0)
                product(0, 1)
                pe.wait_ge(ones_ready, 1)
                pe.wait_ge(part_loaded, 16)
                for n in range(8):
                    if n >= 2:
                        pe.wait_ge(row_added, n - 1)
                    pe.matmul(y[:, 1, ds((n % 2) * 512, 512)], ones[:, :], part[:, ds(n * 512, 512)], start=True, stop=True
                              ).then_inc(row_summed, 1)
                pe.wait_ge(row_added, 8)
                pe.wait_ge(small_loaded, 64)
                for t in range(TILES + 2):
                    if t + 1 < TILES:
                        product(t + 1, 0)
                    if t >= 2:
                        route(t - 2)
                    if t + 1 < TILES:
                        product(t + 1, 1)
                    if 1 <= t <= TILES:
                        turn(t - 1)

            @block.vector
            def _(dve):
                mod_flat = mod[:, :, :].rearrange("p m d -> p (m d)")

                def add_row(n):
                    dve.wait_ge(row_summed, n + 1)
                    cols = ds(n * 512, 512)
                    dve.tensor_tensor(mod_flat[:, cols], y[:, 1, ds((n % 2) * 512, 512)], mod_flat[:, cols], ALU.add).then_inc(row_added, 1)

                for k in range(0, KD, 2):
                    dve.wait_ge(w_hi_ready, k + 1)
                    dve.tensor_tensor(w_lo[:, k, :], w_raw[:, k % RAW, :], w_hi[:, k, :], ALU.subtract).then_inc(w_lo_ready[0], 1)
                dve.wait_ge(bias_loaded, 16)
                for n in range(8):
                    add_row(n)
                dve.wait_ge(row_added, 8)
                dve.wait_ge(gain_loaded, 48)
                dve.scalar_tensor_tensor(out=mod[:, 2, :], in0=mod[:, 2, :], scalar=1.0, in1=gain[:, 1, :],
                                         op0=ALU.add, op1=ALU.mult).then_inc(mod_ready, 1)
                dve.tensor_tensor(mod[:, 0, :], mod[:, 0, :], gain[:, 0, :], ALU.mult).then_inc(mod_ready, 1)
                dve.tensor_tensor(mod[:, 3, :], mod[:, 3, :], gain[:, 2, :], ALU.mult).then_inc(mod_ready, 1)
                dve.wait_ge(mod_ready, 3)
                dve.wait_ge(small_loaded, 64)
                for t in range(TILES + 2):
                    if t < TILES:
                        dve.wait_ge(y_rooted, t + 1)
                        dve.reciprocal(rstd[:, t % 2:t % 2 + 1], root[:, t % 2:t % 2 + 1]).then_inc(recips, 1)
                        dve.wait_ge(recips, 2 * t if t else 1)
                        if t >= 3:
                            dve.wait_ge(x1_stored[t % 3], 16 * (t // 3))
                            dve.wait_ge(h_scaled, t - 2)
                        dve.scalar_tensor_tensor(out=x1[:, t % 3, :], in0=y[:, t % 2, :], scalar=rstd[:, t % 2:t % 2 + 1],
                                                 in1=mod[:, 0, :], op0=ALU.mult, op1=ALU.mult).then_inc(y_scaled, 1)
                    if 1 <= t <= TILES:
                        u = t - 1
                        col = 2 + u % 2
                        dve.wait_ge(x_rooted, t)
                        if u >= 2:
                            dve.wait_ge(h_stored[u % 2], 16 * (u // 2))
                            dve.wait_ge(h_turned, u - 1)
                        dve.reciprocal(rstd[:, col:col + 1], root[:, col:col + 1]).then_inc(recips, 1)
                        dve.wait_ge(recips, 2 * t + 1 if t < TILES else 2 * TILES)
                        dve.scalar_tensor_tensor(out=h[:, u % 2, :], in0=x1[:, u % 3, :], scalar=rstd[:, col:col + 1],
                                                 in1=mod[:, 2, :], op0=ALU.mult, op1=ALU.mult).then_inc(h_scaled, 1)
                    if t >= 2:
                        dve.wait_ge(logit_summed, t - 1)
                        dve.tensor_tensor(logits[:, t - 2, :], p_logit[:, t % 2, 0:NR], rbias[:, :], ALU.add).then_inc(logit_taken, 1)
                    if 1 <= t <= TILES:
                        dve.wait_ge(h_turned, t)
                        dve.tensor_copy(hT[:, :, :].rearrange("p k c -> p (k c)"), turned_h[:, :]).then_inc(hT_ready, 1)


def load_part(eng, g, e, raw_gu, raw_d, w_gate, w_up, w_down, loaded):
    if g < GU:
        half, kp = divmod(g, 4)
        for m, w in enumerate((w_gate, w_up)):
            eng.dma_start(raw_gu[:, g, m, :, :], w[0, ds(e, 1), ds(kp * 2 * P, 2 * P), ds(half * H2, H2)]
                          .rearrange("e (k p) f -> p (e k) f", p=P)).then_inc(loaded, 16)
    else:
        eng.dma_start(raw_d[:, g - GU, :], w_down[0, ds(e, 1), ds((g - GU) * P, P), :].rearrange("e p f -> p (e f)")
                      ).then_inc(loaded, 16)


H2 = DE // 2
GU, PARTS = 8, 12


def route(nc, logits, dest, share, table, slot_rows, raw_gu, raw_d, w_gate, w_up, w_down):
    L, T2 = TILES, 2
    with ExitStack() as ctx:
        s = Scope(nc, ctx, "route")
        iota_e, iota_b = s.sb("iota_e", [P, NE]), s.sb("iota_b", [P, NB + 1])
        thr = s.sb("thr", [P, L])
        upper, ones = s.sb("upper", [P, P]), s.sb("ones", [P, P])
        token, iota_p = s.sb("token", [P, L]), s.sb("iota_p", [P, P])
        slot_low, slot_high = s.sb("slot_low", [P, T2 * L]), s.sb("slot_high", [P, T2 * L])
        is_low, is_high = s.sb("is_low", [P, T2 * L, P]), s.sb("is_high", [P, T2 * L, NB])
        gmax, gsum, gsel = s.sb("gmax", [P, L]), s.sb("gsum", [P, L]), s.sb("gsel", [P, L])
        gexp, gtmp = s.sb("gexp", [P, L, EG]), s.sb("gtmp", [P, L, EG])
        el, etmp = s.sb("el", [P, L, NE]), s.sb("etmp", [P, L, NE])
        pick = s.sb("pick", [P, T2, L, NE])
        both = s.sb("both", [P, L, NE])
        top, sel = s.sb("top", [P, T2, L]), s.sb("sel", [P, L])
        d, ex = s.sb("d", [P, L]), s.sb("ex", [P, L])
        count = s.sb("count", [P, NE])
        over = s.sb("over", [P, NE, L])
        nblk, end = s.sb("nblk", [P, NE]), s.sb("end", [P, 2, NE])
        start = s.sb("start", [P, L, NE])
        pos = s.sb("pos", [P, L, NE])
        where = s.sb("where", [P, T2, L])
        index, index2 = s.sb("index", [P, T2 * L], I32), s.sb("index2", [P, T2 * L], I32)
        cmp = s.sb("cmp", [1, NB + 1, NE])
        blk, tabf = s.sb("blk", [1, NB + 1]), s.sb("tabf", [1, 4, NB + 1])
        p_rank, p_total, p_rows = s.ps("p_rank", [P, 512]), s.ps("p_total", [P, 512]), s.ps("p_rows", [P, 512])
        (made, consts, steps, shifted, exped, picked, ranked, index_ready, low_ready, matched, high_ready, rows_summed, rows_ready,
         table_ready, first_loaded) = (s.sem(n) for n in (
             "made", "consts", "steps", "shifted", "exped", "picked", "ranked", "index_ready", "low_ready", "matched", "high_ready",
             "rows_summed", "rows_ready", "table_ready", "first_loaded"))

        def over_experts(a, n=NE):
            return a.unsqueeze(2).to_broadcast([P, L, n])

        def over_tiles(a, n=NE):
            return a.unsqueeze(1).to_broadcast([P, L, n])

        with nc.Block() as block:
            @block.gpsimd
            def _(pool):
                chain = Chain(pool, made)
                pool.iota(iota_e[:, :], pattern=[[1, NE]], base=0, channel_multiplier=0, allow_small_or_imprecise_dtypes=True)
                pool.iota(iota_b[:, :], pattern=[[1, NB + 1]], base=0, channel_multiplier=0, allow_small_or_imprecise_dtypes=True)
                pool.iota(thr[:, :], pattern=[[P, L]], base=0, channel_multiplier=0, allow_small_or_imprecise_dtypes=True)
                pool.iota(token[:, :], pattern=[[P, L]], base=0, channel_multiplier=1, allow_small_or_imprecise_dtypes=True)
                pool.iota(iota_p[:, :], pattern=[[1, P]], base=0, channel_multiplier=0, allow_small_or_imprecise_dtypes=True)
                chain.link(pool.memset(ones[:, :], 1.0))
                pool.affine_select(out=upper[:, :], in_=ones[:, :], compare_op=ALU.is_gt, fill=0.0, base=0,
                                   pattern=[[1, P]], channel_multiplier=-1).then_inc(consts, 1)
                pool.wait_ge(consts, 1)
                pool.memset(slot_rows[:, NB:NB + 2], 0).then_inc(made, 1)
                for c in range(T2):
                    pool.wait_ge(matched, c + 1)
                    rows = is_high[:, ds(c * L, L), :]
                    pool.tensor_tensor(rows, rows, token[:, :].unsqueeze(2).to_broadcast([P, L, NB]), ALU.mult
                                       ).then_inc(high_ready, 1)
                pool.wait_ge(made, 2)

            @block.tensor
            def _(pe):
                pe.wait_ge(picked, 1)
                pe.wait_ge(consts, 1)
                pe.matmul(p_rank[:, :], upper[:, :], both[:, :, :].rearrange("p t e -> p (t e)"), start=True, stop=True)
                pe.matmul(p_total[:, :], ones[:, :], both[:, :, :].rearrange("p t e -> p (t e)"), start=True, stop=True
                          ).then_inc(ranked, 1)
                for n in range(T2 * L):
                    if n % L == 0:
                        pe.wait_ge(low_ready, n // L + 1)
                        pe.wait_ge(high_ready, n // L + 1)
                    mm = pe.matmul(p_rows[:, 0:NB], is_low[:, n, :], is_high[:, n, :], start=(n == 0), stop=(n == T2 * L - 1))
                mm.then_inc(rows_summed, 1)

            @block.sync
            def _(sp):
                for g in range(PARTS):
                    load_part(sp, g, 0, raw_gu, raw_d, w_gate, w_up, w_down, first_loaded)
                sp.wait_ge(first_loaded, 16 * (2 * GU + KE))

            @block.scalar
            def _(act):
                act.wait_ge(shifted, 1)
                nc.scalar.activation(gexp[:, :, :], gexp[:, :, :], ACT.Exp).then_inc(exped, 1)
                act.wait_ge(shifted, 2)
                nc.scalar.activation(ex[:, :], d[:, :], ACT.Exp).then_inc(exped, 1)

            @block.vector
            def _(dve):
                chain = Chain(dve, steps)
                tt = dve.tensor_tensor
                gl = logits[:, :, 0:EG]
                chain.link(dve.tensor_reduce(gmax[:, :], gl, AX.X, ALU.max))
                tt(gexp[:, :, :], gl, over_experts(gmax[:, :], EG), ALU.subtract).then_inc(shifted, 1)
                dve.wait_ge(consts, 1)

                def first_highest(out, one_hot, tmp, values, highest, n):
                    chain.link(tt(tmp, values, over_experts(highest, n), ALU.is_equal))
                    chain.link(dve.scalar_tensor_tensor(out=tmp, in0=tmp, scalar=-float(NE), in1=over_tiles(iota_e[:, 0:n], n),
                                                        op0=ALU.mult, op1=ALU.add))
                    chain.link(dve.tensor_reduce(out, tmp, AX.X, ALU.min))
                    chain.link(dve.tensor_scalar(out, out, float(NE), None, ALU.add))
                    chain.link(tt(one_hot, over_tiles(iota_e[:, 0:n], n), over_experts(out, n), ALU.is_equal))

                first_highest(gsel[:, :], gtmp[:, :, :], gtmp[:, :, :], gl, gmax[:, :], EG)
                chain.link(dve.tensor_scalar(gtmp[:, :, :], gtmp[:, :, :], MASKED, -MASKED, ALU.mult, ALU.add))
                chain.link(tt(el[:, :, :].rearrange("p t (g e) -> p t g e", g=EG),
                              logits[:, :, EG:NR].rearrange("p t (g e) -> p t g e", g=EG),
                              gtmp[:, :, :].unsqueeze(3).to_broadcast([P, L, EG, EPG]), ALU.add))
                chain.link(dve.tensor_reduce(top[:, 0, :], el[:, :, :], AX.X, ALU.max))
                first_highest(sel[:, :], pick[:, 0, :, :], etmp[:, :, :], el[:, :, :], top[:, 0, :], NE)
                chain.link(dve.scalar_tensor_tensor(out=el[:, :, :], in0=pick[:, 0, :, :], scalar=-3.0 * MASKED, in1=el[:, :, :],
                                                    op0=ALU.mult, op1=ALU.add))
                chain.link(dve.tensor_reduce(top[:, 1, :], el[:, :, :], AX.X, ALU.max))
                tt(d[:, :], top[:, 1, :], top[:, 0, :], ALU.subtract).then_inc(shifted, 1)
                first_highest(sel[:, :], pick[:, 1, :, :], etmp[:, :, :], el[:, :, :], top[:, 1, :], NE)
                tt(both[:, :, :], pick[:, 0, :, :], pick[:, 1, :, :], ALU.add).then_inc(picked, 1)
                dve.wait_ge(exped, 2)
                chain.link(dve.tensor_reduce(gsum[:, :], gexp[:, :, :], AX.X, ALU.add))
                chain.link(dve.tensor_scalar(d[:, :], ex[:, :], 1.0, None, ALU.add))
                chain.link(tt(gsum[:, :], gsum[:, :], d[:, :], ALU.mult))
                chain.link(dve.reciprocal(share[:, 0, :], gsum[:, :]))
                chain.link(tt(share[:, 1, :], share[:, 0, :], ex[:, :], ALU.mult))
                dve.wait_ge(ranked, 1)
                total = p_total[:, :].rearrange("p (t e) -> p t e", e=NE)
                chain.link(dve.tensor_reduce(count[:, :], p_total[:, :].rearrange("p (t e) -> p e t", e=NE), AX.X, ALU.add))
                chain.link(tt(over[:, :, :], count[:, :].unsqueeze(2).to_broadcast([P, NE, L]),
                              thr[:, :].unsqueeze(1).to_broadcast([P, NE, L]), ALU.is_gt))
                chain.link(dve.tensor_reduce(nblk[:, :], over[:, :, :], AX.X, ALU.add))
                chain.link(dve.tensor_scalar(nblk[:, 0:1], nblk[:, 0:1], 1.0, None, ALU.max))
                reach, now = 1, nblk[:, :]
                while reach < NE:
                    new = end[:, reach.bit_length() % 2, :]
                    dve.tensor_copy(new[:, :reach], now[:, :reach])
                    chain.link(tt(new[:, reach:], now[:, reach:], now[:, :NE - reach], ALU.add))
                    reach, now = 2 * reach, new
                chain.link(tt(start[:, 0, :], now, nblk[:, :], ALU.subtract))
                chain.link(dve.tensor_scalar(start[:, 0, :], start[:, 0, :], float(P), None, ALU.mult))
                for t in range(1, L):
                    chain.link(tt(start[:, t, :], start[:, t - 1, :], total[:, t - 1, :], ALU.add))
                chain.link(tt(pos[:, :, :], start[:, :, :], p_rank[:, :].rearrange("p (t e) -> p t e", e=NE), ALU.add))
                for choice in range(T2):
                    chain.link(tt(etmp[:, :, :], pick[:, choice, :, :], pos[:, :, :], ALU.mult))
                    chain.link(dve.tensor_reduce(where[:, choice, :], etmp[:, :, :], AX.X, ALU.add))
                chain.link(dve.tensor_copy(dest[:, :, :], where[:, :, :]))
                flat = dest[:, :, :].rearrange("p c t -> p (c t)")
                chain.link(dve.tensor_scalar(index2[:, :], flat, 7, None, ALU.logical_shift_right))
                dve.tensor_copy(slot_high[:, :], index2[:, :]).then_inc(index_ready, 1)
                chain.link(dve.tensor_scalar(index[:, :], flat, P - 1, None, ALU.bitwise_and))
                dve.tensor_copy(slot_low[:, :], index[:, :]).then_inc(index_ready, 1)
                dve.wait_ge(index_ready, 2)
                for c in range(T2):
                    dve.tensor_tensor(is_high[:, ds(c * L, L), :], slot_high[:, ds(c * L, L)].unsqueeze(2).to_broadcast([P, L, NB]),
                                      iota_b[:, 0:NB].unsqueeze(1).to_broadcast([P, L, NB]), ALU.is_equal).then_inc(matched, 1)
                for c in range(T2):
                    dve.tensor_tensor(is_low[:, ds(c * L, L), :], slot_low[:, ds(c * L, L)].unsqueeze(2).to_broadcast([P, L, P]),
                                      iota_p[:, :].unsqueeze(1).to_broadcast([P, L, P]), ALU.is_equal).then_inc(low_ready, 1)
                last = now[0:1, NE - 1:NE]
                chain.link(dve.tensor_scalar(blk[:, 0:1], last, -1.0, None, ALU.add))
                chain.link(tt(blk[:, 1:], iota_b[0:1, 1:], blk[:, 0:1].to_broadcast([1, NB]), ALU.min))
                chain.link(dve.memset(blk[:, 0:1], 0.0))
                chain.link(tt(cmp[:, :, :], blk[:, :].unsqueeze(2).to_broadcast([1, NB + 1, NE]),
                              now[0:1, :].unsqueeze(1).to_broadcast([1, NB + 1, NE]), ALU.is_ge))
                chain.link(dve.tensor_reduce(tabf[:, 0, :], cmp[:, :, :], AX.X, ALU.add))
                chain.link(dve.memset(tabf[:, 1, 0:1], 0.0))
                chain.link(tt(tabf[:, 1, 1:], tabf[:, 0, 1:], tabf[:, 0, 0:NB], ALU.is_gt))
                reach, src = 1, tabf[:, 1, :]
                spare = (tabf[:, 2, :], tabf[:, 3, :])
                turn = 0
                while reach < NB + 1:
                    new = spare[turn % 2]
                    dve.tensor_copy(new[:, :reach], src[:, :reach])
                    chain.link(tt(new[:, reach:], src[:, reach:], src[:, :NB + 1 - reach], ALU.add))
                    reach, src, turn = 2 * reach, new, turn + 1
                dve.tensor_copy(table[:, 2, :], src)
                dve.tensor_copy(table[:, 0, :], tabf[:, 0, :])
                dve.tensor_copy(table[:, 1, :], tabf[:, 1, :])
                dve.tensor_copy(table[:, 3, 0:1], last).then_inc(table_ready, 1)
                dve.wait_ge(table_ready, 1)
                dve.wait_ge(rows_summed, 1)
                dve.tensor_copy(slot_rows[:, 0:NB], p_rows[:, 0:NB]).then_inc(rows_ready, 1)
                dve.wait_ge(rows_ready, 1)


def experts(nc, table, slot_rows, ident, h_dram, raw_gu, raw_d, w_gate, w_up, w_down, y_dram):
    BY_POOL = (1, 3, 5, 7, 9, 11)
    HI_BY_DVE = (3, 6, 9)
    with ExitStack() as ctx:
        s = Scope(nc, ctx, "moe")
        hi_gu, lo_gu = s.sb("hi_gu", [P, GU, 2, 2, H2], F32R), s.sb("lo_gu", [P, GU, 2, 2, H2], F32R)
        hi_d, lo_d = s.sb("hi_d", [P, KE, D], F32R), s.sb("lo_d", [P, KE, D], F32R)
        row = s.sb("row", [P, 2], I32)
        xg = s.sb("xg", [P, 2, D])
        xT_hi, xT_lo = s.sb("xT_hi", [P, 2, KD, P], F32R), s.sb("xT_lo", [P, 2, KD, P], F32R)
        act_g = s.sb("act_g", [P, 2, H2])
        hid = s.sb("hid", [P, 2, H2])
        hT_hi, hT_lo = s.sb("hT_hi", [P, KE, P], F32R), s.sb("hT_lo", [P, KE, P], F32R)
        ys = s.sb("ys", [P, 2, D])
        zero = s.sb("zero", [P, D])
        p_turn = s.ps("p_turn", [P, 2, 512])
        p_gu = s.ps("p_gu", [P, 2, 2, 512])
        p_y = s.ps("p_y", [P, 2, 512])
        part_loaded = [s.sem(f"part_loaded{g}") for g in range(PARTS)]
        hi_ready = [s.sem(f"hi_ready{g}") for g in range(PARTS)]
        lo_ready = [s.sem(f"lo_ready{g}") for g in range(PARTS)]
        used = [s.sem(f"used{g}") for g in range(PARTS)]
        gathered = [s.sem(f"gathered{i}") for i in range(2)]
        y_stored = [s.sem(f"y_stored{i}") for i in range(2)]
        turned = [s.sem(f"turned{i}") for i in range(2)]
        hi_taken = [s.sem(f"hi_taken{i}") for i in range(2)]
        lo_taken = [s.sem(f"lo_taken{i}") for i in range(2)]
        silu_ready = [s.sem(f"silu_ready{i}") for i in range(2)]
        hid_ready = [s.sem(f"hid_ready{i}") for i in range(2)]
        row_ready, row_seen, all_stored, zeroed, rest_zeroed, y_ready = (s.sem(n) for n in (
            "row_ready", "row_seen", "all_stored", "zeroed", "rest_zeroed", "y_ready"))

        def entry(eng, r, b, top):
            return eng.value_load(table[0:1, r, ds(b, 1)], min_val=0, max_val=top)

        def by_twos(eng, body):
            count = entry(eng, 3, 0, NB)
            with eng.Fori(0, NB // 2) as i:
                with eng.If(2 * i < count):
                    body(i)
            return count

        def raw_part(g):
            return raw_gu[:, g, :, :, :] if g < GU else raw_d[:, g - GU, :]

        def hi_part(g):
            return hi_gu[:, g, :, :, :] if g < GU else hi_d[:, g - GU, :]

        def lo_part(g):
            return lo_gu[:, g, :, :, :] if g < GU else lo_d[:, g - GU, :]

        def cut_high(eng, copy, g, n, b):
            eng.wait_ge(part_loaded[g], (32 if g < GU else 16) * n)
            if b is not None:
                eng.wait_ge(used[g], b + 1)
            copy(hi_part(g), raw_part(g)).then_inc(hi_ready[g], 1)

        def cut_low(eng, g, n, b):
            eng.wait_ge(hi_ready[g], n)
            if b is not None:
                eng.wait_ge(used[g], b + 1)
            eng.tensor_tensor(lo_part(g), raw_part(g), hi_part(g), ALU.subtract).then_inc(lo_ready[g], 1)

        with nc.Block() as block:
            @block.sync
            def _(sp):
                def load(e, before):
                    for g in range(PARTS):
                        sp.wait_ge(lo_ready[g], before)
                        load_part(sp, g, e, raw_gu, raw_d, w_gate, w_up, w_down, part_loaded[g])

                for g in range(PARTS):
                    sp.sem_inc(part_loaded[g], 32 if g < GU else 16)

                def reload(b):
                    with sp.If(entry(sp, 1, b, 1) > 0):
                        load(entry(sp, 0, b, NE - 1), entry(sp, 2, b, NE))

                count = by_twos(sp, lambda i: [reload(2 * i), reload(2 * i + 1)])
                sp.wait_ge(zeroed, 1)
                with sp.Fori(0, NB // 2) as i:
                    with sp.If(2 * i >= count):
                        for u in range(2):
                            sp.dma_start(y_dram[ds((2 * i + u) * P, P), :], zero[:, :]).then_inc(rest_zeroed, 16)
                    with sp.Else():
                        sp.sem_inc(rest_zeroed, 32)
                sp.wait_ge(rest_zeroed, 16 * NB)

            @block.gpsimd
            def _(pool):
                def gather(b, u):
                    pool.wait_ge(turned[1], 2 * b + 1)
                    pool.tensor_copy(row[:, u:u + 1], slot_rows[:, ds(b, 1)]).then_inc(row_ready, 1)
                    pool.wait_ge(row_ready, b + 1)
                    pool.sem_inc(row_seen, 1)
                    pool.indirect_dma_start(out=xg[:, u, :], out_offset=None, in_=h_dram,
                                            in_offset=bass.IndirectOffsetOnAxis(ap=row[:, u:u + 1], axis=0)
                                            ).then_inc(gathered[u], 16)

                def block_of(b, u):
                    gather(b + 2, u)
                    with pool.If(entry(pool, 1, b + 1, 1) > 0):
                        n = entry(pool, 2, b + 1, NE) + 1
                        for g in BY_POOL:
                            cut_low(pool, g, n, b)

                gather(0, 0)
                gather(1, 1)
                pool.memset(zero[:, :], 0.0).then_inc(zeroed, 1)
                for g in BY_POOL:
                    cut_low(pool, g, 1, None)
                by_twos(pool, lambda i: [block_of(2 * i, 0), block_of(2 * i + 1, 1)])

            @block.tensor
            def _(pe):
                pe.sem_inc(turned[1], 4)

                def turn(half, tiles, src, count):
                    pe.wait_ge(lo_taken[half], count)
                    for m in range(tiles):
                        tr = pe.transpose(p_turn[:, half, ds(m * P, P)], src(m), ident[:, :])
                    tr.then_inc(turned[half], 1)

                def turn_x(u, gathers, count):
                    pe.wait_ge(gathered[u], gathers)
                    for half in range(2):
                        turn(half, 4, lambda m: xg[:, u, ds((4 * half + m) * P, P)], count)

                def three(bank, x_hi, x_lo, w_hi, w_lo, first, last):
                    pe.matmul(bank, x_hi, w_hi, start=first, stop=False)
                    pe.matmul(bank, x_hi, w_lo, start=False, stop=False)
                    return pe.matmul(bank, x_lo, w_hi, start=False, stop=last)

                def block_of(b, u):
                    n = entry(pe, 2, b, NE) + 1

                    def gate_up(half, kp):
                        g = 4 * half + kp
                        pe.wait_ge(lo_ready[g], n)
                        for k in range(2):
                            for m in range(2):
                                mm = three(p_gu[:, half, m, 0:H2], xT_hi[:, u, 2 * kp + k, :], xT_lo[:, u, 2 * kp + k, :],
                                           hi_gu[:, g, m, k, :], lo_gu[:, g, m, k, :], kp + k == 0, kp == 3 and k == 1)
                        mm.then_inc(used[g], 1)

                    def down(k):
                        pe.wait_ge(lo_ready[GU + k], n)
                        for half in range(2):
                            cols = ds(half * 512, 512)
                            mm = three(p_y[:, half, :], hT_hi[:, k, :], hT_lo[:, k, :], hi_d[:, k, cols], lo_d[:, k, cols],
                                       k == 0, k == KE - 1)
                        mm.then_inc(used[GU + k], 1)

                    def turn_h(half):
                        pe.wait_ge(hid_ready[half], b + 2)
                        turn(half, 2, lambda m: hid[:, half, ds(m * P, P)], 2 * b + 3)

                    for half in range(2):
                        pe.wait_ge(lo_taken[half], 2 * b + 2)
                    pe.wait_ge(hid_ready[0], b + 1)
                    for kp in range(4):
                        gate_up(0, kp)
                    turn_x(1 - u, 8 * b + 16 + 8 * u, 2 * b + 2)
                    pe.wait_ge(hid_ready[1], b + 1)
                    gate_up(1, 0)
                    gate_up(1, 1)
                    turn_h(0)
                    gate_up(1, 2)
                    gate_up(1, 3)
                    pe.wait_ge(lo_taken[0], 2 * b + 4)
                    pe.wait_ge(y_ready, b + 1)
                    down(0)
                    turn_h(1)
                    down(1)
                    pe.wait_ge(lo_taken[1], 2 * b + 4)
                    down(2)
                    down(3)

                turn_x(0, 16, 1)
                by_twos(pe, lambda i: [block_of(2 * i, 0), block_of(2 * i + 1, 1)])

            @block.scalar
            def _(act):
                copy = lambda dst, src: nc.scalar.activation(dst, src, ACT.Copy)

                def take_high(half, dst, n_tiles, count):
                    act.wait_ge(turned[half], count + (4 if half else 0))
                    copy(dst, p_turn[:, half, 0:n_tiles * P]).then_inc(hi_taken[half], 1)

                def take_x(u, count):
                    for half in range(2):
                        take_high(half, xT_hi[:, u, ds(4 * half, 4), :].rearrange("p k c -> p (k c)"), 4, count)

                def block_of(b, u):
                    new = entry(act, 1, b + 1, 1)
                    n = entry(act, 2, b + 1, NE) + 1

                    def cuts(parts):
                        with act.If(new > 0):
                            for g in parts:
                                if g not in HI_BY_DVE:
                                    cut_high(act, copy, g, n, b)

                    def silu(half):
                        act.wait_ge(used[4 * half + 3], b + 1)
                        nc.scalar.activation(act_g[:, half, :], p_gu[:, half, 0, 0:H2], ACT.Silu).then_inc(silu_ready[half], 1)

                    def take_h(half):
                        take_high(half, hT_hi[:, ds(2 * half, 2), :].rearrange("p k c -> p (k c)"), 2, 2 * b + 3)

                    silu(0)
                    take_x(1 - u, 2 * b + 2)
                    cuts(range(0, 2))
                    take_h(0)
                    cuts(range(2, 3))
                    silu(1)
                    cuts(range(3, 5))
                    take_h(1)
                    cuts(range(5, PARTS))
                    act.wait_ge(y_ready, b + 2)
                    act.dma_start(y_dram[ds(b * P, P), :], ys[:, u, :]).then_inc(y_stored[u], 16)

                for g in range(PARTS):
                    if g not in HI_BY_DVE:
                        cut_high(act, copy, g, 1, None)
                    if g == 1:
                        take_x(0, 1)
                count = by_twos(act, lambda i: [block_of(2 * i, 0), block_of(2 * i + 1, 1)])
                for u in range(2):
                    act.wait_ge(y_stored[u], 16 * ((count + 1) >> 1) + 16)
                    act.sem_inc(all_stored, 1)

            @block.vector
            def _(dve):
                dve.sem_inc(y_ready, 1)
                for u in range(2):
                    dve.sem_inc(y_stored[u], 16)
                    dve.sem_inc(hid_ready[u], 1)
                    dve.sem_inc(lo_taken[u], 1)

                def take_low(half, dst, hi, n_tiles, count):
                    dve.wait_ge(hi_taken[half], count)
                    dve.tensor_tensor(dst, p_turn[:, half, 0:n_tiles * P], hi, ALU.subtract).then_inc(lo_taken[half], 1)

                def flat(t, k, n):
                    return t[:, ds(k, n), :].rearrange("p k c -> p (k c)")

                def take_x(u, count):
                    for half in range(2):
                        take_low(half, flat(xT_lo[:, u, :, :], 4 * half, 4), flat(xT_hi[:, u, :, :], 4 * half, 4), 4, count)

                def cut(g, n, b):
                    if g in HI_BY_DVE:
                        cut_high(dve, dve.tensor_copy, g, n, b)
                    if g not in BY_POOL:
                        cut_low(dve, g, n, b)

                def block_of(b, u):
                    new = entry(dve, 1, b + 1, 1)
                    n = entry(dve, 2, b + 1, NE) + 1

                    def cuts(parts):
                        with dve.If(new > 0):
                            for g in parts:
                                cut(g, n, b)

                    def multiply(half):
                        dve.wait_ge(silu_ready[half], b + 1)
                        dve.wait_ge(used[4 * half + 3], b + 1)
                        dve.tensor_tensor(hid[:, half, :], p_gu[:, half, 1, 0:H2], act_g[:, half, :], ALU.mult
                                          ).then_inc(hid_ready[half], 1)

                    def take_h(half):
                        take_low(half, flat(hT_lo, 2 * half, 2), flat(hT_hi, 2 * half, 2), 2, 2 * b + 3)

                    multiply(0)
                    take_x(1 - u, 2 * b + 2)
                    cuts(range(0, 2))
                    take_h(0)
                    cuts(range(2, 3))
                    multiply(1)
                    cuts(range(3, 5))
                    take_h(1)
                    cuts(range(5, PARTS))
                    dve.wait_ge(used[PARTS - 1], b + 1)
                    dve.wait_ge(y_stored[u], 8 * b + (16 - 8 * u))
                    dve.tensor_copy(ys[:, u, :], p_y[:, :, :].rearrange("p a c -> p (a c)")).then_inc(y_ready, 1)

                for g in range(PARTS):
                    cut(g, 1, None)
                    if g == 1:
                        take_x(0, 1)
                by_twos(dve, lambda i: [block_of(2 * i, 0), block_of(2 * i + 1, 1)])


def combine(nc, dest, share, y_dram, x1_dram, gate_dram, out):
    BUF = 3
    with ExitStack() as ctx:
        s = Scope(nc, ctx, "comb")
        yy = s.sb("yy", [P, BUF, 2, D])
        x1 = s.sb("x1", [P, BUF, D])
        y = s.sb("y", [P, BUF, D])
        sq = s.sb("sq", [P, D])
        mod = s.sb("mod", [P, D])
        eps = s.sb("eps", [P, 1])
        ms, root, rstd = s.sb("ms", [P, 2]), s.sb("root", [P, 2]), s.sb("rstd", [P, 2])
        gathered = [s.sem(f"gathered{i}") for i in range(BUF)]
        x_loaded = [s.sem(f"x_loaded{i}") for i in range(BUF)]
        stored = [s.sem(f"stored{i}") for i in range(BUF)]
        mod_loaded, eps_ready, first, mixed, squared, rooted, recips, scaled, summed = (s.sem(n) for n in (
            "mod_loaded", "eps_ready", "first", "mixed", "squared", "rooted", "recips", "scaled", "summed"))
        with nc.Block() as block:
            @block.gpsimd
            def _(pool):
                pool.memset(eps[:, :], EPS).then_inc(eps_ready, 1)

                for t in range(TILES):
                    if t >= BUF:
                        pool.wait_ge(mixed, t - BUF + 1)
                    for c in range(2):
                        pool.indirect_dma_start(out=yy[:, t % BUF, c, :], out_offset=None, in_=y_dram,
                                                in_offset=bass.IndirectOffsetOnAxis(ap=dest[:, c, t:t + 1], axis=0)
                                                ).then_inc(gathered[t % BUF], 16)

            @block.sync
            def _(sp):
                sp.dma_start(mod[:, :], gate_dram.partition_broadcast(P)).then_inc(mod_loaded, 16)

                def load(t):
                    if t >= BUF:
                        sp.wait_ge(stored[t % BUF], 16 * (t // BUF))
                    sp.dma_start(x1[:, t % BUF, :], x1_dram[ds(t * P, P), :]).then_inc(x_loaded[t % BUF], 16)

                load(0)
                load(1)
                for t in range(TILES):
                    if t + 2 < TILES:
                        load(t + 2)
                    sp.wait_ge(summed, t + 1)
                    sp.dma_start(out[0, ds(t * P, P), :], x1[:, t % BUF, :]).then_inc(stored[t % BUF], 16)
                for i in range(BUF):
                    sp.wait_ge(stored[i], 16 * len(range(i, TILES, BUF)))

            @block.scalar
            def _(act):
                act.wait_ge(eps_ready, 1)
                for t in range(TILES):
                    act.wait_ge(mixed, t + 1)
                    if t >= 2:
                        act.wait_ge(recips, t - 1)
                    nc.scalar.activation(sq[:, :], y[:, t % BUF, :], ACT.Square, accum_out=ms[:, t % 2:t % 2 + 1]).then_inc(squared, 1)
                    act.wait_ge(squared, t + 1)
                    nc.scalar.activation(root[:, t % 2:t % 2 + 1], ms[:, t % 2:t % 2 + 1], ACT.Sqrt, scale=1.0 / D,
                                         bias=eps[:, 0:1]).then_inc(rooted, 1)

            @block.vector
            def _(dve):
                def mix(t):
                    dve.wait_ge(gathered[t % BUF], 32 * (t // BUF + 1))
                    dve.tensor_scalar(y[:, t % BUF, :], yy[:, t % BUF, 0, :], share[:, 0, t:t + 1], None, ALU.mult).then_inc(first, 1)
                    dve.wait_ge(first, t + 1)
                    dve.scalar_tensor_tensor(out=y[:, t % BUF, :], in0=yy[:, t % BUF, 1, :], scalar=share[:, 1, t:t + 1],
                                             in1=y[:, t % BUF, :], op0=ALU.mult, op1=ALU.add).then_inc(mixed, 1)

                dve.wait_ge(mod_loaded, 16)
                mix(0)
                for t in range(TILES):
                    if t + 1 < TILES:
                        mix(t + 1)
                    dve.wait_ge(rooted, t + 1)
                    dve.reciprocal(rstd[:, t % 2:t % 2 + 1], root[:, t % 2:t % 2 + 1]).then_inc(recips, 1)
                    dve.wait_ge(recips, t + 1)
                    dve.scalar_tensor_tensor(out=y[:, t % BUF, :], in0=y[:, t % BUF, :], scalar=rstd[:, t % 2:t % 2 + 1],
                                             in1=mod[:, :], op0=ALU.mult, op1=ALU.mult).then_inc(scaled, 1)
                    dve.wait_ge(scaled, t + 1)
                    dve.wait_ge(x_loaded[t % BUF], 16 * (t // BUF + 1))
                    dve.tensor_tensor(x1[:, t % BUF, :], y[:, t % BUF, :], x1[:, t % BUF, :], ALU.add).then_inc(summed, 1)


def build(nc, x, c, w_ada, b_ada, g_pre_mix, g_post_mix, g_pre_ffn, g_post_ffn, w_in, w_pool_group, pool_scale,
          w_branch_pool, w_branch_att, w_out, w_group_router, b_group_router, w_expert_router, b_expert_router,
          w_exp_gate, w_exp_up, w_exp_down, out):
    def dram(name, shape, dt=F32):
        return nc.dram_tensor(name, shape, dt).ap()

    ada_part = dram("ada_part", (P, 4 * D))
    gate_dram = dram("gate_ffn", (1, D))
    proj = dram("projected", (IN_TILES * P, SEQ))
    att = dram("attended", (len(DILATIONS), SEQ, HPG * ROW))
    merged = dram("merged", (D, SEQ))
    x1_dram = dram("x_mixed", (SEQ, D))
    h_dram = dram("h_moe", (SEQ, D))
    y_dram = dram("y_slots", (NB * P, D))
    with ExitStack() as ctx:
        def top(name, shape, dt=F32):
            return ctx.enter_context(nc.sbuf_tensor(name, shape, dt))

        ident = top("ident", [P, P])
        constants(nc, ident)
        with ExitStack() as mixer:
            h_hi = mixer.enter_context(nc.sbuf_tensor("h_hi", [P, KD, SEQ], F32R))
            h_lo = mixer.enter_context(nc.sbuf_tensor("h_lo", [P, KD, SEQ], F32R))
            act_c = mixer.enter_context(nc.sbuf_tensor("act_c", [P, KD], F32))
            normalise(nc, x, c, w_ada, b_ada, g_pre_mix, ident, act_c, h_hi, h_lo)
            project(nc, w_in, w_ada, act_c, h_hi, h_lo, proj, ada_part)
        attend(nc, proj, ident, att)
        merge(nc, proj, att, ident, w_pool_group, pool_scale, w_branch_pool, w_branch_att, merged)
        dest, share = top("dest", [P, 2, TILES], I32), top("share", [P, 2, TILES])
        table, slot_rows = top("table", [1, 4, NB + 1], I32), top("slot_rows", [P, NB + 2], I32)
        with nc.sbuf_tensor("logits", [P, TILES, NR], F32) as logits:
            mix_out(nc, x, merged, w_out, ada_part, b_ada, (g_post_mix, g_pre_ffn, g_post_ffn), ident, w_group_router,
                    w_expert_router, b_group_router, b_expert_router, gate_dram, x1_dram, h_dram, logits)
            with nc.sbuf_tensor("raw_gu", [P, GU, 2, 2, H2], F32) as raw_gu, nc.sbuf_tensor("raw_d", [P, KE, D], F32) as raw_d:
                route(nc, logits, dest, share, table, slot_rows, raw_gu, raw_d, w_exp_gate, w_exp_up, w_exp_down)
                experts(nc, table, slot_rows, ident, h_dram, raw_gu, raw_d, w_exp_gate, w_exp_up, w_exp_down, y_dram)
        combine(nc, dest, share, y_dram, x1_dram, gate_dram, out)


_INS = ["x", "c", "w_ada", "b_ada", "g_pre_mix", "g_post_mix", "g_pre_ffn", "g_post_ffn", "w_in", "w_pool_group",
        "pool_scale", "w_branch_pool", "w_branch_att", "w_out", "w_group_router", "b_group_router", "w_expert_router",
        "b_expert_router", "w_exp_gate", "w_exp_up", "w_exp_down"]


def kernel(**inputs):
    import numpy as np
    import concourse.bacc as bacc
    from concourse.bass_utils import run_bass_kernel_spmd

    nc = bacc.Bacc("TRN2", target_bir_lowering=False, num_devices=1)
    arrays, args = {}, {}
    for name in _INS:
        a = np.ascontiguousarray(inputs[name])
        arrays[f"in_{name}"] = a
        args[name] = nc.dram_tensor(f"in_{name}", a.shape, mybir.dt.from_np(a.dtype), kind="ExternalInput").ap()
    args["out"] = nc.dram_tensor("out_0", (1, SEQ, D), F32, kind="ExternalOutput").ap()
    build(nc, **args)
    r = run_bass_kernel_spmd(nc, [arrays], core_ids=[0])
    return r.results[0]["out_0"]
```
